# Optimizing a Trainium2 kernel written in Bass

```python
import math
import jax
import jax.numpy as jnp
from jax import lax
import numpy as np

D_MODEL = 1024
BATCH = 1
SEQ = 256
DEPTH = 2

CTX_LEN = 256
GRID_W = 64
EPS = 1e-6
ROPE_BASE = 10000.0
Q_BLOCK = 128

MLA_HEADS = 8
MLA_NOPE = 64
MLA_ROPE = 32
MLA_V = 64
MLA_Q_RANK = 512
MLA_KV_RANK = 256
MLA_SCALE = 1.0 / math.sqrt(MLA_NOPE + MLA_ROPE)

DIFF_HEADS = 4
DIFF_DH = 64
DIFF_V = 2 * DIFF_DH
DIFF_SCALE = 1.0 / math.sqrt(DIFF_DH)

MLA_WIDTH = MLA_HEADS * MLA_V
DIFF_WIDTH = DIFF_HEADS * DIFF_V

OFF_CKV = 0
OFF_KR = OFF_CKV + MLA_KV_RANK
OFF_KD = OFF_KR + MLA_ROPE
OFF_VD = OFF_KD + DIFF_HEADS * 2 * DIFF_DH
KV_COLS = OFF_VD + DIFF_HEADS * DIFF_V
OFF_CQ = KV_COLS
OFF_QD = OFF_CQ + MLA_Q_RANK
OFF_GATE = OFF_QD + DIFF_HEADS * 2 * DIFF_DH
IN_COLS = OFF_GATE + 2 * D_MODEL

N_EXPERTS = 16
N_GROUPS = 4
EXPERTS_PER_GROUP = N_EXPERTS // N_GROUPS
TOP_K = 2
D_EXPERT = 512
D_SHARED = 512

N_MOD = 6

kernel_name = 'hybrid_mla_diffattn_grouped_moe_dit'

def rms_norm(x, g):
    xf = x.astype(jnp.float32)
    y = xf * lax.rsqrt(jnp.mean(xf * xf, axis=-1, keepdims=True) + EPS)
    return (y * g.astype(jnp.float32)).astype(x.dtype)

def modulate(h, shift, scale):
    return h * (1 + scale) + shift

def axial_rope_tables(rows, d_rope):
    d_axis = d_rope // 2
    inv = ROPE_BASE ** (-jnp.arange(0, d_axis, 2, dtype=jnp.float32) / d_axis)
    r = jnp.repeat(jnp.arange(rows, dtype=jnp.float32), GRID_W)
    col = jnp.tile(jnp.arange(GRID_W, dtype=jnp.float32), rows)
    ang = jnp.stack([r[:, None] * inv, col[:, None] * inv], axis=1)
    return jnp.cos(ang), jnp.sin(ang)

def apply_rope(x, cos, sin):
    shp = x.shape
    xa = x.reshape(*shp[:-1], 2, 2, shp[-1] // 4)
    x1, x2 = xa[..., 0, :], xa[..., 1, :]
    cos = cos.astype(x.dtype)
    sin = sin.astype(x.dtype)
    out = jnp.stack([x1 * cos - x2 * sin, x1 * sin + x2 * cos], axis=-2)
    return out.reshape(shp)

def sweep_query_blocks(fn, queries):
    B, n = queries[0].shape[:2]
    nb = n // Q_BLOCK
    blocks = tuple(q.reshape(B, nb, Q_BLOCK, *q.shape[2:]).swapaxes(0, 1) for q in queries)
    out = lax.map(lambda qb: fn(*qb), blocks)
    return out.swapaxes(0, 1).reshape(B, n, *out.shape[3:])

def mla_attend(q_nope, q_rope, k_nope, k_rope, v):
    s = (jnp.einsum('bqhd,bkhd->bhqk', q_nope, k_nope)
         + jnp.einsum('bqhr,bkr->bhqk', q_rope, k_rope))
    p = jax.nn.softmax(s.astype(jnp.float32) * MLA_SCALE, axis=-1).astype(v.dtype)
    return jnp.einsum('bhqk,bkhd->bqhd', p, v)

def diff_attend(q, k, v, lam):
    s = jnp.einsum('bqhmd,bkhmd->mbhqk', q, k).astype(jnp.float32) * DIFF_SCALE
    p = jax.nn.softmax(s, axis=-1)
    a = (p[0] - lam * p[1]).astype(v.dtype)
    return jnp.einsum('bhqk,bkhd->bqhd', a, v)

def mla_keys(p, lp, rope):
    B, n = p.shape[:2]
    kv = rms_norm(p[..., OFF_CKV:OFF_KR], lp['mla_kv_norm_g']) @ lp['mla_w_ukv']
    kv = kv.reshape(B, n, MLA_HEADS, MLA_NOPE + MLA_V)
    k_nope = rms_norm(kv[..., :MLA_NOPE], lp['mla_k_g'][:MLA_NOPE])
    k_rope = rms_norm(p[..., OFF_KR:OFF_KD], lp['mla_k_g'][MLA_NOPE:])
    if rope is not None:
        k_rope = apply_rope(k_rope, *rope)
    return k_nope, k_rope, kv[..., MLA_NOPE:]

def mla_queries(p, lp, rope):
    B, n = p.shape[:2]
    q = rms_norm(p[..., OFF_CQ:OFF_QD], lp['mla_q_norm_g']) @ lp['mla_w_uq']
    q = q.reshape(B, n, MLA_HEADS, MLA_NOPE + MLA_ROPE)
    q_nope = rms_norm(q[..., :MLA_NOPE], lp['mla_q_g'][:MLA_NOPE])
    q_rope = rms_norm(q[..., MLA_NOPE:], lp['mla_q_g'][MLA_NOPE:])
    if rope is not None:
        cos, sin = rope
        q_rope = apply_rope(q_rope, cos[:, None], sin[:, None])
    return q_nope, q_rope

def diff_keys(p, lp, rope):
    B, n = p.shape[:2]
    k = rms_norm(p[..., OFF_KD:OFF_VD].reshape(B, n, DIFF_HEADS, 2, DIFF_DH), lp['diff_k_g'])
    if rope is not None:
        cos, sin = rope
        k = apply_rope(k, cos[:, None, None], sin[:, None, None])
    v = p[..., OFF_VD:KV_COLS].reshape(B, n, DIFF_HEADS, DIFF_V)
    return k, v

def diff_queries(p, lp, rope):
    B, n = p.shape[:2]
    q = rms_norm(p[..., OFF_QD:OFF_GATE].reshape(B, n, DIFF_HEADS, 2, DIFF_DH), lp['diff_q_g'])
    if rope is not None:
        cos, sin = rope
        q = apply_rope(q, cos[:, None, None], sin[:, None, None])
    return q

def lambda_value(lam_p, lam_init):
    lf = lam_p.astype(jnp.float32)
    return jnp.exp(jnp.sum(lf[0] * lf[1])) - jnp.exp(jnp.sum(lf[2] * lf[3])) + lam_init

def merge_branches(p, o_mla, o_diff, lp, lam_init):
    B, n = p.shape[:2]
    g = jax.nn.sigmoid(p[..., OFF_GATE:].astype(jnp.float32)).astype(p.dtype)
    o_d = rms_norm(o_diff, lp['diff_sub_g']) * (1.0 - lam_init)
    y = (g[..., :D_MODEL] * (o_mla.reshape(B, n, MLA_WIDTH) @ lp['w_o_mla'])
         + g[..., D_MODEL:] * (o_d.reshape(B, n, DIFF_WIDTH) @ lp['w_o_diff']))
    return y @ lp['w_out']

def grouped_moe(h, router_w, router_b, lp):
    N = h.shape[0]
    aff = jax.nn.sigmoid(h.astype(jnp.float32) @ router_w.astype(jnp.float32))
    sel = (aff + router_b.astype(jnp.float32)).reshape(N, N_GROUPS, EXPERTS_PER_GROUP)
    group_score = jnp.sum(lax.top_k(sel, TOP_K)[0], axis=-1)
    best_group = jnp.argmax(group_score, axis=-1)
    in_group = jnp.take_along_axis(sel, best_group[:, None, None], axis=1)[:, 0]
    local = lax.top_k(in_group, TOP_K)[1]
    idx = best_group[:, None] * EXPERTS_PER_GROUP + local
    w = jnp.take_along_axis(aff, idx, axis=-1)
    w = w / jnp.sum(w, axis=-1, keepdims=True)
    combine = jnp.sum(jax.nn.one_hot(idx, N_EXPERTS, dtype=jnp.float32) * w[..., None],
                      axis=1).astype(h.dtype)
    out = (jax.nn.silu(h @ lp['sh_w_gate']) * (h @ lp['sh_w_up'])) @ lp['sh_w_down']
    for e in range(N_EXPERTS):
        he = jax.nn.silu(h @ lp['moe_w_gate'][e]) * (h @ lp['moe_w_up'][e])
        out = out + combine[:, e:e + 1] * (he @ lp['moe_w_down'][e])
    return out

def setup_inputs(seed: int = 0) -> dict:
    key = jax.random.key(seed)
    ks = iter(jax.random.split(key, 40))

    def nrm(shape, scale):
        return jax.random.normal(next(ks), shape, jnp.float32) * scale

    def gain(shape):
        return 1.0 + 0.02 * jax.random.normal(next(ks), shape, jnp.float32)

    L, D = DEPTH, D_MODEL
    return {
        'x': nrm((BATCH, SEQ, D), 1.0),
        'c': nrm((BATCH, D), 1.0),
        'ctx': nrm((BATCH, CTX_LEN, D), 1.0),
        'c_ctx': nrm((D,), 1.0),
        'ada_w': nrm((L, D, N_MOD * D), 0.5 * D ** -0.5),
        'ada_b': nrm((L, N_MOD * D), 0.02),
        'attn_norm_g': gain((L, D)),
        'ffn_norm_g': gain((L, D)),
        'w_in': nrm((L, D, IN_COLS), D ** -0.5),
        'mla_q_norm_g': gain((L, MLA_Q_RANK)),
        'mla_w_uq': nrm((L, MLA_Q_RANK, MLA_HEADS * (MLA_NOPE + MLA_ROPE)), MLA_Q_RANK ** -0.5),
        'mla_kv_norm_g': gain((L, MLA_KV_RANK)),
        'mla_w_ukv': nrm((L, MLA_KV_RANK, MLA_HEADS * (MLA_NOPE + MLA_V)), MLA_KV_RANK ** -0.5),
        'mla_q_g': gain((L, MLA_NOPE + MLA_ROPE)),
        'mla_k_g': gain((L, MLA_NOPE + MLA_ROPE)),
        'diff_q_g': gain((L, 2, DIFF_DH)),
        'diff_k_g': gain((L, 2, DIFF_DH)),
        'diff_lam': nrm((L, 4, DIFF_DH), 0.1),
        'diff_sub_g': gain((L, DIFF_V)),
        'w_o_mla': nrm((L, MLA_WIDTH, D), MLA_WIDTH ** -0.5),
        'w_o_diff': nrm((L, DIFF_WIDTH, D), DIFF_WIDTH ** -0.5),
        'w_out': nrm((L, D, D), D ** -0.5),
        'router_w': nrm((D, N_EXPERTS), D ** -0.5),
        'router_b': nrm((N_EXPERTS,), 0.01),
        'moe_w_gate': nrm((L, N_EXPERTS, D, D_EXPERT), D ** -0.5),
        'moe_w_up': nrm((L, N_EXPERTS, D, D_EXPERT), D ** -0.5),
        'moe_w_down': nrm((L, N_EXPERTS, D_EXPERT, D), D_EXPERT ** -0.5),
        'sh_w_gate': nrm((L, D, D_SHARED), D ** -0.5),
        'sh_w_up': nrm((L, D, D_SHARED), D ** -0.5),
        'sh_w_down': nrm((L, D_SHARED, D), D_SHARED ** -0.5),
    }

def reference(x, c, ctx, c_ctx, ada_w, ada_b, attn_norm_g, ffn_norm_g, w_in,
              mla_q_norm_g, mla_w_uq, mla_kv_norm_g, mla_w_ukv, mla_q_g, mla_k_g,
              diff_q_g, diff_k_g, diff_lam, diff_sub_g, w_o_mla, w_o_diff, w_out,
              router_w, router_b, moe_w_gate, moe_w_up, moe_w_down,
              sh_w_gate, sh_w_up, sh_w_down):
    B, n, _ = x.shape
    n_ctx = ctx.shape[1]
    rows = n // GRID_W
    rope_m = axial_rope_tables(rows, MLA_ROPE)
    rope_d = axial_rope_tables(rows, DIFF_DH)
    silu_c = jax.nn.silu(c)
    silu_cc = jax.nn.silu(c_ctx)
    xc = ctx
    for l in range(DEPTH):
        last = l == DEPTH - 1
        lam_init = 0.8 - 0.6 * math.exp(-0.3 * l)
        lp = {
            'mla_q_norm_g': mla_q_norm_g[l], 'mla_w_uq': mla_w_uq[l],
            'mla_kv_norm_g': mla_kv_norm_g[l], 'mla_w_ukv': mla_w_ukv[l],
            'mla_q_g': mla_q_g[l], 'mla_k_g': mla_k_g[l],
            'diff_q_g': diff_q_g[l], 'diff_k_g': diff_k_g[l], 'diff_sub_g': diff_sub_g[l],
            'w_o_mla': w_o_mla[l], 'w_o_diff': w_o_diff[l], 'w_out': w_out[l],
            'moe_w_gate': moe_w_gate[l], 'moe_w_up': moe_w_up[l], 'moe_w_down': moe_w_down[l],
            'sh_w_gate': sh_w_gate[l], 'sh_w_up': sh_w_up[l], 'sh_w_down': sh_w_down[l],
        }
        mod = (silu_c @ ada_w[l] + ada_b[l])[:, None, :]
        sh_a, sc_a, g_a, sh_f, sc_f, g_f = jnp.split(mod, N_MOD, axis=-1)
        n_mod_ctx = 2 if last else N_MOD
        mod_c = silu_cc @ ada_w[l][:, :n_mod_ctx * D_MODEL] + ada_b[l][:n_mod_ctx * D_MODEL]
        mods_c = jnp.split(mod_c, n_mod_ctx)

        h_lat = modulate(rms_norm(x, attn_norm_g[l]), sh_a, sc_a)
        h_ctx = modulate(rms_norm(xc, attn_norm_g[l]), mods_c[0], mods_c[1])
        p_lat = h_lat @ w_in[l]
        p_ctx = h_ctx @ (w_in[l][:, :KV_COLS] if last else w_in[l])

        kn_c, kr_c, vm_c = mla_keys(p_ctx, lp, None)
        kd_c, vd_c = diff_keys(p_ctx, lp, None)
        kn_l, kr_l, vm_l = mla_keys(p_lat, lp, rope_m)
        kd_l, vd_l = diff_keys(p_lat, lp, rope_d)
        kn_all = jnp.concatenate([kn_c, kn_l], axis=1)
        kr_all = jnp.concatenate([kr_c, kr_l], axis=1)
        vm_all = jnp.concatenate([vm_c, vm_l], axis=1)
        kd_all = jnp.concatenate([kd_c, kd_l], axis=1)
        vd_all = jnp.concatenate([vd_c, vd_l], axis=1)
        lam = lambda_value(diff_lam[l], lam_init)

        qn_l, qr_l = mla_queries(p_lat, lp, rope_m)
        qd_l = diff_queries(p_lat, lp, rope_d)
        o_m = sweep_query_blocks(lambda qn, qr: mla_attend(qn, qr, kn_all, kr_all, vm_all),
                                 (qn_l, qr_l))
        o_d = sweep_query_blocks(lambda q: diff_attend(q, kd_all, vd_all, lam), (qd_l,))
        x = x + g_a * merge_branches(p_lat, o_m, o_d, lp, lam_init)
        if not last:
            qn_c, qr_c = mla_queries(p_ctx, lp, None)
            qd_c = diff_queries(p_ctx, lp, None)
            oc_m = mla_attend(qn_c, qr_c, kn_c, kr_c, vm_c)
            oc_d = diff_attend(qd_c, kd_c, vd_c, lam)
            xc = xc + mods_c[2] * merge_branches(p_ctx, oc_m, oc_d, lp, lam_init)

        f_lat = modulate(rms_norm(x, ffn_norm_g[l]), sh_f, sc_f).reshape(-1, D_MODEL)
        if last:
            y = grouped_moe(f_lat, router_w, router_b, lp)
            x = x + g_f * y.reshape(B, n, D_MODEL)
        else:
            f_ctx = modulate(rms_norm(xc, ffn_norm_g[l]), mods_c[3], mods_c[4]).reshape(-1, D_MODEL)
            y = grouped_moe(jnp.concatenate([f_lat, f_ctx], axis=0), router_w, router_b, lp)
            x = x + g_f * y[:B * n].reshape(B, n, D_MODEL)
            xc = xc + mods_c[5] * y[B * n:].reshape(B, n_ctx, D_MODEL)
    return x


_drawn_inputs = setup_inputs


def setup_inputs(seed=0):
    import zlib

    import numpy as np

    out = dict(_drawn_inputs(seed))
    spreads = {}
    factors = {'attn_norm_g': 6.053,
     'mla_q_norm_g': 8.0,
     'mla_kv_norm_g': 8.0,
     'mla_q_g': 8.0,
     'mla_k_g': 8.0,
     'diff_q_g': 8.0,
     'diff_k_g': 6.606,
     'diff_sub_g': 3.792}
    for name, (base, spread) in spreads.items():
        noise = np.random.default_rng([zlib.crc32(name.encode()), seed]).standard_normal(out[name].shape)
        drawn = base * np.exp(spread * noise) if base else spread * noise
        out[name] = jnp.asarray(drawn.astype(out[name].dtype))
    for name, factor in factors.items():
        out[name] = (out[name] * factor).astype(out[name].dtype)
    return out
```

```python
import concourse.bass as bass
from concourse import mybir
from contextlib import ExitStack
import math
import numpy as np

F32 = mybir.dt.float32
I32 = mybir.dt.int32
U32 = mybir.dt.uint32
ALU = mybir.AluOpType
ACT = mybir.ActivationFunctionType
AX = mybir.AxisListType

P = 128
D = 1024
KD = D // P
SEQ = 256
CTX = 256
NTOK = SEQ + CTX
TILES = NTOK // P
LTILES = SEQ // P
DEPTH = 2
EPS = 1e-6
GRID_W = 64
ROPE_BASE = 10000.0
MH, NOPE, ROPE, MV = 8, 64, 32, 64
HQ = NOPE + ROPE
QR, KVR = 512, 256
DH, DD, DV = 4, 64, 128
MLA_SCALE = 1.0 / math.sqrt(HQ)
DIFF_SCALE = 1.0 / math.sqrt(DD)
OFF_KD = KVR + ROPE
OFF_VD = OFF_KD + 2 * DH * DD
OFF_CQ = OFF_VD + DH * DV
OFF_QD = OFF_CQ + QR
OFF_GATE = OFF_QD + 2 * DH * DD
NE, EPG, NG = 16, 4, 4
FE = 512
KF = FE // P
CAND = NE * TILES
SORTED = 2 * NTOK
TURNS = (NE + (SORTED - NE) // P + 1) // 2
CHUNK = 4096
WSLOTS = 4
BIG = 1.0e30

C_ID, C_TRI, C_ONE = 0, 128, 256
C_IOTA, C_TIE, C_ECAND, C_RCAND, C_JOB = 384, 400, 404, 468, 532
C_COSM, C_SINM, C_COSD, C_SIND = 533, 565, 597, 661
C_END = 725


def constants():
    c = np.zeros((P, C_END), np.float32)
    c[:, C_ID:C_ID + P] = np.eye(P)
    c[:, C_TRI:C_TRI + P] = np.triu(np.ones((P, P)), 1)
    c[:, C_ONE:C_ONE + P] = 1.0
    c[:, C_IOTA:C_IOTA + NE] = np.arange(NE)
    c[:, C_TIE:C_TIE + NG] = NG - np.arange(NG)
    c[:, C_ECAND:C_ECAND + CAND] = np.arange(CAND) // TILES
    c[:, C_RCAND:C_RCAND + CAND] = P * (np.arange(CAND) % TILES)
    c[:, C_JOB] = np.arange(P) + 1
    pos = np.arange(SEQ)
    for width, cos_at, sin_at in ((ROPE, C_COSM, C_SINM), (DD, C_COSD, C_SIND)):
        axis = width // 2
        inv = (np.float32(ROPE_BASE) ** (-np.arange(0, axis, 2, dtype=np.float32) / np.float32(axis))).astype(np.float32)
        row = (pos // GRID_W).astype(np.float32)[:, None] * inv
        col = (pos % GRID_W).astype(np.float32)[:, None] * inv
        ang = np.concatenate([row, col], axis=1)
        for at, table in ((cos_at, np.cos(ang)), (sin_at, np.sin(ang))):
            for t in range(LTILES):
                c[:, at + t * axis:at + (t + 1) * axis] = table[t * P:(t + 1) * P]
    return c


V_ADAB, V_AG, V_FG, V_QG, V_KVG, V_SUB, V_END = 0, 48, 56, 64, 68, 70, 71
G_MQ, G_MK, G_DQ, G_DK, G_END = 0, 96, 192, 320, 448


def layer_chunks(l):
    order = [(f"ada{n}", n % 4) for n in range(4)]
    order += [("ckv", 0), ("cq", 1), ("kd", 2), ("qd", 3), ("vd", 0), ("ukv", 1), ("uq", 2)]
    order += [(f"ada{n}", (n + 3) % 4) for n in range(4, 12)]
    order += [("om", 3), ("od", 0), ("g0", 1), ("g2", 2), ("g1", 1), ("g3", 2), ("out0", 3), ("out1", 0)]
    order += [("shg", 1), ("shu", 2), ("shd", 3)]
    return order


def norm_tasks(l):
    nq = TILES if l < DEPTH - 1 else LTILES
    tasks = [("ckv", t, 0) for t in range(TILES)]
    tasks += [("cq", t, 0) for t in range(nq)]
    tasks += [("kd", t, 0) for t in range(TILES)]
    tasks += [("qd", t, 0) for t in range(nq)]
    late = [("ukv", t, h) for t in range(TILES) for h in range(2)]
    late += [("uq", t, h) for t in range(nq) for h in range(2)]
    return tasks, late


def attention_units(l):
    nq = TILES if l < DEPTH - 1 else LTILES
    return [u for t in range(nq) for u in [("m", t, h) for h in range(MH)] + [("d", t, h) for h in range(DH)]]


T_LAG = 3
A_TLAG = 2
A_VLAG = 3
NP = 5


def keys_of(t):
    return (0, TILES) if t < LTILES else (LTILES, TILES - LTILES)


def build(nc, A, book):
    ctx = ExitStack()
    with ctx:
        def sb(name, shape, dt=F32):
            return ctx.enter_context(nc.sbuf_tensor(name, shape, dt))

        sems = {}

        def sem(name):
            if name not in sems:
                sems[name] = ctx.enter_context(nc.semaphore(name))
            return sems[name]

        counts, seen = {}, {}

        def sig(ins, name, key, n=1):
            counts[name] = counts.get(name, 0) + n
            book[name, key] = counts[name]
            ins.then_inc(sem(name), n)

        def after(eng, name, key):
            count = book.get((name, key), 1)
            if seen.get((id(eng), name), 0) < count:
                seen[id(eng), name] = count
                eng.wait_ge(sem(name), count)

        def chained(eng, name, ins):
            sig(ins, name, counts.get(name, 0))
            after(eng, name, counts[name] - 1)

        X = sb("X", [P, TILES, D])
        HT = sb("HT", [P, KD, NTOK])
        QT = sb("QT", [P, MH, NTOK])
        KTM = sb("KTM", [P, MH, NTOK])
        QTD = sb("QTD", [P, DH, NTOK])
        KTD = sb("KTD", [P, DH, NTOK])
        VS = sb("VS", [P, 2, TILES, 512])
        OT = sb("OT", [P, 2, 4, NTOK])
        W = sb("W", [P, WSLOTS, CHUNK])
        STG = sb("STG", [P, 4096])
        CST = sb("CST", [P, C_END])
        GAIN = sb("GAIN", [P, DEPTH, G_END])
        VEC = sb("VEC", [P, DEPTH, V_END])
        CROW = sb("CROW", [2 * KD, P])
        CS = sb("CS", [P, 2 * KD])
        CT = sb("CT", [P, 2, 2 * KD])
        MOD = sb("MOD", [P, 48, 2])
        SCL = sb("SCL", [P, 2, KD, 2])
        NLAM = sb("NLAM", [P, DEPTH])
        LT = sb("LT", [P, 8])
        SUBG = sb("SUBG", [P, 1])
        RW = sb("RW", [P, KD, NE])
        RB = sb("RB", [P, NE])
        SSX = sb("SSX", [P, TILES])
        RX = sb("RX", [P, TILES])
        HALF = sb("HALF", [P, 16])
        SS = sb("SS", [P, 4, 16])
        RR = sb("RR", [P, 4, 16])
        KR = sb("KR", [P, TILES, ROPE])
        RT = sb("RT", [P, 4, 256])
        MX = sb("MX", [P, 8])
        MB = sb("MB", [P, 8])
        RSUM = sb("RSUM", [P, 8])
        RINV = sb("RINV", [P, 2, 8])
        RDIF = sb("RDIF", [P, 8])
        SSO = sb("SSO", [P, 4])
        RO = sb("RO", [P, 4])
        TAB = sb("TAB", [1, 72], I32)
        SLOT = sb("SLOT", [P, TILES, 2], U32)
        WTS = sb("WTS", [P, TILES, 2])

        SQ = [STG[:, 512 * i:512 * (i + 1)] for i in range(2)]
        TM = [STG[:, 1024 + 512 * i:1024 + 512 * (i + 1)] for i in range(4)]
        PB = [STG[:, 512 * i:512 * (i + 1)] for i in range(NP)]
        PTS = [STG[:, 2560 + 512 * i:2560 + 512 * (i + 1)] for i in range(2)]
        OTM = STG[:, 3584:4096]
        OWN = OT[:, :, :, :].rearrange("p a k n -> p (a k n)")
        CQT = OWN[:, 0:2048].rearrange("p (k n) -> p k n", k=4)
        CKT = OWN[:, 2048:3072].rearrange("p (k n) -> p k n", k=2)
        XN = QT[:, :, :].rearrange("p a n -> p (a n)").rearrange("p (t d) -> p t d", t=TILES)
        YT = QT
        GATE = QTD[:, :, :].rearrange("p a n -> p (a n)").rearrange("p (s d) -> p s d", s=2)
        HET = KTD
        YS = VS[:, :, :, :].rearrange("p a t n -> p (a t n)").rearrange("p (t d) -> p t d", t=TILES)
        ESLOT = [W[:, i, :] for i in range(WSLOTS)] + [
            QT[:, :, :].rearrange("p a n -> p (a n)"), KTM[:, :, :].rearrange("p a n -> p (a n)")]
        HE = [OWN[:, 1024 * i:1024 * (i + 1)] for i in range(2)]
        HEX = [OWN[:, 2048 + 1024 * i:2048 + 1024 * (i + 1)].rearrange("p (k n) -> p k n", k=KD) for i in range(2)]
        HID = [STG[:, 512 * i:512 * (i + 1)] for i in range(2)]
        THB = [STG[:, 1024 + 512 * i:1024 + 512 * (i + 1)] for i in range(2)]
        YB = [STG[:, 2048 + 1024 * i:2048 + 1024 * (i + 1)] for i in range(2)]
        HTOK = [OWN[:, 1024 * i:1024 * (i + 1)] for i in range(TILES)]
        YG = [[OWN[:, 1024 * (2 * i + k):1024 * (2 * i + k + 1)] for k in range(2)] for i in range(2)]
        HTX = [KTD[:, i, :].rearrange("p (k n) -> p k n", k=KF) for i in range(2)]
        DIAG = STG[:, 0:1024].rearrange("p (h n) -> p h n", h=2)
        MT = [[STG[:, 1024 * b + 512 * j:1024 * b + 512 * (j + 1)] for j in range(2)] for b in range(2)]
        MY = [[STG[:, 2048 + 1024 * b + 512 * j:2048 + 1024 * b + 512 * (j + 1)] for j in range(2)] for b in range(2)]
        STH = [STG[:, 2048 + 512 * i:2048 + 512 * (i + 1)] for i in range(2)]
        SVV = [STG[:, 3072 + 512 * i:3072 + 512 * (i + 1)] for i in range(2)]
        RTF = RT[:, :, :].rearrange("p a n -> p (a n)")
        ZERO = HT[:, 4:6, :].rearrange("p a n -> p (a n)")
        at = [0]

        def route(*shape, dt=None):
            n = int(np.prod(shape))
            v = STG[:, at[0]:at[0] + n]
            at[0] += n
            v = v.bitcast(dt) if dt is not None else v
            if len(shape) == 2:
                v = v.rearrange("p (a b) -> p a b", a=shape[0])
            return v

        AFF, SEL, TMPR = (route(TILES * NE) for _ in range(3))
        PAIR = route(TILES * NG * 6)
        GRP = route(3, TILES * NG)
        BEST = route(TILES, 8)
        BIDX = route(TILES, 8, dt=U32)
        FIDX = route(TILES, 2)
        HOT = [route(TILES, NE) for _ in range(2)]
        MSK = route(TILES, NE)
        CNT = route(3, NE)
        SLF = route(TILES, 2)
        CND = route(4, CAND)
        JOBC = route(4)
        TABI = route(1, dt=I32)[0:1, :]
        CONES = CST[:, C_ONE:C_ONE + CAND]
        assert at[0] <= 2048

        def MASK(t):
            return MSK[:, t, :]

        def tm_sem(kind):
            return "dve_tm" if kind in ("ckv", "cq") else "pool_tm"

        def first_hidden(eng):
            eng.wait_ge(sem("pad_stored"), 16)
            after(eng, "dve_vec", DEPTH - 1)
            after(eng, "dve_lam", 0)

        ROW_LOADS = 2 + 6 * DEPTH
        LAMR = HT[:, 0:2, 0:256]
        VROW = HT[:, 2:4, 0:P]

        PS = [ctx.enter_context(nc.psum_tensor(f"PS{i}", [P, 512], F32)) for i in range(8)]
        Hs = nc.dram_tensor("sorted_h", [SORTED + P, D], F32, kind="Internal").ap()
        Ys = nc.dram_tensor("sorted_y", [SORTED + P, D], F32, kind="Internal").ap()

        ident = CST[:, C_ID:C_ID + P]
        ones = CST[:, C_ONE:C_ONE + P]

        bank_of, turn, holder = {}, [0, 0], {}

        def bank_open(pe, key, acc=False):
            b = 6 + turn[1] % 2 if acc else turn[0] % 6
            turn[acc] += 1
            if b in holder:
                after(pe, *book.get(("read", holder[b]), ("none", 0)))
            holder[b] = key
            book["bank", key] = b
            return PS[b]

        def bank_read(eng, key):
            after(eng, "pe_" + key[0], key)
            return PS[book.get(("bank", key), 0)]

        def last_read(key, name, event):
            book["read", key] = (name, event)

        def product(last, key):
            sig(last, "pe_" + key[0], key)

        ring, before, in_slot = {}, {}, {}
        for l in range(DEPTH):
            for name, s in layer_chunks(l):
                before[l, name] = in_slot.get(s)
                n = 1 + (ring[in_slot[s]][1] if s in in_slot else 0)
                ring[l, name] = (s, n)
                in_slot[s] = (l, name)

        def chunk(pe, l, name):
            s, n = ring[l, name]
            if seen.get((id(pe), s), 0) < n:
                seen[id(pe), s] = n
                pe.wait_ge(sem(f"w_loaded{s}"), 16 * n)
            return W[:, s, :]

        def chunk_done(l, name, product_key):
            book["chunk_done", (l, name)] = product_key

        def nq_of(l):
            return TILES if l < DEPTH - 1 else LTILES

        def streams(n):
            return [(0, 0, SEQ)] + ([(1, SEQ, CTX)] if n > SEQ else [])

        block = ctx.enter_context(nc.Block())

        @block.tensor
        def _(pe):
            mm, tp = nc.tensor.matmul, nc.tensor.transpose

            def small_vectors():
                pe.wait_ge(sem("const_loaded"), 16)
                pe.wait_ge(sem("rows_loaded"), 16 * ROW_LOADS)
                ps = bank_open(pe, ("small", 0))
                tp(ps[:, 0:2 * KD], CROW[:, :], ident[0:2 * KD, 0:2 * KD])
                for l in range(DEPTH):
                    last = tp(ps[:, P * (l + 1):P * (l + 1) + V_END], VROW[0:V_END, l, :], ident[0:V_END, 0:V_END])
                product(last, ("small", 0))

            def ada(l, part):
                ps = bank_open(pe, ("ada", l, part))
                for n in (range(4) if part == 0 else range(4, 12)):
                    w = chunk(pe, l, f"ada{n}").rearrange("p (k n) -> p k n", k=KD)
                    after(pe, "dve_c", 0)
                    for c in range(4):
                        m = 4 * n + c
                        for k in range(KD):
                            last = mm(ps[:, 2 * m:2 * m + 2], w[:, k, c * P:(c + 1) * P], CS[:, k::KD],
                                      start=(k == 0), stop=(k == KD - 1))
                    key = ("ada", l, part) if n in (3, 11) else ("ada", l, part, n)
                    product(last, key)
                    chunk_done(l, f"ada{n}", key)

            def gate_rows(l, which):
                for s in range(2 if l < DEPTH - 1 else 1):
                    for h in range(2):
                        after(pe, "dve_diag", (l, which, s, h))
                        key = ("gate", l, which, s, h)
                        ps = bank_open(pe, key)
                        product(mm(ps[:, :], ones, DIAG[:, h, :], start=True, stop=True), key)

            def hidden_t(l, f):
                nt = TILES if f == 0 else nq_of(l)
                after(pe, "dve_xn", (l, f, nt - 1))
                for k in range(KD):
                    ps = bank_open(pe, ("hT", l, f, k))
                    for t in range(nt):
                        last = tp(ps[:, t * P:(t + 1) * P], XN[:, t, k * P:(k + 1) * P], ident)
                    product(last, ("hT", l, f, k))

            def project(l, kind, t, half):
                key = ("proj", l, kind, t, half)
                w = chunk(pe, l, kind)
                if kind == "ukv":
                    w = w[:, 0:2 * D].rearrange("p (k n) -> p k n", k=2)
                    src, n0, n, kk = CKT, 512 * half, 512, 2
                elif kind == "uq":
                    w = w[:, 0:4 * MH * HQ].rearrange("p (k n) -> p k n", k=4)
                    src, n0, n, kk = CQT, 384 * half, 384, 4
                elif kind == "ckv":
                    w = w[:, 0:KD * OFF_KD].rearrange("p (k n) -> p k n", k=KD)
                    src, n0, n, kk = HT, 0, OFF_KD, KD
                else:
                    w = w.rearrange("p (k n) -> p k n", k=KD)
                    src, n0, n, kk = HT, 0, 512, KD
                ps = bank_open(pe, key)
                for k in range(kk):
                    last = mm(ps[:, 0:n], src[:, k, t * P:(t + 1) * P], w[:, k, n0:n0 + n],
                              start=(k == 0), stop=(k == kk - 1))
                product(last, key)
                chunk_done(l, kind, key)

            def task_t(l, i, task):
                kind, t, half = task
                after(pe, tm_sem(kind), (l, i))
                ps = bank_open(pe, ("T", l, i))
                src = TM[i % 4]
                if kind in ("ukv", "uq"):
                    for h in range(4):
                        last = tp(ps[0:HQ, h * P:(h + 1) * P], src[:, h * HQ:(h + 1) * HQ], ident)
                else:
                    for b in range(2 if kind == "ckv" else 4):
                        last = tp(ps[:, b * P:(b + 1) * P], src[:, b * P:(b + 1) * P], ident)
                product(last, ("T", l, i))

            def prep(l):
                early, late = norm_tasks(l)
                tasks = early + late
                after(pe, "dve_hT", (l, 0, KD - 2))
                after(pe, "act_hT", (l, 0, KD - 1))
                done = 0
                for i, (kind, t, half) in enumerate(tasks):
                    if i == len(early):
                        for tt in range(TILES):
                            project(l, "vd", tt, 0)
                        while done < i:
                            task_t(l, done, tasks[done])
                            done += 1
                        after(pe, "act_T", (l, TILES + nq_of(l) - 1))
                    project(l, kind, t, half)
                    if i - T_LAG >= done:
                        task_t(l, done, tasks[done])
                        done += 1
                while done < len(tasks):
                    task_t(l, done, tasks[done])
                    done += 1

            def attention(l):
                units = attention_units(l)
                ntask = sum(map(len, norm_tasks(l)))
                after(pe, "act_T", (l, ntask - 1))
                after(pe, "act_vd", (l, TILES - 1))
                after(pe, "act_vm", (l, TILES - 1, 1))
                maps = 0

                def scores(u, kind, t, h):
                    k0, kn = keys_of(t)
                    for m in range(1 if kind == "m" else 2):
                        key = ("S", l, u, m)
                        ps = bank_open(pe, key)
                        if kind == "m":
                            last = mm(ps[:, 0:kn * P], QT[0:HQ, h, t * P:(t + 1) * P],
                                      KTM[0:HQ, h, k0 * P:(k0 + kn) * P], start=True, stop=True)
                        else:
                            last = mm(ps[:, 0:kn * P], QTD[64 * m:64 * m + 64, h, t * P:(t + 1) * P],
                                      KTD[64 * m:64 * m + 64, h, k0 * P:(k0 + kn) * P], start=True, stop=True)
                        product(last, key)

                def prob_t(u, kind, t, h):
                    k0, kn = keys_of(t)
                    after(pe, "act_p" if kind == "m" else "dve_a", (l, u))
                    key = ("PT", l, u)
                    ps = bank_open(pe, key)
                    src = PB[book.get(("pbuf", (l, u)), 0)]
                    for c in range(kn):
                        last = tp(ps[:, c * P:(c + 1) * P], src[:, c * P:(c + 1) * P], ident)
                    product(last, key)

                def values(u, kind, t, h):
                    k0, kn = keys_of(t)
                    key = ("O", l, kind, t)
                    if h == 0:
                        bank_open(pe, key, acc=True)
                    ps = PS[book["bank", key]]
                    after(pe, "act_pts" if u % 2 == 0 else "dve_pts", (l, u))
                    w = MV if kind == "m" else DV
                    for c in range(kn):
                        last = mm(ps[:, h * w:(h + 1) * w], PTS[u % 2][:, c * P:(c + 1) * P],
                                  VS[:, int(kind == "d"), k0 + c, h * w:(h + 1) * w], start=(c == 0), stop=(c == kn - 1))
                    done = h == (MH if kind == "m" else DH) - 1
                    product(last, key if done else ("O", l, u))
                    book["pv_done", (l, u)] = key if done else ("O", l, u)

                def out_t(kind, t):
                    after(pe, "dve_o" , (l, kind, t))
                    key = ("OT", l, kind, t)
                    ps = bank_open(pe, key)
                    for b in range(4):
                        last = tp(ps[:, b * P:(b + 1) * P], OTM[:, b * P:(b + 1) * P], ident)
                    product(last, key)

                waiting = []
                for i in range(len(units) + A_VLAG + 2):
                    if i < len(units):
                        scores(i, *units[i])
                    if 0 <= i - A_TLAG < len(units):
                        prob_t(i - A_TLAG, *units[i - A_TLAG])
                    if 0 <= i - A_VLAG < len(units):
                        kind, t, h = units[i - A_VLAG]
                        values(i - A_VLAG, kind, t, h)
                        if h == (MH if kind == "m" else DH) - 1:
                            waiting.append((i + 2, kind, t))
                    while waiting and waiting[0][0] <= i:
                        out_t(*waiting.pop(0)[1:])

            def merge(l):
                nt = nq_of(l)
                n = nt * P
                after(pe, "act_oT", (l, "d", nt - 1))
                om = chunk(pe, l, "om").rearrange("p (k n) -> p k n", k=4)
                od = chunk(pe, l, "od").rearrange("p (k n) -> p k n", k=4)
                for b in range(KD):
                    c = (b % 4) * P
                    g = [chunk(pe, l, f"g{b // 4}"), chunk(pe, l, f"g{2 + b // 4}")]
                    for j, (kk, w, src, c0) in enumerate((
                            (KD, g[0].rearrange("p (k n) -> p k n", k=KD), HT, c),
                            (KD, g[1].rearrange("p (k n) -> p k n", k=KD), HT, c),
                            (4, om, OT[:, 0], b * P), (4, od, OT[:, 1], b * P))):
                        key = ("mg", l, b, j)
                        ps = bank_open(pe, key)
                        for k in range(kk):
                            last = mm(ps[:, 0:n], w[:, k, c0:c0 + P], src[:, k, 0:n], start=(k == 0), stop=(k == kk - 1))
                        product(last, key)
                        chunk_done(l, (f"g{b // 4}", f"g{2 + b // 4}", "om", "od")[j], key)

            def out_proj(l):
                after(pe, "pool_y", (l, KD - 1))
                for h in range(2):
                    w = chunk(pe, l, f"out{h}").rearrange("p (k n) -> p k n", k=KD)
                    for t in range(nq_of(l)):
                        key = ("out", l, h, t)
                        ps = bank_open(pe, key)
                        for k in range(KD):
                            last = mm(ps[:, :], YT[:, k, t * P:(t + 1) * P], w[:, k, :], start=(k == 0), stop=(k == KD - 1))
                        product(last, key)
                        chunk_done(l, f"out{h}", key)

            def router(l):
                after(pe, "dve_hT", (l, 1, KD - 2))
                after(pe, "act_hT", (l, 1, KD - 1))
                key = ("logit", l)
                pe.wait_ge(sem("router_loaded"), 32)
                ps = bank_open(pe, key)
                for t in range(nq_of(l)):
                    for k in range(KD):
                        last = mm(ps[:, NE * t:NE * (t + 1)], HT[:, k, t * P:(t + 1) * P], RW[:, k, :],
                                  start=(k == 0), stop=(k == KD - 1))
                product(last, key)
                for t in range(nq_of(l)):
                    for h in range(2):
                        key = ("htok", l, t, h)
                        ps = bank_open(pe, key)
                        for b in range(4):
                            last = tp(ps[:, b * P:(b + 1) * P], HT[:, 4 * h + b, t * P:(t + 1) * P], ident)
                        product(last, key)

            def places(l):
                nt = nq_of(l)
                after(pe, "dve_mask", l)
                key = ("place", l)
                ps = bank_open(pe, key)
                for t in range(nt):
                    for s in range(t + 1):
                        mm(ps[:, NE * t:NE * (t + 1)], CST[:, C_TRI:C_TRI + P] if s == t else ones,
                           MASK(s), start=(s == 0), stop=(s == t))
                for s in range(nt):
                    last = mm(ps[:, 64:64 + NE], ones, MASK(s), start=(s == 0), stop=(s == nt - 1))
                product(last, key)

            def job_rows(l):
                after(pe, "dve_jobcol", l)
                key = ("jobs", l)
                ps = bank_open(pe, key)
                for j in range(2):
                    last = mm(ps[0:1, j * P:(j + 1) * P], JOBC[:, j:j + 1], ident, start=True, stop=True)
                product(last, key)

            def shared(l):
                nt = nq_of(l)
                n = nt * P
                w = [chunk(pe, l, x).rearrange("p (k n) -> p k n", k=KD) for x in ("shg", "shu")]
                for f in range(KF):
                    for j in range(2):
                        key = ("sh", l, f, j)
                        ps = bank_open(pe, key)
                        for k in range(KD):
                            last = mm(ps[:, 0:n], w[j][:, k, f * P:(f + 1) * P], HT[:, k, 0:n], start=(k == 0), stop=(k == KD - 1))
                        product(last, key)
                        chunk_done(l, ("shg", "shu")[j], key)
                    if f == 0:
                        places(l)
                    if f == 2:
                        job_rows(l)
                w = chunk(pe, l, "shd").rearrange("p (k n) -> p k n", k=KF)
                after(pe, "dve_sh", (l, KF - 1))
                for t in range(nt):
                    for h in range(2):
                        key = ("shd", l, t, h)
                        ps = bank_open(pe, key)
                        for k in range(KF):
                            last = mm(ps[:, :], HET[:, k, t * P:(t + 1) * P], w[:, k, 512 * h:512 * (h + 1)],
                                      start=(k == 0), stop=(k == KF - 1))
                        product(last, key)
                        chunk_done(l, "shd", key)

            def experts(l):
                e = lambda name: sem(f"{name}{l}")
                for b in range(8):
                    after(pe, *book.get(("read", holder[b]), ("none", 0)))
                pe.wait_ge(e("tab_ready"), 1)
                turns = pe.value_load(TAB[0:1, 64:65], min_val=1, max_val=TURNS)

                pe.wait_ge(e("he_loaded0"), 16)
                for h in range(2):
                    for b in range(4):
                        last = tp(PS[h][:, b * P:(b + 1) * P], HE[0][:, (4 * h + b) * P:(4 * h + b + 1) * P], ident)
                    last.then_inc(e(f"e_in_done{h}"), 1)
                with pe.Fori(0, turns) as i:
                    for j in range(2):
                        wg, wu, wd = (ESLOT[3 * j + x] for x in range(3))
                        wg, wu = (x.rearrange("p (k n) -> p k n", k=KD) for x in (wg, wu))
                        wd = wd.rearrange("p (k n) -> p k n", k=KF)
                        pe.wait_ge(e("e_hex_dve"), 2 * i + j + 1)
                        pe.wait_ge(e("e_hex_act"), 2 * i + j + 1)
                        pe.wait_ge(e(f"ew_loaded{3 * j}_"), 16 * i + 16)
                        pe.wait_ge(e("e_hid_done"), 2 * i + j)
                        for k in range(KD):
                            last = mm(PS[2][:, :], HEX[j][:, k, :], wg[:, k, :], start=(k == 0), stop=(k == KD - 1))
                        last.then_inc(e("e_g_done"), 1)
                        pe.wait_ge(e(f"ew_loaded{3 * j + 1}_"), 16 * i + 16)
                        for k in range(KD):
                            last = mm(PS[3][:, :], HEX[j][:, k, :], wu[:, k, :], start=(k == 0), stop=(k == KD - 1))
                        last.then_inc(e("e_u_done"), 1)
                        pe.wait_ge(e(f"he_loaded{1 - j}"), 16 * i + 16 * (1 + j))
                        for h in range(2):
                            for b in range(4):
                                last = tp(PS[h][:, b * P:(b + 1) * P],
                                          HE[1 - j][:, (4 * h + b) * P:(4 * h + b + 1) * P], ident)
                            last.then_inc(e(f"e_in_done{h}"), 1)
                        pe.wait_ge(e("e_hid_done"), 2 * i + j + 1)
                        for b in range(KF):
                            last = tp(PS[4][:, b * P:(b + 1) * P], HID[j][:, b * P:(b + 1) * P], ident)
                        last.then_inc(e("e_ht_done"), 1)
                        pe.wait_ge(e(f"ew_loaded{3 * j + 2}_"), 16 * i + 16)
                        pe.wait_ge(e("e_htx"), 2 * i + j + 1)
                        pe.wait_ge(e("e_y_dve"), 2 * i + j)
                        pe.wait_ge(e("e_y_act"), 2 * i + j)
                        for h in range(2):
                            for k in range(KF):
                                last = mm(PS[5 + h][:, :], HTX[j][:, k, :], wd[:, k, 512 * h:512 * (h + 1)],
                                          start=(k == 0), stop=(k == KF - 1))
                            last.then_inc(e(f"e_d_done{h}"), 1)
                pe.wait_ge(e("e_y_dve"), 2 * turns)
                pe.wait_ge(e("e_y_act"), 2 * turns)
                pe.wait_ge(e("e_hex_dve"), 2 * turns + 1)
                pe.wait_ge(e("e_hex_act"), 2 * turns + 1)
                holder.clear()

            small_vectors()
            for l in range(DEPTH):
                ada(l, 0)
                hidden_t(l, 0)
                prep(l)
                ada(l, 1)
                attention(l)
                gate_rows(l, 0)
                merge(l)
                out_proj(l)
                hidden_t(l, 1)
                router(l)
                shared(l)
                gate_rows(l, 1)
                experts(l)

        @block.sync
        def _(sp):
            sp.dma_start(CST[:, :], A["consts"]).then_inc(sem("const_loaded"), 16)
            sp.dma_start(CROW[0:KD, :], A["c"].rearrange("o (k p) -> (o k) p", p=P)).then_inc(sem("rows_loaded"), 16)
            sp.dma_start(CROW[KD:2 * KD, :], A["c_ctx"].rearrange("(k p) -> k p", p=P)).then_inc(sem("rows_loaded"), 16)
            for l in range(DEPTH):
                for name, at, end in (("ada_b", V_ADAB, V_AG), ("attn_norm_g", V_AG, V_FG), ("ffn_norm_g", V_FG, V_QG),
                                      ("mla_q_norm_g", V_QG, V_KVG), ("mla_kv_norm_g", V_KVG, V_SUB), ("diff_sub_g", V_SUB, V_END)):
                    sp.dma_start(VROW[at:end, l, :], A[name][l, :].rearrange("(k p) -> k p", p=P)).then_inc(sem("rows_loaded"), 16)
            for t in range(TILES):
                src = A["x"][0, t * P:(t + 1) * P, :] if t < LTILES else A["ctx"][0, (t - LTILES) * P:(t - LTILES + 1) * P, :]
                sp.dma_start(X[:, t, :], src).then_inc(sem(f"x_loaded{t}"), 16)

            def source(l, name):
                w_in = A["w_in"][l].rearrange("(k p) n -> p k n", p=P)
                if name.startswith("ada"):
                    n = int(name[3:])
                    return A["ada_w"][l].rearrange("(k p) n -> p k n", p=P)[:, :, 512 * n:512 * (n + 1)], KD
                cols = {"ckv": (0, OFF_KD), "kd": (OFF_KD, OFF_VD), "vd": (OFF_VD, OFF_CQ), "cq": (OFF_CQ, OFF_QD), "qd": (OFF_QD, OFF_GATE)}
                if name in cols:
                    return w_in[:, :, cols[name][0]:cols[name][1]], KD
                if name[0] == "g":
                    c = OFF_GATE + 512 * int(name[1])
                    return w_in[:, :, c:c + 512], KD
                if name[:3] == "out":
                    c = 512 * int(name[3])
                    return A["w_out"][l].rearrange("(k p) n -> p k n", p=P)[:, :, c:c + 512], KD
                tensor, k = {"ukv": ("mla_w_ukv", 2), "uq": ("mla_w_uq", 4), "om": ("w_o_mla", 4), "od": ("w_o_diff", 4),
                             "shg": ("sh_w_gate", KD), "shu": ("sh_w_up", KD), "shd": ("sh_w_down", KF)}[name]
                return A[tensor][l].rearrange("(k p) n -> p k n", p=P), k

            def load(l, name):
                s, n = ring[l, name]
                old = before[l, name]
                if old is not None and old[0] == l:
                    key = book.get(("chunk_done", old), ("none", 0))
                    after(sp, "pe_" + key[0], key)
                src, k = source(l, name)
                width = src.shape[2]
                dst = W[:, s, 0:k * width].rearrange("p (k n) -> p k n", k=k)
                sp.dma_start(dst, src).then_inc(sem(f"w_loaded{s}"), 16)

            expert_w = [A["moe_w_gate"].rearrange("l e (k p) n -> (l e) p k n", p=P),
                        A["moe_w_up"].rearrange("l e (k p) n -> (l e) p k n", p=P),
                        A["moe_w_down"].rearrange("l e (k p) n -> (l e) p k n", p=P)]

            def experts(l):
                e = lambda name: sem(f"{name}{l}")
                nq = nq_of(l)
                sp.wait_ge(e("tab_ready"), 1)
                before_last = sp.value_load(TAB[0:1, 65:66], min_val=1, max_val=TURNS - 1)
                sp.wait_ge(e("sorted_stored"), 2 * 16 * nq)
                if l == 0:
                    sp.wait_ge(sem("pad_stored"), 16)

                def rows(j, n):
                    r = sp.value_load(TAB[0:1, 32 + n:33 + n] if isinstance(n, int) else TAB[0:1, bass.ds(n + 32, 1)], min_val=0, max_val=SORTED)
                    return r

                def weights(j, n):
                    ex = sp.value_load(TAB[0:1, n:n + 1] if isinstance(n, int) else TAB[0:1, bass.ds(n, 1)], min_val=0, max_val=NE - 1)
                    return ex + NE * l

                def load_w(ex, j, x):
                    k = KF if x == 2 else KD
                    sp.dma_start(ESLOT[3 * j + x].rearrange("p (k n) -> p k n", k=k),
                                 expert_w[x][bass.ds(ex, 1)].rearrange("o p k n -> p (o k) n")).then_inc(e(f"ew_loaded{3 * j + x}_"), 16)

                for s in range(WSLOTS):
                    key = book.get(("chunk_done", last_in_slot[l, s]), ("none", 0))
                    after(sp, "pe_" + key[0], key)
                after(sp, "pe_hT", ("hT", l, 1, KD - 1))
                r0 = rows(0, 0)
                sp.dma_start(HE[0], Hs[bass.ds(r0, P), :]).then_inc(e("he_loaded0"), 16)
                for j in range(2):
                    ex = weights(j, j)
                    for x in range(3):
                        load_w(ex, j, x)
                r1 = rows(1, 1)
                sp.dma_start(HE[1], Hs[bass.ds(r1, P), :]).then_inc(e("he_loaded1"), 16)
                def turn_of(i, more):
                    for j in range(2):
                        here = sp.snap(rows(j, 2 * i + j))
                        if more:
                            ex = sp.snap(weights(j, 2 * i + (2 + j)))
                        if more or j == 0:
                            r = sp.snap(rows(j, 2 * i + (2 + j)))
                        if more or j == 0:
                            sp.wait_ge(e("e_in_done1"), 2 * i + j + 1)
                            sp.dma_start(HE[j], Hs[bass.ds(r, P), :]).then_inc(e(f"he_loaded{j}"), 16)
                        if more:
                            sp.wait_ge(e("e_g_done"), 2 * i + j + 1)
                            load_w(ex, j, 0)
                            sp.wait_ge(e("e_u_done"), 2 * i + j + 1)
                            load_w(ex, j, 1)
                            sp.wait_ge(e("e_d_done1"), 2 * i + j + 1)
                            load_w(ex, j, 2)
                        sp.wait_ge(e("e_y_dve"), 2 * i + j + 1)
                        sp.wait_ge(e("e_y_act"), 2 * i + j + 1)
                        sp.dma_start(Ys[bass.ds(here, P), :], YB[j]).then_inc(e(f"y_stored{j}_"), 16)
                with sp.Fori(0, before_last) as i:
                    turn_of(i, True)
                turn_of(before_last, False)
                sp.wait_ge(e("y_stored1_"), 16 * before_last + 16)
                sp.nop().then_inc(e("experts_over"), 1)

            last_in_slot = {}
            for l in range(DEPTH):
                for name, s in layer_chunks(l):
                    last_in_slot[l, s] = (l, name)
            for l in range(DEPTH):
                for name, s in layer_chunks(l):
                    load(l, name)
                experts(l)
            for t in range(LTILES):
                after(sp, "dve_x", (DEPTH - 1, 1, t))
                sp.dma_start(A["out"][0, t * P:(t + 1) * P, :], X[:, t, :]).then_inc(sem("out_stored"), 16)
            sp.wait_ge(sem("out_stored"), 16 * LTILES)

        @block.scalar
        def _(act):
            fn = nc.scalar.activation

            def start():
                for l in range(DEPTH):
                    for name, at in (("mla_q_g", G_MQ), ("mla_k_g", G_MK), ("diff_q_g", G_DQ), ("diff_k_g", G_DK)):
                        g = A[name][l]
                        g = g.rearrange("m d -> (m d)") if len(g.shape) == 2 else g
                        n = g.shape[0]
                        act.dma_start(GAIN[:, l, at:at + n], g.rearrange("(o n) -> o n", o=1).to_broadcast([P, n])).then_inc(sem("gain_loaded"), 16)
                    act.dma_start(LAMR[:, l, :], A["diff_lam"][l].rearrange("m d -> (m d)").rearrange("(o n) -> o n", o=1)
                                  .to_broadcast([P, 4 * DD])).then_inc(sem("lam_loaded"), 16)
                act.dma_start(RB[:, :], A["router_b"].rearrange("(o n) -> o n", o=1).to_broadcast([P, NE])).then_inc(sem("router_loaded"), 16)
                act.dma_start(RW[:, :, :], A["router_w"].rearrange("(k p) n -> p k n", p=P)).then_inc(sem("router_loaded"), 16)
                ps = bank_read(act, ("small", 0))
                sig(fn(CT[:, 0, :], ps[:, 0:2 * KD], ACT.Exp, scale=-1.0), "act_c", 0)
                after(act, "dve_lam", 0)
                sig(fn(LT[:, 4:8], LT[:, 0:4], ACT.Exp), "act_lam", 0)

            def norm(l, f):
                nt = TILES if f == 0 else nq_of(l)
                for t in range(nt):
                    if f == 1:
                        after(act, "dve_x", (l, 0, 1, t))
                        out = OWN[:, 1024 * t:1024 * (t + 1)]
                    else:
                        if l == 0:
                            act.wait_ge(sem(f"x_loaded{t}"), 16)
                        else:
                            after(act, "dve_x", (l - 1, 1, t))
                            if t == 0:
                                after(act, "dve_x", (l - 1, 1, TILES - 1))
                        out = XN[:, t, :]
                    sig(fn(out, X[:, t, :], ACT.Square, accum_out=SSX[:, t:t + 1]), "act_ssx", (l, f, t))
                after(act, "dve_scl", (l, f))
                for k in range(1, KD, 2):
                    ps = bank_read(act, ("hT", l, f, k))
                    if (l, f, k) == (0, 0, 1):
                        first_hidden(act)
                    for s, c0, cn in streams(nt * P):
                        ins = fn(HT[:, k, c0:c0 + cn], ps[:, c0:c0 + cn], ACT.Identity,
                                 bias=MOD[:, 24 * f + k, s:s + 1], scale=SCL[:, f, k, s:s + 1])
                        last = s == streams(nt * P)[-1][0]
                        sig(ins, "act_hT", (l, f, k) if last else (l, f, k, s))
                    last_read(("hT", l, f, k), "act_hT", (l, f, k))

            def prep(l):
                early, late = norm_tasks(l)
                tasks = early + late
                done = 0

                def evac_t(i, task):
                    kind, t, half = task
                    ps = bank_read(act, ("T", l, i))
                    if kind in ("ckv", "cq"):
                        n, dst, v = (2, CKT, V_KVG) if kind == "ckv" else (4, CQT, V_QG)
                        for b in range(n):
                            sig(fn(dst[:, b, t * P:(t + 1) * P], ps[:, b * P:(b + 1) * P], ACT.Copy, scale=VEC[:, l, v + b:v + b + 1]),
                                "act_T", (l, i) if b == n - 1 else (l, i, b))
                    elif kind in ("ukv", "uq"):
                        dst = KTM if kind == "ukv" else QT
                        sig(fn(dst[0:HQ, 4 * half:4 * half + 4, t * P:(t + 1) * P],
                               ps[0:HQ, :].rearrange("p (h n) -> p h n", h=4), ACT.Copy), "act_T", (l, i))
                    else:
                        dst = KTD if kind == "kd" else QTD
                        sig(fn(dst[:, :, t * P:(t + 1) * P], ps[:, :].rearrange("p (h n) -> p h n", h=4), ACT.Copy), "act_T", (l, i))
                    last_read(("T", l, i), "act_T", (l, i))

                for i, (kind, t, half) in enumerate(tasks):
                    if i == len(early):
                        for tt in range(TILES):
                            key = ("proj", l, "vd", tt, 0)
                            ps = bank_read(act, key)
                            sig(fn(VS[:, 1, tt, :], ps[:, :], ACT.Copy), "act_vd", (l, tt))
                            last_read(key, "act_vd", (l, tt))
                        while done < i:
                            evac_t(done, tasks[done])
                            done += 1
                    ps = bank_read(act, ("proj", l, kind, t, half))
                    if kind == "ukv":
                        sig(fn(VS[:, 0, t, 256 * half:256 * (half + 1)].rearrange("p (h d) -> p h d", h=4),
                               ps[:, :].rearrange("p (h d) -> p h d", h=4)[:, :, NOPE:NOPE + MV], ACT.Copy), "act_vm", (l, t, half))
                    if i >= 2:
                        after(act, "dve_ss", (l, i - 2))
                    n = {"ckv": OFF_KD, "uq": 384}.get(kind, 512)
                    sig(fn(SQ[i % 2][:, 0:n], ps[:, 0:n], ACT.Square), "act_sq", (l, i))
                    if i - T_LAG >= done:
                        evac_t(done, tasks[done])
                        done += 1
                while done < len(tasks):
                    evac_t(done, tasks[done])
                    done += 1

            def gate_rows(l, which):
                for s in range(2 if l < DEPTH - 1 else 1):
                    for h in range(2):
                        key = ("gate", l, which, s, h)
                        ps = bank_read(act, key)
                        sig(fn(GATE[:, s, 512 * h:512 * (h + 1)], ps[:, :], ACT.Copy, scale=0.5 if which == 0 else 1.0),
                            "act_gate", (l, which, s, h))
                        last_read(key, "act_gate", (l, which, s, h))

            def attention(l):
                units = attention_units(l)
                nbuf, owner = [0], {}

                def probabilities(u, kind, t, h):
                    k0, kn = keys_of(t)
                    for m in range(1 if kind == "m" else 2):
                        b = nbuf[0] % NP
                        nbuf[0] += 1
                        if b in owner:
                            after(act, "pe_PT", ("PT", l, owner[b]))
                        owner[b] = u
                        book["pbuf" if m == 0 else "pbuf1", (l, u)] = b
                        c = (2 * u + m) % 8
                        after(act, "dve_mx", (l, u, m))
                        ps = bank_read(act, ("S", l, u, m))
                        name, key = ("act_p", (l, u)) if kind == "m" else ("act_pd", (l, u, m))
                        sig(fn(PB[b][:, 0:kn * P], ps[:, 0:kn * P], ACT.Exp, bias=MB[:, c:c + 1],
                               scale=MLA_SCALE if kind == "m" else DIFF_SCALE, accum_out=RSUM[:, c:c + 1]), name, key)
                        last_read(("S", l, u, m), name, key)

                def transposed(u, kind, t, h):
                    if u % 2:
                        return
                    k0, kn = keys_of(t)
                    if u >= 2:
                        key = book.get(("pv_done", (l, u - 2)), ("none", 0))
                        after(act, "pe_O", key)
                    ps = bank_read(act, ("PT", l, u))
                    sig(fn(PTS[0][:, 0:kn * P], ps[:, 0:kn * P], ACT.Copy), "act_pts", (l, u))
                    last_read(("PT", l, u), "act_pts", (l, u))

                def out_t(kind, t):
                    key = ("OT", l, kind, t)
                    ps = bank_read(act, key)
                    scale = 1.0 if kind == "m" else SUBG[:, 0:1]
                    sig(fn(OT[:, int(kind == "d"), :, t * P:(t + 1) * P], ps[:, :].rearrange("p (b n) -> p b n", b=4), ACT.Copy, scale=scale),
                        "act_oT", (l, kind, t))
                    last_read(key, "act_oT", (l, kind, t))

                after(act, "dve_subg", l)
                waiting = []
                for i in range(len(units) + A_VLAG + 2):
                    if i < len(units):
                        probabilities(i, *units[i])
                    if 0 <= i - A_TLAG < len(units):
                        transposed(i - A_TLAG, *units[i - A_TLAG])
                    if 0 <= i - A_VLAG < len(units):
                        kind, t, h = units[i - A_VLAG]
                        if h == (MH if kind == "m" else DH) - 1:
                            if kind == "d":
                                ps = bank_read(act, ("O", l, "d", t))
                                sig(fn(RTF[:, 0:512], ps[:, :], ACT.Square), "act_osq", (l, t))
                            waiting.append((i + 2, kind, t))
                    while waiting and waiting[0][0] <= i:
                        out_t(*waiting.pop(0)[1:])

            def merge(l):
                n = nq_of(l) * P
                for b in range(KD):
                    for j in range(2):
                        if b >= 2:
                            after(act, "dve_mg", (l, b - 2, j))
                        ps = bank_read(act, ("mg", l, b, j))
                        sig(fn(MT[b % 2][j][:, 0:n], ps[:, 0:n], ACT.Tanh, scale=0.5), "act_mg", (l, b, j))
                        last_read(("mg", l, b, j), "act_mg", (l, b, j))

            def router(l):
                nt = nq_of(l)
                ps = bank_read(act, ("logit", l))
                sig(fn(AFF[:, 0:nt * NE], ps[:, 0:nt * NE], ACT.Exp, scale=-1.0), "act_rt", l)
                last_read(("logit", l), "act_rt", l)
                for t in range(nt):
                    key = ("htok", l, t, 0)
                    ps = bank_read(act, key)
                    sig(fn(HTOK[t][:, 0:512], ps[:, :], ACT.Copy), "act_htok", (l, t))
                    last_read(key, "act_htok", (l, t))

            def shared(l):
                nt = nq_of(l)
                for f in range(KF):
                    if f >= 2:
                        after(act, "dve_sh", (l, f - 2))
                    ps = bank_read(act, ("sh", l, f, 0))
                    sig(fn(STH[f % 2][:, 0:nt * P], ps[:, 0:nt * P], ACT.Tanh, scale=0.5), "act_sh", (l, f))
                for t in range(nt):
                    for h in range(2):
                        key = ("shd", l, t, h)
                        ps = bank_read(act, key)
                        sig(fn(YS[:, t, 512 * h:512 * (h + 1)], ps[:, :], ACT.Copy), "act_ys", (l, t, h))
                        last_read(key, "act_ys", (l, t, h))

            def experts(l):
                e = lambda name: sem(f"{name}{l}")
                act.wait_ge(e("tab_ready"), 1)
                turns = act.value_load(TAB[0:1, 64:65], min_val=1, max_val=TURNS)

                def rows(j):
                    fn(HEX[j][:, 4:8, :], PS[1][:, :].rearrange("p (b n) -> p b n", b=4), ACT.Copy).then_inc(e("e_hex_act"), 1)

                act.wait_ge(e("e_in_done1"), 1)
                rows(0)
                with act.Fori(0, turns) as i:
                    for j in range(2):
                        act.wait_ge(e("e_g_done"), 2 * i + (j + 1))
                        fn(THB[j], PS[2][:, :], ACT.Tanh, scale=0.5).then_inc(e("e_th"), 1)
                        act.wait_ge(e("e_in_done1"), 2 * i + (j + 2))
                        rows(1 - j)
                        act.wait_ge(e("e_ht_done"), 2 * i + (j + 1))
                        fn(HTX[j][:, :, :], PS[4][:, :].rearrange("p (b n) -> p b n", b=4), ACT.Copy).then_inc(e("e_htx"), 1)
                        act.wait_ge(e(f"y_stored{j}_"), 16 * i)
                        act.wait_ge(e("e_d_done1"), 2 * i + (j + 1))
                        fn(YB[j][:, 512:1024], PS[6][:, :], ACT.Copy).then_inc(e("e_y_act"), 1)

            start()
            for l in range(DEPTH):
                norm(l, 0)
                prep(l)
                attention(l)
                gate_rows(l, 0)
                merge(l)
                norm(l, 1)
                router(l)
                shared(l)
                gate_rows(l, 1)
                experts(l)

        @block.vector
        def _(dve):
            tt, ts, stt = nc.vector.tensor_tensor, nc.vector.tensor_scalar, nc.vector.scalar_tensor_tensor
            red, cp, rec = nc.vector.tensor_reduce, nc.vector.tensor_copy, nc.vector.reciprocal

            def link(ins):
                chained(dve, "dve_step", ins)

            def start():
                dve.wait_ge(sem("lam_loaded"), 16 * DEPTH)
                r = LAMR.rearrange("p l (a b d) -> p l a b d", a=2, b=2)
                prod = RTF[:, 0:DEPTH * 2 * DD].rearrange("p (l a d) -> p l a d", l=DEPTH, a=2)
                for l in range(DEPTH):
                    link(tt(prod[:, l], r[:, l, :, 0], r[:, l, :, 1], ALU.mult))
                sig(red(LT[:, 0:4], RTF[:, 0:256].rearrange("p (a d) -> p a d", a=4), AX.X, ALU.add), "dve_lam", 0)
                after(dve, "act_lam", 0)
                for l in range(DEPTH):
                    lam_init = 0.8 - 0.6 * math.exp(-0.3 * l)
                    link(tt(NLAM[:, l:l + 1], LT[:, 5 + 2 * l:6 + 2 * l], LT[:, 4 + 2 * l:5 + 2 * l], ALU.subtract))
                    link(ts(NLAM[:, l:l + 1], NLAM[:, l:l + 1], -lam_init, None, ALU.add))
                after(dve, "act_c", 0)
                ps = bank_read(dve, ("small", 0))
                link(ts(CT[:, 1, :], CT[:, 0, :], 1.0, None, ALU.add))
                link(rec(CT[:, 0, :], CT[:, 1, :]))
                sig(tt(CS[:, :], CT[:, 0, :], ps[:, 0:2 * KD], ALU.mult), "dve_c", 0)
                for l in range(DEPTH):
                    sig(cp(VEC[:, l, :], ps[:, P * (l + 1):P * (l + 1) + V_END]), "dve_vec", l)
                last_read(("small", 0), "dve_vec", DEPTH - 1)
                after(dve, "dve_vec", DEPTH - 1)

            def modulation(l, part):
                m0, m1 = (0, 16) if part == 0 else (16, 48)
                ps = bank_read(dve, ("ada", l, part))
                b = VEC[:, l, V_ADAB + m0:V_ADAB + m1].rearrange("p (m o) -> p m o", o=1).to_broadcast([P, m1 - m0, 2])
                sig(tt(MOD[:, m0:m1, :], ps[:, 2 * m0:2 * m1].rearrange("p (m s) -> p m s", s=2), b, ALU.add), "dve_mod", (l, part))
                last_read(("ada", l, part), "dve_mod", (l, part))
                after(dve, "dve_mod", (l, part))
                f, sc, v = (0, 8, V_AG) if part == 0 else (1, 32, V_FG)
                g = VEC[:, l, v:v + KD].rearrange("p (m o) -> p m o", o=1).to_broadcast([P, KD, 2])
                sig(stt(SCL[:, f], MOD[:, sc:sc + KD, :], 1.0, g, ALU.add, ALU.mult), "dve_scl", (l, f))
                after(dve, "dve_scl", (l, f))

            def norm(l, f):
                nt = TILES if f == 0 else nq_of(l)
                after(dve, "pool_rx", (l, f))
                for t in range(nt):
                    sig(ts(XN[:, t, :], X[:, t, :], RX[:, t:t + 1], None, ALU.mult), "dve_xn", (l, f, t))

            def hidden(l, f):
                nt = TILES if f == 0 else nq_of(l)
                for k in range(0, KD, 2):
                    ps = bank_read(dve, ("hT", l, f, k))
                    if (l, f, k) == (0, 0, 0):
                        first_hidden(dve)
                    st = streams(nt * P)
                    for s, c0, cn in st:
                        sig(ts(HT[:, k, c0:c0 + cn], ps[:, c0:c0 + cn], SCL[:, f, k, s:s + 1], MOD[:, 24 * f + k, s:s + 1], ALU.mult, ALU.add),
                            "dve_hT", (l, f, k) if s == st[-1][0] else (l, f, k, s))
                    last_read(("hT", l, f, k), "dve_hT", (l, f, k))

            def wide(col, n, w):
                return col.rearrange("p (g o) -> p g o", o=1).to_broadcast([P, n, w])

            def prep(l):
                early, late = norm_tasks(l)
                tasks = early + late

                def sums(i):
                    kind, t, half = tasks[i]
                    after(dve, "act_sq", (l, i))
                    if i >= 4:
                        after(dve, "pool_r", (l, i - 4))
                    sq, ss = SQ[i % 2], SS[:, i % 4]
                    if kind == "ckv":
                        sig(red(ss[:, 0:1], sq[:, 0:KVR], AX.X, ALU.add), "dve_ss", (l, i, 0))
                        ins = red(ss[:, 1:2], sq[:, KVR:OFF_KD], AX.X, ALU.add)
                    elif kind == "cq":
                        ins = red(ss[:, 0:1], sq[:, :], AX.X, ALU.add)
                    elif kind == "ukv":
                        ins = red(ss[:, 0:4], sq.rearrange("p (h d) -> p h d", h=4)[:, :, 0:NOPE], AX.X, ALU.add)
                    elif kind == "uq":
                        q = sq[:, 0:384].rearrange("p (h d) -> p h d", h=4)
                        sig(red(ss[:, 0:4], q[:, :, 0:NOPE], AX.X, ALU.add), "dve_ss", (l, i, 0))
                        ins = red(ss[:, 4:8], q[:, :, NOPE:HQ], AX.X, ALU.add)
                    else:
                        ins = red(ss[:, 0:8], sq.rearrange("p (h d) -> p h d", h=8), AX.X, ALU.add)
                    sig(ins, "dve_ss", (l, i))

                def scale(i):
                    kind, t, half = tasks[i]
                    key = ("proj", l, kind, t, half)
                    after(dve, "pool_r", (l, i))
                    if i >= 4:
                        after(dve, "pe_T", ("T", l, i - 4))
                    ps, r, tm = bank_read(dve, key), RR[:, i % 4], TM[i % 4]
                    name = tm_sem(kind) if kind in ("ckv", "cq") else "dve_sc"
                    if kind == "ckv":
                        sig(ts(KR[:, t, :], ps[:, KVR:OFF_KD], r[:, 1:2], None, ALU.mult), "dve_kr", (l, t))
                        ins = ts(tm[:, 0:KVR], ps[:, 0:KVR], r[:, 0:1], None, ALU.mult)
                    elif kind == "cq":
                        ins = ts(tm, ps[:, :], r[:, 0:1], None, ALU.mult)
                    elif kind == "ukv":
                        ins = tt(tm[:, 0:384].rearrange("p (h d) -> p h d", h=4)[:, :, 0:NOPE],
                                 ps[:, :].rearrange("p (h d) -> p h d", h=4)[:, :, 0:NOPE], wide(r[:, 0:4], 4, NOPE), ALU.mult)
                    elif kind == "uq":
                        q, o = (x[:, 0:384].rearrange("p (h d) -> p h d", h=4) for x in (ps, tm))
                        sig(tt(o[:, :, 0:NOPE], q[:, :, 0:NOPE], wide(r[:, 0:4], 4, NOPE), ALU.mult), name, (l, i, 0))
                        ins = tt(o[:, :, NOPE:HQ], q[:, :, NOPE:HQ], wide(r[:, 4:8], 4, ROPE), ALU.mult)
                    else:
                        ins = tt(tm.rearrange("p (h d) -> p h d", h=8), ps[:, :].rearrange("p (h d) -> p h d", h=8),
                                 wide(r[:, 0:8], 8, DD), ALU.mult)
                    sig(ins, name, (l, i))
                    last_read(key, name, (l, i))

                sums(0)
                for i in range(len(tasks)):
                    if i + 1 < len(tasks) and i + 1 != len(early):
                        sums(i + 1)
                    scale(i)
                    if i + 1 == len(early):
                        sums(i + 1)

            def gate_diagonals(l, which):
                m0 = 16 if which == 0 else 40
                for s in range(2 if l < DEPTH - 1 else 1):
                    for h in range(2):
                        if s:
                            after(dve, "pe_gate", ("gate", l, which, s - 1, h))
                        for b in range(4):
                            g = MOD[:, m0 + 4 * h + b, s:s + 1]
                            sig(ts(DIAG[:, h, b * P:(b + 1) * P], ident, g, None, ALU.mult), "dve_diag",
                                (l, which, s, h) if b == 3 else (l, which, s, h, b))

            def attention(l):
                units = attention_units(l)
                lam_init = 0.8 - 0.6 * math.exp(-0.3 * l)
                sig(ts(SUBG[:, :], VEC[:, l, V_SUB:V_SUB + 1], 1.0 - lam_init, None, ALU.mult), "dve_subg", l)

                def maxima(u, kind, t, h):
                    k0, kn = keys_of(t)
                    for m in range(1 if kind == "m" else 2):
                        c = (2 * u + m) % 8
                        ps = bank_read(dve, ("S", l, u, m))
                        link(red(MX[:, c:c + 1], ps[:, 0:kn * P], AX.X, ALU.max, negate=True))
                        sig(ts(MB[:, c:c + 1], MX[:, c:c + 1], MLA_SCALE if kind == "m" else DIFF_SCALE, None, ALU.mult),
                            "dve_mx", (l, u, m))

                def weights(u, kind, t, h):
                    k0, kn = keys_of(t)
                    c = (2 * u) % 8
                    if kind == "m":
                        after(dve, "act_p", (l, u))
                        sig(rec(RINV[:, t % 2, h:h + 1], RSUM[:, c:c + 1]), "dve_rinv", (l, u))
                        return
                    after(dve, "act_pd", (l, u, 1))
                    link(rec(RDIF[:, c:c + 2], RSUM[:, c:c + 2]))
                    link(tt(RDIF[:, c + 1:c + 2], RDIF[:, c + 1:c + 2], NLAM[:, l:l + 1], ALU.mult))
                    b0, b1 = (PB[book.get((x, (l, u)), 0)][:, 0:kn * P] for x in ("pbuf", "pbuf1"))
                    link(ts(b1, b1, RDIF[:, c + 1:c + 2], None, ALU.mult))
                    sig(stt(b0, b0, RDIF[:, c:c + 1], b1, ALU.mult, ALU.add), "dve_a", (l, u))

                def transposed(u, kind, t, h):
                    if u % 2 == 0:
                        return
                    k0, kn = keys_of(t)
                    if u >= 2:
                        after(dve, "pe_O", book.get(("pv_done", (l, u - 2)), ("none", 0)))
                    ps = bank_read(dve, ("PT", l, u))
                    sig(cp(PTS[1][:, 0:kn * P], ps[:, 0:kn * P]), "dve_pts", (l, u))
                    last_read(("PT", l, u), "dve_pts", (l, u))

                def out_rows(kind, t):
                    ps = bank_read(dve, ("O", l, kind, t))
                    before_ = ("OT", l, "m", t) if kind == "d" else ("OT", l, "d", t - 1) if t else None
                    if before_:
                        after(dve, "pe_OT", before_)
                    if kind == "m":
                        after(dve, "dve_rinv", (l, 12 * t + MH - 1))
                        r, n, w = RINV[:, t % 2, :], MH, MV
                    else:
                        after(dve, "pool_ro", (l, t))
                        r, n, w = RO, DH, DV
                    sig(tt(OTM.rearrange("p (h d) -> p h d", h=n), ps[:, :].rearrange("p (h d) -> p h d", h=n), wide(r, n, w), ALU.mult),
                        "dve_o", (l, kind, t))
                    last_read(("O", l, kind, t), "dve_o", (l, kind, t))

                waiting = []
                for i in range(len(units) + A_VLAG + 2):
                    if i < len(units):
                        maxima(i, *units[i])
                    if 0 <= i - 1 < len(units):
                        weights(i - 1, *units[i - 1])
                    if 0 <= i - A_TLAG < len(units):
                        transposed(i - A_TLAG, *units[i - A_TLAG])
                    if 0 <= i - A_VLAG < len(units):
                        kind, t, h = units[i - A_VLAG]
                        if h == (MH if kind == "m" else DH) - 1:
                            if kind == "d":
                                after(dve, "act_osq", (l, t))
                                sig(red(SSO[:, :], RTF[:, 0:512].rearrange("p (h d) -> p h d", h=DH), AX.X, ALU.add), "dve_sso", (l, t))
                            waiting.append((i + 1, kind, t))
                    while waiting and waiting[0][0] <= i:
                        out_rows(*waiting.pop(0)[1:])

            def merge(l):
                n = nq_of(l) * P
                for b in range(KD):
                    for j in range(2):
                        if b >= 2:
                            after(dve, "pool_y", (l, b - 2))
                        after(dve, "act_mg", (l, b, j))
                        key = ("mg", l, b, 2 + j)
                        ps = bank_read(dve, key)
                        sig(stt(MY[b % 2][j][:, 0:n], MT[b % 2][j][:, 0:n], 1.0, ps[:, 0:n], ALU.add, ALU.mult), "dve_mg", (l, b, j))
                        last_read(key, "dve_mg", (l, b, j))

            def out_proj(l):
                after(dve, "act_gate", (l, 0, 1 if l < DEPTH - 1 else 0, 1))
                for h in range(2):
                    for t in range(nq_of(l)):
                        key = ("out", l, h, t)
                        ps = bank_read(dve, key)
                        tmp = STG[:, 512 * (t % 2):512 * (t % 2 + 1)]
                        cols = slice(512 * h, 512 * (h + 1))
                        sig(tt(tmp, ps[:, :], GATE[:, t // LTILES, cols], ALU.mult), "dve_og", (l, h, t))
                        last_read(key, "dve_og", (l, h, t))
                        after(dve, "dve_og", (l, h, t))
                        sig(tt(X[:, t, cols], X[:, t, cols], tmp, ALU.add), "dve_x", (l, 0, h, t))

            def htok(l):
                for t in range(nq_of(l)):
                    key = ("htok", l, t, 1)
                    ps = bank_read(dve, key)
                    sig(cp(HTOK[t][:, 512:1024], ps[:, :]), "dve_htok", (l, t))
                    last_read(key, "dve_htok", (l, t))

            def route_choice(l):
                nt = nq_of(l)
                g3 = lambda x, a, b: x.rearrange("p (a b) -> p a b", a=a)
                aff, sel, t1 = (x[:, 0:nt * NE] for x in (AFF, SEL, TMPR))
                after(dve, "act_rt", l)
                dve.wait_ge(sem("router_loaded"), 32)
                link(ts(t1, aff, 1.0, None, ALU.add))
                link(rec(aff, t1))
                rb = RB[:, :].rearrange("p (o n) -> p o n", o=1).to_broadcast([P, nt, NE])
                link(tt(g3(sel, nt, NE), g3(aff, nt, NE), rb, ALU.add))
                s4 = g3(sel, nt * NG, EPG)
                pr = PAIR[:, 0:nt * NG * 6].rearrange("p (g n) -> p g n", n=6)
                link(tt(pr[:, :, 0:3], s4[:, :, 0:3], s4[:, :, 1:4], ALU.add))
                link(tt(pr[:, :, 3:5], s4[:, :, 0:2], s4[:, :, 2:4], ALU.add))
                link(tt(pr[:, :, 5:6], s4[:, :, 0:1], s4[:, :, 3:4], ALU.add))
                gs, gm, gk = (GRP[:, i, 0:nt * NG] for i in range(3))
                link(red(gs, pr, AX.X, ALU.max))
                link(red(gm[:, 0:nt], g3(gs, nt, NG), AX.X, ALU.max))
                link(tt(g3(gk, nt, NG), g3(gs, nt, NG), wide(gm[:, 0:nt], nt, NG), ALU.is_equal))
                tie = CST[:, C_TIE:C_TIE + NG].rearrange("p (o n) -> p o n", o=1).to_broadcast([P, nt, NG])
                link(tt(g3(gk, nt, NG), g3(gk, nt, NG), tie, ALU.mult))
                link(red(gm[:, 0:nt], g3(gk, nt, NG), AX.X, ALU.max))
                link(tt(g3(gk, nt, NG), g3(gk, nt, NG), wide(gm[:, 0:nt], nt, NG), ALU.is_equal))
                link(tt(s4, s4, wide(gk, nt * NG, EPG), ALU.mult))
                link(ts(gs, gk, 1.0, BIG, ALU.subtract, ALU.mult))
                link(tt(s4, s4, wide(gs, nt * NG, EPG), ALU.add))
                for t in range(nt):
                    link(nc.vector.max(out=BEST[:, t, :], in_=sel[:, NE * t:NE * (t + 1)]))
                    link(nc.vector.max_index(out=BIDX[:, t, :], in_max=BEST[:, t, :], in_values=sel[:, NE * t:NE * (t + 1)]))
                link(cp(FIDX[:, 0:nt, :], BIDX[:, 0:nt, 0:2]))
                iota = CST[:, C_IOTA:C_IOTA + NE].rearrange("p (o n) -> p o n", o=1).to_broadcast([P, nt, NE])
                for k in range(2):
                    link(tt(HOT[k][:, 0:nt, :], iota, FIDX[:, 0:nt, k:k + 1].to_broadcast([P, nt, NE]), ALU.is_equal))
                    link(tt(g3(t1, nt, NE), HOT[k][:, 0:nt, :], g3(aff, nt, NE), ALU.mult))
                    link(red(WTS[:, 0:nt, k], g3(t1, nt, NE), AX.X, ALU.add))
                link(tt(gm[:, 0:nt], WTS[:, 0:nt, 0], WTS[:, 0:nt, 1], ALU.add))
                link(rec(gs[:, 0:nt], gm[:, 0:nt]))
                link(tt(WTS[:, 0:nt, :], WTS[:, 0:nt, :], wide(gs[:, 0:nt], nt, 2), ALU.mult))
                sig(tt(MSK[:, 0:nt, :], HOT[0][:, 0:nt, :], HOT[1][:, 0:nt, :], ALU.add), "dve_mask", l)

            def route_places(l):
                nt = nq_of(l)
                g3 = lambda x, a: x.rearrange("p (a b) -> p a b", a=a)
                ps = bank_read(dve, ("place", l))
                cnt, inc, off = (CNT[:, i, :] for i in range(3))
                link(cp(cnt, ps[:, 64:64 + NE]))
                link(nc.vector.tensor_tensor_scan(inc, ones[:, 0:NE], cnt, 0.0, ALU.mult, ALU.add))
                link(tt(off, inc, cnt, ALU.subtract))
                t1 = TMPR[:, 0:nt * NE]
                off_w = off.rearrange("p (o n) -> p o n", o=1).to_broadcast([P, nt, NE])
                sig(tt(g3(SEL[:, 0:nt * NE], nt), g3(ps[:, 0:nt * NE], nt), off_w, ALU.add), "dve_plc", l)
                last_read(("place", l), "dve_plc", l)
                after(dve, "dve_plc", l)
                for k in range(2):
                    link(tt(g3(t1, nt), HOT[k][:, 0:nt, :], g3(SEL[:, 0:nt * NE], nt), ALU.mult))
                    link(red(SLF[:, 0:nt, k], g3(t1, nt), AX.X, ALU.add))
                sig(cp(SLOT[:, 0:nt, :], SLF[:, 0:nt, :]), "dve_slot", l)
                rc = CST[:, C_RCAND:C_RCAND + CAND]
                act_, run, row, hit = (CND[:, i, :] for i in range(4))
                link(tt(g3(act_, NE), wide(cnt, NE, TILES), g3(rc, NE), ALU.is_gt))
                link(nc.vector.tensor_tensor_scan(run, CONES, act_, 0.0, ALU.mult, ALU.add))
                link(tt(g3(row, NE), wide(off, NE, TILES), g3(rc, NE), ALU.add))
                link(stt(hit, run, CST[:, C_JOB:C_JOB + 1], act_, ALU.is_equal, ALU.mult))
                link(tt(act_, hit, CST[:, C_ECAND:C_ECAND + CAND], ALU.mult))
                link(red(JOBC[:, 0:1], act_, AX.X, ALU.add))
                link(tt(row, hit, row, ALU.mult))
                link(red(JOBC[:, 1:2], row, AX.X, ALU.add))
                link(red(JOBC[:, 2:3], hit, AX.X, ALU.add))
                link(ts(JOBC[:, 2:3], JOBC[:, 2:3], -float(SORTED), float(SORTED), ALU.mult, ALU.add))
                sig(tt(JOBC[:, 1:2], JOBC[:, 1:2], JOBC[:, 2:3], ALU.add), "dve_jobcol", l)
                link(ts(TABI[:, 0:1], run[0:1, CAND - 1:CAND], 1.0, None, ALU.add))
                link(ts(TAB[0:1, 64:65], TABI[:, 0:1], 1, None, ALU.arith_shift_right))
                link(ts(TAB[0:1, 65:66], TAB[0:1, 64:65], 1.0, None, ALU.subtract))

            def route_table(l):
                ps = bank_read(dve, ("jobs", l))
                link(cp(TAB[0:1, 0:32], ps[0:1, 0:32]))
                cp(TAB[0:1, 32:64], ps[0:1, P:P + 32]).then_inc(sem(f"tab_ready{l}"), 1)
                book["read", ("jobs", l)] = (f"tab_ready{l}", 0)
                book[f"tab_ready{l}", 0] = 1

            def shared(l, f):
                n = nq_of(l) * P
                after(dve, "act_sh", (l, f))
                ps = bank_read(dve, ("sh", l, f, 0))
                sig(stt(SVV[f % 2][:, 0:n], STH[f % 2][:, 0:n], 1.0, ps[:, 0:n], ALU.add, ALU.mult), "dve_sv", (l, f))
                last_read(("sh", l, f, 0), "dve_sv", (l, f))
                after(dve, "dve_sv", (l, f))
                ps = bank_read(dve, ("sh", l, f, 1))
                sig(stt(HET[:, f, 0:n], SVV[f % 2][:, 0:n], 0.5, ps[:, 0:n], ALU.mult, ALU.mult), "dve_sh", (l, f))
                last_read(("sh", l, f, 1), "dve_sh", (l, f))

            def experts(l):
                e = lambda name: sem(f"{name}{l}")
                dve.wait_ge(e("tab_ready"), 1)
                turns = dve.value_load(TAB[0:1, 64:65], min_val=1, max_val=TURNS)

                def rows(j):
                    cp(HEX[j][:, 0:4, :], PS[0][:, :].rearrange("p (b n) -> p b n", b=4)).then_inc(e("e_hex_dve"), 1)

                dve.wait_ge(e("e_in_done0"), 1)
                rows(0)
                with dve.Fori(0, turns) as i:
                    for j in range(2):
                        dve.wait_ge(e("e_th"), 2 * i + (j + 1))
                        stt(THB[j], THB[j], 1.0, PS[2][:, :], ALU.add, ALU.mult).then_inc(e("e_v"), 1)
                        dve.wait_ge(e("e_v"), 2 * i + (j + 1))
                        dve.wait_ge(e("e_u_done"), 2 * i + (j + 1))
                        stt(HID[j], THB[j], 0.5, PS[3][:, :], ALU.mult, ALU.mult).then_inc(e("e_hid_done"), 1)
                        dve.wait_ge(e("e_in_done0"), 2 * i + (j + 2))
                        rows(1 - j)
                        if j == 1:
                            dve.wait_ge(e("y_stored0_"), 16 * i + 16)
                        else:
                            dve.wait_ge(e("y_stored1_"), 16 * i)
                        dve.wait_ge(e("e_d_done0"), 2 * i + (j + 1))
                        cp(YB[j][:, 0:512], PS[5][:, :]).then_inc(e("e_y_dve"), 1)
                dve.wait_ge(e("experts_over"), 1)

            def combine(l):
                for t in range(nq_of(l)):
                    for k in range(2):
                        dve.wait_ge(sem(f"y_gathered{l}{t % 2}{k}"), 16 * (t // 2 + 1))
                    y0, y1 = YG[t % 2]
                    link(ts(y0, y0, WTS[:, t, 0:1], None, ALU.mult))
                    link(stt(y0, y1, WTS[:, t, 1:2], y0, ALU.mult, ALU.add))
                    link(tt(y0, y0, YS[:, t, :], ALU.add))
                    link(tt(y0, y0, GATE[:, t // LTILES, :], ALU.mult))
                    sig(tt(X[:, t, :], X[:, t, :], y0, ALU.add), "dve_x", (l, 1, t))

            start()
            for l in range(DEPTH):
                norm(l, 0) if l else None
                modulation(l, 0)
                if l == 0:
                    norm(l, 0)
                hidden(l, 0)
                prep(l)
                modulation(l, 1)
                attention(l)
                after(dve, "pe_OT", ("OT", l, "d", nq_of(l) - 1))
                gate_diagonals(l, 0)
                merge(l)
                out_proj(l)
                norm(l, 1)
                hidden(l, 1)
                route_choice(l)
                htok(l)
                shared(l, 0)
                route_places(l)
                shared(l, 1)
                shared(l, 2)
                route_table(l)
                shared(l, 3)
                gate_diagonals(l, 1)
                after(dve, "act_gate", (l, 1, 1 if l < DEPTH - 1 else 0, 1))
                after(dve, "act_ys", (l, nq_of(l) - 1, 1))
                experts(l)
                combine(l)

        @block.gpsimd
        def _(pool):
            gt, gs_, gc = nc.gpsimd.tensor_tensor, nc.gpsimd.tensor_scalar, nc.gpsimd.tensor_copy

            def link(ins):
                chained(pool, "pool_step", ins)

            def start():
                link(pool.memset(HALF[:, :], -0.5))
                link(pool.memset(ZERO, 0.0))
                pool.dma_start(Hs[SORTED:SORTED + P, :], ZERO).then_inc(sem("pad_stored"), 16)
                pool.wait_ge(sem("gain_loaded"), 16 * 4 * DEPTH)
                pool.wait_ge(sem("const_loaded"), 16)

            def norm(l, f):
                nt = TILES if f == 0 else nq_of(l)
                after(pool, "act_ssx", (l, f, nt - 1))
                link(gs_(RX[:, 0:nt], SSX[:, 0:nt], 1.0 / D, EPS, ALU.mult, ALU.add))
                sig(gt(RX[:, 0:nt], RX[:, 0:nt], HALF[:, 0:nt], ALU.pow), "pool_rx", (l, f))

            def rotate(view, cos, sin, groups, q):
                x1, x2 = view
                shape = [P, groups, 2, q]
                c, s = (x.rearrange("p (o a q) -> p o a q", o=1, a=2).to_broadcast(shape) for x in (cos, sin))
                a, b, cc, d = (RT[:, i, 0:groups * 2 * q].rearrange("p (g a q) -> p g a q", g=groups, a=2) for i in range(4))
                link(gt(a, x1, c, ALU.mult))
                link(gt(b, x2, s, ALU.mult))
                link(gt(cc, x1, s, ALU.mult))
                link(gt(d, x2, c, ALU.mult))
                link(gt(x1, a, b, ALU.subtract))
                return gt(x2, cc, d, ALU.add)

            def halves(x, groups, q):
                v = x.rearrange("p g (a h q) -> p g a h q", a=2, h=2)
                return v[:, :, :, 0, :], v[:, :, :, 1, :]

            def prep(l):
                early, late = norm_tasks(l)
                tasks = early + late

                def roots(i):
                    kind, t, half = tasks[i]
                    after(pool, "dve_ss", (l, i))
                    ss, r = SS[:, i % 4], RR[:, i % 4]
                    parts = {"ckv": [(0, 1, KVR), (1, 2, ROPE)], "cq": [(0, 1, QR)], "ukv": [(0, 4, NOPE)],
                             "uq": [(0, 4, NOPE), (4, 8, ROPE)]}.get(kind, [(0, 8, DD)])
                    for a, b, w in parts:
                        link(gs_(r[:, a:b], ss[:, a:b], 1.0 / w, EPS, ALU.mult, ALU.add))
                    n = parts[-1][1]
                    sig(gt(r[:, 0:n], r[:, 0:n], HALF[:, 0:n], ALU.pow), "pool_r", (l, i))

                def gains(i):
                    kind, t, half = tasks[i]
                    if kind == "cq":
                        return
                    lat = t < LTILES
                    tm = TM[i % 4]
                    if kind == "ckv":
                        after(pool, "dve_kr", (l, t))
                        x = KR[:, t, :]
                        ins = gt(x, x, GAIN[:, l, G_MK + NOPE:G_MK + HQ], ALU.mult)
                        if lat:
                            link(ins)
                            ins = rotate(halves(x.rearrange("p (g d) -> p g d", g=1), 1, 8), CST[:, C_COSM + 16 * t:C_COSM + 16 * (t + 1)],
                                         CST[:, C_SINM + 16 * t:C_SINM + 16 * (t + 1)], 1, 8)
                        sig(ins, "pool_kr", (l, t))
                        return
                    after(pool, "dve_sc", (l, i))
                    row = lambda at, n, g: GAIN[:, l, at:at + n].rearrange("p (o n) -> p o n", o=1).to_broadcast([P, g, n])
                    if kind == "ukv":
                        k = tm[:, 0:384].rearrange("p (h d) -> p h d", h=4)
                        link(gt(k[:, :, 0:NOPE], k[:, :, 0:NOPE], row(G_MK, NOPE, 4), ALU.mult))
                        after(pool, "pool_kr", (l, t))
                        ins = gc(k[:, :, NOPE:HQ], KR[:, t, :].rearrange("p (o n) -> p o n", o=1).to_broadcast([P, 4, ROPE]))
                    elif kind == "uq":
                        q = tm[:, 0:384].rearrange("p (h d) -> p h d", h=4)
                        ins = gt(q, q, row(G_MQ, HQ, 4), ALU.mult)
                        if lat:
                            link(ins)
                            ins = rotate(halves(q[:, :, NOPE:HQ], 4, 8), CST[:, C_COSM + 16 * t:C_COSM + 16 * (t + 1)],
                                         CST[:, C_SINM + 16 * t:C_SINM + 16 * (t + 1)], 4, 8)
                    else:
                        x = tm.rearrange("p (h d) -> p h d", h=4)
                        ins = gt(x, x, row(G_DK if kind == "kd" else G_DQ, 2 * DD, 4), ALU.mult)
                        if lat:
                            link(ins)
                            ins = rotate(halves(tm.rearrange("p (h d) -> p h d", h=8), 8, 16), CST[:, C_COSD + 32 * t:C_COSD + 32 * (t + 1)],
                                         CST[:, C_SIND + 32 * t:C_SIND + 32 * (t + 1)], 8, 16)
                    sig(ins, "pool_tm", (l, i))

                roots(0)
                for i in range(len(tasks)):
                    if i + 1 < len(tasks) and i + 1 != len(early):
                        roots(i + 1)
                    gains(i)
                    if i + 1 == len(early):
                        roots(i + 1)

            def attention(l):
                for t in range(nq_of(l)):
                    after(pool, "dve_sso", (l, t))
                    link(gs_(RO[:, :], SSO[:, :], 1.0 / DV, EPS, ALU.mult, ALU.add))
                    sig(gt(RO[:, :], RO[:, :], HALF[:, 0:DH], ALU.pow), "pool_ro", (l, t))

            def merge(l):
                n = nq_of(l) * P
                for b in range(KD):
                    after(pool, "dve_mg", (l, b, 1))
                    sig(gt(YT[:, b, 0:n], MY[b % 2][0][:, 0:n], MY[b % 2][1][:, 0:n], ALU.add), "pool_y", (l, b))

            def scatter(l):
                after(pool, "dve_slot", l)
                for t in range(nq_of(l)):
                    after(pool, "act_htok", (l, t))
                    after(pool, "dve_htok", (l, t))
                    for k in range(2):
                        pool.indirect_dma_start(Hs[0:SORTED, :], bass.IndirectOffsetOnAxis(ap=SLOT[:, t, k:k + 1], axis=0),
                                                HTOK[t], None).then_inc(sem(f"sorted_stored{l}"), 16)

            def gather(l):
                pool.wait_ge(sem(f"experts_over{l}"), 1)
                for t in range(nq_of(l)):
                    if t >= 2:
                        after(pool, "dve_x", (l, 1, t - 2))
                    for k in range(2):
                        pool.indirect_dma_start(YG[t % 2][k], None, Ys[0:SORTED, :],
                                                bass.IndirectOffsetOnAxis(ap=SLOT[:, t, k:k + 1], axis=0)).then_inc(sem(f"y_gathered{l}{t % 2}{k}"), 16)

            start()
            for l in range(DEPTH):
                norm(l, 0)
                prep(l)
                attention(l)
                merge(l)
                norm(l, 1)
                scatter(l)
                gather(l)


_INS = ["x", "c", "ctx", "c_ctx", "ada_w", "ada_b", "attn_norm_g", "ffn_norm_g", "w_in", "mla_q_norm_g", "mla_w_uq",
        "mla_kv_norm_g", "mla_w_ukv", "mla_q_g", "mla_k_g", "diff_q_g", "diff_k_g", "diff_lam", "diff_sub_g", "w_o_mla",
        "w_o_diff", "w_out", "router_w", "router_b", "moe_w_gate", "moe_w_up", "moe_w_down", "sh_w_gate", "sh_w_up", "sh_w_down"]


def kernel(**inputs):
    import numpy as _np
    import concourse.bacc as _bacc
    from concourse import mybir as _mybir
    from concourse.bass_utils import run_bass_kernel_spmd as _run

    def program(book):
        nc = _bacc.Bacc("TRN2", target_bir_lowering=False, num_devices=1)
        args = {}
        for name, a in arrays.items():
            args[name[3:]] = nc.dram_tensor(name, a.shape, _mybir.dt.from_np(a.dtype), kind="ExternalInput").ap()
        args["out"] = nc.dram_tensor("out_0", (1, SEQ, D), _mybir.dt.float32, kind="ExternalOutput").ap()
        build(nc, args, book)
        return nc

    arrays = {f"in_{name}": _np.ascontiguousarray(inputs[name]) for name in _INS}
    arrays["in_consts"] = constants()
    book = {}
    program(book)
    r = _run(program(book), [arrays], core_ids=[0])
    return r.results[0]["out_0"]
```

```python
import concourse.bass as bass
from concourse import mybir
from contextlib import ExitStack
import math
import numpy as np

F32 = mybir.dt.float32
I32 = mybir.dt.int32
U32 = mybir.dt.uint32
ALU = mybir.AluOpType
ACT = mybir.ActivationFunctionType
AX = mybir.AxisListType

P = 128
D = 1024
KD = D // P
SEQ = 256
CTX = 256
NTOK = SEQ + CTX
TILES = NTOK // P
LTILES = SEQ // P
DEPTH = 2
EPS = 1e-6
GRID_W = 64
ROPE_BASE = 10000.0
MH, NOPE, ROPE, MV = 8, 64, 32, 64
HQ = NOPE + ROPE
QR, KVR = 512, 256
DH, DD, DV = 4, 64, 128
MLA_SCALE = 1.0 / math.sqrt(HQ)
DIFF_SCALE = 1.0 / math.sqrt(DD)
OFF_KD = KVR + ROPE
OFF_VD = OFF_KD + 2 * DH * DD
OFF_CQ = OFF_VD + DH * DV
OFF_QD = OFF_CQ + QR
OFF_GATE = OFF_QD + 2 * DH * DD
NE, EPG, NG = 16, 4, 4
FE = 512
KF = FE // P
CAND = NE * TILES
SORTED = 2 * NTOK
TURNS = (NE + (SORTED - NE) // P + 1) // 2
CHUNK = 4096
WSLOTS = 4
BIG = 1.0e30

C_ID, C_TRI, C_ONE = 0, 128, 256
C_IOTA, C_TIE, C_ECAND, C_RCAND, C_JOB = 384, 400, 404, 468, 532
C_COSM, C_SINM, C_COSD, C_SIND = 533, 565, 597, 661
C_END = 725


def constants():
    c = np.zeros((P, C_END), np.float32)
    c[:, C_ID:C_ID + P] = np.eye(P)
    c[:, C_TRI:C_TRI + P] = np.triu(np.ones((P, P)), 1)
    c[:, C_ONE:C_ONE + P] = 1.0
    c[:, C_IOTA:C_IOTA + NE] = np.arange(NE)
    c[:, C_TIE:C_TIE + NG] = NG - np.arange(NG)
    c[:, C_ECAND:C_ECAND + CAND] = np.arange(CAND) // TILES
    c[:, C_RCAND:C_RCAND + CAND] = P * (np.arange(CAND) % TILES)
    c[:, C_JOB] = np.arange(P) + 1
    pos = np.arange(SEQ)
    for width, cos_at, sin_at in ((ROPE, C_COSM, C_SINM), (DD, C_COSD, C_SIND)):
        axis = width // 2
        inv = (np.float32(ROPE_BASE) ** (-np.arange(0, axis, 2, dtype=np.float32) / np.float32(axis))).astype(np.float32)
        row = (pos // GRID_W).astype(np.float32)[:, None] * inv
        col = (pos % GRID_W).astype(np.float32)[:, None] * inv
        ang = np.concatenate([row, col], axis=1)
        for at, table in ((cos_at, np.cos(ang)), (sin_at, np.sin(ang))):
            for t in range(LTILES):
                c[:, at + t * axis:at + (t + 1) * axis] = table[t * P:(t + 1) * P]
    return c


V_ADAB, V_AG, V_FG, V_QG, V_KVG, V_SUB, V_END = 0, 48, 56, 64, 68, 70, 71
G_MQ, G_MK, G_DQ, G_DK, G_END = 0, 96, 192, 320, 448


def layer_chunks(l):
    if l == 0:
        order = [(0, f"ada{n}", n) for n in range(4)]
        order += [(0, "ckv", 0), (0, "ada4", 1), (0, "ada5", 2), (0, "cq", 3), (0, "ada6", 0), (0, "kd", 1), (0, "ada7", 2),
                  (0, "ada8", 3), (0, "qd", 0), (0, "ada9", 1), (0, "vd", 2), (0, "ada10", 3), (0, "ukv", 0), (0, "uq", 1),
                  (0, "om", 2), (0, "od", 3), (0, "g0", 0), (0, "g2", 1), (0, "ada11", 4)]
        order += [(1, f"ada{n}", 5 - n % 2) for n in range(4)]
        order += [(0, "g1", 0), (0, "g3", 1)]
        order += [(1, f"ada{n}", 5 - n % 2) for n in range(4, 12)]
        order += [(0, "out0", 5), (0, "out1", 2), (0, "shg", 3), (0, "shu", 0), (0, "shd", 1)]
        return order
    return [(l, name, s) for name, s in (
        ("ckv", 0), ("cq", 1), ("kd", 2), ("qd", 3), ("vd", 0), ("ukv", 1), ("uq", 2), ("om", 3), ("od", 0), ("g0", 1), ("g2", 2),
        ("g1", 1), ("g3", 2), ("out0", 4), ("out1", 3), ("shg", 0), ("shu", 1), ("shd", 2))]


def mod_streams(l, n):
    return 2 if l < DEPTH - 1 or n < 4 else 1


ADA_PLAN = {"prep": ([(0, n) for n in range(4, 10)], 16, 6),
            "vd": ([(0, 10)], 1, 16),
            "merge": ([(0, 11)] + [(1, n) for n in range(12)], 16, 9)}


def ada_share(phase, step):
    chunks, steps, per = ADA_PLAN[phase]
    ops = [(l, n, k, s) for l, n in chunks for k in range(KD) for s in range(mod_streams(l, n))]
    assert len(ops) <= steps * per
    mine = ops[step * per:(step + 1) * per]
    return mine, [(l, n) for l, n, k, s in mine if k == KD - 1 and s == mod_streams(l, n) - 1]


def norm_tasks(l):
    nq = TILES if l < DEPTH - 1 else LTILES
    tasks = [("ckv", t, 0) for t in range(TILES)]
    tasks += [("cq", t, 0) for t in range(nq)]
    tasks += [("kd", t, 0) for t in range(TILES)]
    tasks += [("qd", t, 0) for t in range(nq)]
    late = [("ukv", t, h) for t in range(TILES) for h in range(2)]
    late += [("uq", t, h) for t in range(nq) for h in range(2)]
    return tasks, late


def attention_units(l):
    nq = TILES if l < DEPTH - 1 else LTILES
    return [u for t in range(nq) for u in [("m", t, h) for h in range(MH)] + [("d", t, h) for h in range(DH)]]


T_LAG = 3
A_TLAG = 2
A_VLAG = 3
NP = 5


def keys_of(t):
    return (0, TILES) if t < LTILES else (LTILES, TILES - LTILES)


def build(nc, A, book):
    ctx = ExitStack()
    with ctx:
        def sb(name, shape, dt=F32):
            return ctx.enter_context(nc.sbuf_tensor(name, shape, dt))

        sems = {}

        def sem(name):
            if name not in sems:
                sems[name] = ctx.enter_context(nc.semaphore(name))
            return sems[name]

        counts, seen = {}, {}

        def sig(ins, name, key, n=1):
            counts[name] = counts.get(name, 0) + n
            book[name, key] = counts[name]
            ins.then_inc(sem(name), n)

        def after(eng, name, key):
            count = book.get((name, key), 1)
            if seen.get((id(eng), name), 0) < count:
                seen[id(eng), name] = count
                eng.wait_ge(sem(name), count)

        def chained(eng, name, ins):
            sig(ins, name, counts.get(name, 0))
            after(eng, name, counts[name] - 1)

        X = sb("X", [P, TILES, D])
        HT = sb("HT", [P, KD, NTOK])
        QT = sb("QT", [P, MH, NTOK])
        KTM = sb("KTM", [P, MH, NTOK])
        QTD = sb("QTD", [P, DH, NTOK])
        KTD = sb("KTD", [P, DH, NTOK])
        VS = sb("VS", [P, 2, TILES, 512])
        OT = sb("OT", [P, 2, 4, NTOK])
        W = sb("W", [P, WSLOTS, CHUNK])
        STG = sb("STG", [P, 4096])
        CST = sb("CST", [P, C_END])
        GAIN = sb("GAIN", [P, DEPTH, G_END])
        VEC = sb("VEC", [P, DEPTH, V_END])
        CS = sb("CS", [P, 2 * KD])
        CT = sb("CT", [P, 2, 2 * KD])
        MODS = sb("MODS", [P, DEPTH, 48, 2])
        SCLS = sb("SCLS", [P, DEPTH, 2, KD, 2])
        NLAM = sb("NLAM", [P, DEPTH])
        LT = sb("LT", [P, 8])
        SUBG = sb("SUBG", [P, 1])
        RW = sb("RW", [P, KD, NE])
        RB = sb("RB", [P, NE])
        SSX = sb("SSX", [P, TILES])
        RX = sb("RX", [P, TILES])
        HALF = sb("HALF", [P, 16])
        SS = sb("SS", [P, 4, 16])
        RR = sb("RR", [P, 4, 16])
        KR = sb("KR", [P, TILES, ROPE])
        RT = sb("RT", [P, 4, 256])
        MX = sb("MX", [P, 8])
        MB = sb("MB", [P, 8])
        RSUM = sb("RSUM", [P, 8])
        RINV = sb("RINV", [P, 2, 8])
        RDIF = sb("RDIF", [P, 8])
        SSO = sb("SSO", [P, 4])
        RO = sb("RO", [P, 4])
        TAB = sb("TAB", [1, 72], I32)
        SLOT = sb("SLOT", [P, TILES, 2], U32)
        WTS = sb("WTS", [P, TILES, 2])

        SQ = [STG[:, 512 * i:512 * (i + 1)] for i in range(2)]
        TM = [STG[:, 1024 + 512 * i:1024 + 512 * (i + 1)] for i in range(4)]
        PB = [STG[:, 512 * i:512 * (i + 1)] for i in range(NP)]
        PTS = [STG[:, 2560 + 512 * i:2560 + 512 * (i + 1)] for i in range(2)]
        OTM = STG[:, 3584:4096]
        OWN = OT[:, :, :, :].rearrange("p a k n -> p (a k n)")
        CQT = OWN[:, 0:2048].rearrange("p (k n) -> p k n", k=4)
        CKT = OWN[:, 2048:3072].rearrange("p (k n) -> p k n", k=2)
        XN = QT[:, :, :].rearrange("p a n -> p (a n)").rearrange("p (t d) -> p t d", t=TILES)
        YT = QT
        GATE = QTD[:, :, :].rearrange("p a n -> p (a n)").rearrange("p (s d) -> p s d", s=2)
        HET = KTD
        YS = VS[:, :, :, :].rearrange("p a t n -> p (a t n)").rearrange("p (t d) -> p t d", t=TILES)
        ESLOT = [W[:, i, :] for i in range(WSLOTS)] + [
            QT[:, :, :].rearrange("p a n -> p (a n)"), KTM[:, :, :].rearrange("p a n -> p (a n)")]
        HE = [OWN[:, 1024 * i:1024 * (i + 1)] for i in range(2)]
        HEX = [OWN[:, 2048 + 1024 * i:2048 + 1024 * (i + 1)].rearrange("p (k n) -> p k n", k=KD) for i in range(2)]
        HID = [STG[:, 512 * i:512 * (i + 1)] for i in range(2)]
        THB = [STG[:, 1024 + 512 * i:1024 + 512 * (i + 1)] for i in range(2)]
        YB = [STG[:, 2048 + 1024 * i:2048 + 1024 * (i + 1)] for i in range(2)]
        HTOK = [OWN[:, 1024 * i:1024 * (i + 1)] for i in range(TILES)]
        KFLAT = KTM[:, :, :].rearrange("p a n -> p (a n)")
        YG = [[(OWN if i < 2 else KFLAT)[:, 1024 * (2 * (i % 2) + k):1024 * (2 * (i % 2) + k + 1)] for k in range(2)]
              for i in range(TILES)]
        HTX = [KTD[:, i, :].rearrange("p (k n) -> p k n", k=KF) for i in range(2)]
        DIAG = STG[:, 0:1024].rearrange("p (h n) -> p h n", h=2)
        MT = [[STG[:, 1024 * b + 512 * j:1024 * b + 512 * (j + 1)] for j in range(2)] for b in range(2)]
        MY = [[STG[:, 2048 + 1024 * b + 512 * j:2048 + 1024 * b + 512 * (j + 1)] for j in range(2)] for b in range(2)]
        STH = [STG[:, 2048 + 512 * i:2048 + 512 * (i + 1)] for i in range(2)]
        SVV = [STG[:, 3072 + 512 * i:3072 + 512 * (i + 1)] for i in range(2)]
        RTF = RT[:, :, :].rearrange("p a n -> p (a n)")
        ACC = [[STG[:, 3072 + 512 * i:3584 + 512 * i] for i in range(2)], [RTF[:, 512 * i:512 * (i + 1)] for i in range(2)]]
        AROW = [STG[0:2, 512 * i:512 * (i + 1)] for i in range(4)]
        ZERO = HT[:, 4:6, :].rearrange("p a n -> p (a n)")
        at = [0]

        def route(*shape, dt=None):
            n = int(np.prod(shape))
            v = STG[:, at[0]:at[0] + n]
            at[0] += n
            v = v.bitcast(dt) if dt is not None else v
            if len(shape) == 2:
                v = v.rearrange("p (a b) -> p a b", a=shape[0])
            return v

        AFF, SEL, TMPR = (route(TILES * NE) for _ in range(3))
        PAIR = route(TILES * NG * 6)
        GRP = route(3, TILES * NG)
        BEST = route(TILES, 8)
        BIDX = route(TILES, 8, dt=U32)
        FIDX = route(TILES, 2)
        HOT = [route(TILES, NE) for _ in range(2)]
        MSK = route(TILES, NE)
        CNT = route(3, NE)
        SLF = route(TILES, 2)
        CND = route(4, CAND)
        JOBC = route(4)
        TABI = route(1, dt=I32)[0:1, :]
        CONES = CST[:, C_ONE:C_ONE + CAND]
        assert at[0] <= 2048

        def MASK(t):
            return MSK[:, t, :]

        def tm_sem(kind):
            return "dve_tm" if kind in ("ckv", "cq") else "pool_tm"

        def first_hidden(eng):
            eng.wait_ge(sem("pad_stored"), 16)
            after(eng, "dve_vec", DEPTH - 1)
            after(eng, "dve_lam", 0)

        ROW_LOADS = 6 * DEPTH
        LAMR = HT[:, 0:2, 0:256]
        VROW = HT[:, 2:4, 0:P]
        CROW = HT[0:2 * KD, 6, 0:P]

        PS = [ctx.enter_context(nc.psum_tensor(f"PS{i}", [P, 512], F32)) for i in range(8)]
        Hs = nc.dram_tensor("sorted_h", [SORTED + P, D], F32, kind="Internal").ap()
        Ys = nc.dram_tensor("sorted_y", [SORTED + P, D], F32, kind="Internal").ap()

        SLOTS = [W[:, i, :] for i in range(WSLOTS)] + [
            KTM[:, :, :].rearrange("p a n -> p (a n)"), VS[:, :, :, :].rearrange("p a t n -> p (a t n)")]
        ident = CST[:, C_ID:C_ID + P]
        ones = CST[:, C_ONE:C_ONE + P]

        bank_of, turn, holder = {}, [0, 0], {}

        def bank_open(pe, key, acc=False):
            b = 6 + turn[1] % 2 if acc else turn[0] % 6
            turn[acc] += 1
            if b in holder:
                after(pe, *book.get(("read", holder[b]), ("none", 0)))
            holder[b] = key
            book["bank", key] = b
            return PS[b]

        def bank_read(eng, key):
            after(eng, "pe_" + key[0], key)
            return PS[book.get(("bank", key), 0)]

        def last_read(key, name, event):
            book["read", key] = (name, event)

        def product(last, key):
            sig(last, "pe_" + key[0], key)

        ring, before, in_slot = {}, {}, {}
        for l in range(DEPTH):
            for cl, name, s in layer_chunks(l):
                was_in, old = in_slot.get(s, (None, None))
                before[cl, name] = (l, old if was_in == l else None)
                n = 1 + (ring[old][1] if old else 0)
                ring[cl, name] = (s, n)
                in_slot[s] = (l, (cl, name))

        def chunk(eng, l, name):
            s, n = ring[l, name]
            if seen.get((id(eng), s), 0) < n:
                seen[id(eng), s] = n
                eng.wait_ge(sem(f"w_loaded{s}"), 16 * n)
            return SLOTS[s]

        def chunk_free(eng, l, name):
            after(eng, *book.get(("chunk_done", (l, name)), ("none", 0)))

        def ada_buffer(l, n, s):
            i = s if mod_streams(l, n) == 2 else n % 2
            return ACC[(l, n) >= (0, 11)][i]

        def chunk_done(l, name, product_key):
            book["chunk_done", (l, name)] = ("pe_" + product_key[0], product_key)

        def nq_of(l):
            return TILES if l < DEPTH - 1 else LTILES

        def streams(n):
            return [(0, 0, SEQ)] + ([(1, SEQ, CTX)] if n > SEQ else [])

        block = ctx.enter_context(nc.Block())

        @block.tensor
        def _(pe):
            mm, tp = nc.tensor.matmul, nc.tensor.transpose

            def small_vectors():
                pe.wait_ge(sem("const_loaded"), 16)
                pe.wait_ge(sem("c_loaded"), 32)
                product(tp(bank_open(pe, ("small", 0))[:, 0:2 * KD], CROW, ident[0:2 * KD, 0:2 * KD]), ("small", 0))
                pe.wait_ge(sem("rows_loaded"), 16 * ROW_LOADS)
                ps = bank_open(pe, ("small", 1))
                for l in range(DEPTH):
                    last = tp(ps[:, P * l:P * l + V_END], VROW[0:V_END, l, :], ident[0:V_END, 0:V_END])
                product(last, ("small", 1))

            def ada_first():
                for n in range(5):
                    if n < 4:
                        key = ("adar", 0, n)
                        ps = bank_open(pe, key)
                        w = chunk(pe, 0, f"ada{n}").rearrange("p (k n) -> p k n", k=KD)
                        after(pe, "dve_c", 0)
                        for k in range(KD):
                            last = mm(ps[0:2, :], CS[:, k::KD], w[:, k, :], start=(k == 0), stop=(k == KD - 1))
                        product(last, key)
                        chunk_done(0, f"ada{n}", key)
                    if n:
                        after(pe, "act_adar", n - 1)
                        key = ("ada", 0, n - 1)
                        ps = bank_open(pe, key)
                        for c in range(4):
                            last = tp(ps[:, 2 * c:2 * c + 2], AROW[n - 1][:, c * P:(c + 1) * P], ident[0:2, 0:2])
                        product(last, key)

            def ada_columns(phase, step):
                for l, n in ada_share(phase, step)[1]:
                    for s in range(mod_streams(l, n)):
                        after(pe, "dve_acc", (l, n, KD - 1, s))
                    key = ("ada", l, n)
                    ps = bank_open(pe, key)
                    for c in range(4):
                        for s in range(mod_streams(l, n)):
                            last = mm(ps[:, 2 * c + s:2 * c + s + 1], ada_buffer(l, n, s)[:, c * P:(c + 1) * P],
                                      ones[:, 0:1], start=True, stop=True)
                    product(last, key)

            def gate_rows(l, which):
                for s in range(2 if l < DEPTH - 1 else 1):
                    for h in range(2):
                        after(pe, "dve_diag", (l, which, s, h))
                        key = ("gate", l, which, s, h)
                        ps = bank_open(pe, key)
                        product(mm(ps[:, :], ones, DIAG[:, h, :], start=True, stop=True), key)

            def hidden_t(l, f):
                nt = TILES if f == 0 else nq_of(l)
                after(pe, "dve_xn", (l, f, nt - 1))
                for k in range(KD):
                    ps = bank_open(pe, ("hT", l, f, k))
                    for t in range(nt):
                        last = tp(ps[:, t * P:(t + 1) * P], XN[:, t, k * P:(k + 1) * P], ident)
                    product(last, ("hT", l, f, k))

            def project(l, kind, t, half):
                key = ("proj", l, kind, t, half)
                w = chunk(pe, l, kind)
                if kind == "ukv":
                    w = w[:, 0:2 * D].rearrange("p (k n) -> p k n", k=2)
                    src, n0, n, kk = CKT, 512 * half, 512, 2
                elif kind == "uq":
                    w = w[:, 0:4 * MH * HQ].rearrange("p (k n) -> p k n", k=4)
                    src, n0, n, kk = CQT, 384 * half, 384, 4
                elif kind == "ckv":
                    w = w[:, 0:KD * OFF_KD].rearrange("p (k n) -> p k n", k=KD)
                    src, n0, n, kk = HT, 0, OFF_KD, KD
                else:
                    w = w.rearrange("p (k n) -> p k n", k=KD)
                    src, n0, n, kk = HT, 0, 512, KD
                ps = bank_open(pe, key)
                for k in range(kk):
                    last = mm(ps[:, 0:n], src[:, k, t * P:(t + 1) * P], w[:, k, n0:n0 + n],
                              start=(k == 0), stop=(k == kk - 1))
                product(last, key)
                chunk_done(l, kind, key)

            def task_t(l, i, task):
                kind, t, half = task
                after(pe, tm_sem(kind), (l, i))
                ps = bank_open(pe, ("T", l, i))
                src = TM[i % 4]
                if kind in ("ukv", "uq"):
                    for h in range(4):
                        last = tp(ps[0:HQ, h * P:(h + 1) * P], src[:, h * HQ:(h + 1) * HQ], ident)
                else:
                    for b in range(2 if kind == "ckv" else 4):
                        last = tp(ps[:, b * P:(b + 1) * P], src[:, b * P:(b + 1) * P], ident)
                product(last, ("T", l, i))

            def prep(l):
                early, late = norm_tasks(l)
                tasks = early + late
                after(pe, "dve_hT", (l, 0, KD - 2))
                after(pe, "act_hT", (l, 0, KD - 1))
                done = 0
                for i, (kind, t, half) in enumerate(tasks):
                    if i == len(early):
                        for tt in range(TILES):
                            project(l, "vd", tt, 0)
                            if l == 0 and tt < 2:
                                ada_columns("prep", len(early) - 2 + tt)
                        if l == 0:
                            ada_columns("vd", 0)
                        while done < i:
                            task_t(l, done, tasks[done])
                            done += 1
                        after(pe, "act_T", (l, TILES + nq_of(l) - 1))
                    project(l, kind, t, half)
                    if l == 0 and 2 <= i < len(early):
                        ada_columns("prep", i - 2)
                    if i - T_LAG >= done:
                        task_t(l, done, tasks[done])
                        done += 1
                while done < len(tasks):
                    task_t(l, done, tasks[done])
                    done += 1

            def attention(l):
                units = attention_units(l)
                ntask = sum(map(len, norm_tasks(l)))
                after(pe, "act_T", (l, ntask - 1))
                after(pe, "act_vd", (l, TILES - 1))
                after(pe, "act_vm", (l, TILES - 1, 1))
                maps = 0

                def scores(u, kind, t, h):
                    k0, kn = keys_of(t)
                    for m in range(1 if kind == "m" else 2):
                        key = ("S", l, u, m)
                        ps = bank_open(pe, key)
                        if kind == "m":
                            last = mm(ps[:, 0:kn * P], QT[0:HQ, h, t * P:(t + 1) * P],
                                      KTM[0:HQ, h, k0 * P:(k0 + kn) * P], start=True, stop=True)
                        else:
                            last = mm(ps[:, 0:kn * P], QTD[64 * m:64 * m + 64, h, t * P:(t + 1) * P],
                                      KTD[64 * m:64 * m + 64, h, k0 * P:(k0 + kn) * P], start=True, stop=True)
                        product(last, key)

                def prob_t(u, kind, t, h):
                    k0, kn = keys_of(t)
                    after(pe, "act_p" if kind == "m" else "dve_a", (l, u))
                    key = ("PT", l, u)
                    ps = bank_open(pe, key)
                    src = PB[book.get(("pbuf", (l, u)), 0)]
                    for c in range(kn):
                        last = tp(ps[:, c * P:(c + 1) * P], src[:, c * P:(c + 1) * P], ident)
                    product(last, key)

                def values(u, kind, t, h):
                    k0, kn = keys_of(t)
                    key = ("O", l, kind, t)
                    if h == 0:
                        bank_open(pe, key, acc=True)
                    ps = PS[book["bank", key]]
                    after(pe, "act_pts" if u % 2 == 0 else "dve_pts", (l, u))
                    w = MV if kind == "m" else DV
                    for c in range(kn):
                        last = mm(ps[:, h * w:(h + 1) * w], PTS[u % 2][:, c * P:(c + 1) * P],
                                  VS[:, int(kind == "d"), k0 + c, h * w:(h + 1) * w], start=(c == 0), stop=(c == kn - 1))
                    done = h == (MH if kind == "m" else DH) - 1
                    product(last, key if done else ("O", l, u))
                    book["pv_done", (l, u)] = key if done else ("O", l, u)

                def out_t(kind, t):
                    after(pe, "dve_o" , (l, kind, t))
                    key = ("OT", l, kind, t)
                    ps = bank_open(pe, key)
                    for b in range(4):
                        last = tp(ps[:, b * P:(b + 1) * P], OTM[:, b * P:(b + 1) * P], ident)
                    product(last, key)

                waiting = []
                for i in range(len(units) + A_VLAG + 2):
                    if i < len(units):
                        scores(i, *units[i])
                    if 0 <= i - A_TLAG < len(units):
                        prob_t(i - A_TLAG, *units[i - A_TLAG])
                    if 0 <= i - A_VLAG < len(units):
                        kind, t, h = units[i - A_VLAG]
                        values(i - A_VLAG, kind, t, h)
                        if h == (MH if kind == "m" else DH) - 1:
                            waiting.append((i + 2, kind, t))
                    while waiting and waiting[0][0] <= i:
                        out_t(*waiting.pop(0)[1:])

            def merge(l):
                nt = nq_of(l)
                n = nt * P
                after(pe, "act_oT", (l, "d", nt - 1))
                om = chunk(pe, l, "om").rearrange("p (k n) -> p k n", k=4)
                od = chunk(pe, l, "od").rearrange("p (k n) -> p k n", k=4)
                for b in range(KD):
                    c = (b % 4) * P
                    g = [chunk(pe, l, f"g{b // 4}"), chunk(pe, l, f"g{2 + b // 4}")]
                    for j, (kk, w, src, c0) in enumerate((
                            (KD, g[0].rearrange("p (k n) -> p k n", k=KD), HT, c),
                            (KD, g[1].rearrange("p (k n) -> p k n", k=KD), HT, c),
                            (4, om, OT[:, 0], b * P), (4, od, OT[:, 1], b * P))):
                        key = ("mg", l, b, j)
                        ps = bank_open(pe, key)
                        for k in range(kk):
                            last = mm(ps[:, 0:n], w[:, k, c0:c0 + P], src[:, k, 0:n], start=(k == 0), stop=(k == kk - 1))
                        product(last, key)
                        chunk_done(l, (f"g{b // 4}", f"g{2 + b // 4}", "om", "od")[j], key)
                        if l == 0 and b and j < 2:
                            ada_columns("merge", 2 * (b - 1) + j)

            def out_proj(l):
                if l == 0:
                    ada_columns("merge", 14)
                    ada_columns("merge", 15)
                after(pe, "pool_y", (l, KD - 1))
                for h in range(2):
                    w = chunk(pe, l, f"out{h}").rearrange("p (k n) -> p k n", k=KD)
                    for t in range(nq_of(l)):
                        key = ("out", l, h, t)
                        ps = bank_open(pe, key)
                        for k in range(KD):
                            last = mm(ps[:, :], YT[:, k, t * P:(t + 1) * P], w[:, k, :], start=(k == 0), stop=(k == KD - 1))
                        product(last, key)
                        chunk_done(l, f"out{h}", key)

            def router(l):
                after(pe, "dve_hT", (l, 1, KD - 2))
                after(pe, "act_hT", (l, 1, KD - 1))
                key = ("logit", l)
                pe.wait_ge(sem("router_loaded"), 32)
                ps = bank_open(pe, key)
                for t in range(nq_of(l)):
                    for k in range(KD):
                        last = mm(ps[:, NE * t:NE * (t + 1)], HT[:, k, t * P:(t + 1) * P], RW[:, k, :],
                                  start=(k == 0), stop=(k == KD - 1))
                product(last, key)
                for t in range(nq_of(l)):
                    for h in range(2):
                        key = ("htok", l, t, h)
                        ps = bank_open(pe, key)
                        for b in range(4):
                            last = tp(ps[:, b * P:(b + 1) * P], HT[:, 4 * h + b, t * P:(t + 1) * P], ident)
                        product(last, key)

            def places(l):
                nt = nq_of(l)
                after(pe, "dve_mask", l)
                key = ("place", l)
                ps = bank_open(pe, key)
                for t in range(nt):
                    for s in range(t + 1):
                        mm(ps[:, NE * t:NE * (t + 1)], CST[:, C_TRI:C_TRI + P] if s == t else ones,
                           MASK(s), start=(s == 0), stop=(s == t))
                for s in range(nt):
                    last = mm(ps[:, 64:64 + NE], ones, MASK(s), start=(s == 0), stop=(s == nt - 1))
                product(last, key)

            def job_rows(l):
                after(pe, "dve_jobcol", l)
                key = ("jobs", l)
                ps = bank_open(pe, key)
                for j in range(2):
                    last = mm(ps[0:1, j * P:(j + 1) * P], JOBC[:, j:j + 1], ident, start=True, stop=True)
                product(last, key)

            def shared(l):
                nt = nq_of(l)
                n = nt * P
                w = [chunk(pe, l, x).rearrange("p (k n) -> p k n", k=KD) for x in ("shg", "shu")]
                for f in range(KF):
                    for j in range(2):
                        key = ("sh", l, f, j)
                        ps = bank_open(pe, key)
                        for k in range(KD):
                            last = mm(ps[:, 0:n], w[j][:, k, f * P:(f + 1) * P], HT[:, k, 0:n], start=(k == 0), stop=(k == KD - 1))
                        product(last, key)
                        chunk_done(l, ("shg", "shu")[j], key)
                    if f == 0:
                        places(l)
                    if f == 2:
                        job_rows(l)
                w = chunk(pe, l, "shd").rearrange("p (k n) -> p k n", k=KF)
                after(pe, "dve_sh", (l, KF - 1))
                for t in range(nt):
                    for h in range(2):
                        key = ("shd", l, t, h)
                        ps = bank_open(pe, key)
                        for k in range(KF):
                            last = mm(ps[:, :], HET[:, k, t * P:(t + 1) * P], w[:, k, 512 * h:512 * (h + 1)],
                                      start=(k == 0), stop=(k == KF - 1))
                        product(last, key)
                        chunk_done(l, "shd", key)

            def experts(l):
                e = lambda name: sem(f"{name}{l}")
                for b in range(8):
                    after(pe, *book.get(("read", holder[b]), ("none", 0)))
                pe.wait_ge(e("tab_ready"), 1)
                turns = pe.value_load(TAB[0:1, 64:65], min_val=1, max_val=TURNS)

                pe.wait_ge(e("he_loaded0"), 16)
                for h in range(2):
                    for b in range(4):
                        last = tp(PS[h][:, b * P:(b + 1) * P], HE[0][:, (4 * h + b) * P:(4 * h + b + 1) * P], ident)
                    last.then_inc(e(f"e_in_done{h}"), 1)
                with pe.Fori(0, turns) as i:
                    for j in range(2):
                        wg, wu, wd = (ESLOT[3 * j + x] for x in range(3))
                        wg, wu = (x.rearrange("p (k n) -> p k n", k=KD) for x in (wg, wu))
                        wd = wd.rearrange("p (k n) -> p k n", k=KF)
                        pe.wait_ge(e("e_hex_dve"), 2 * i + j + 1)
                        pe.wait_ge(e("e_hex_act"), 2 * i + j + 1)
                        pe.wait_ge(e(f"ew_loaded{3 * j}_"), 16 * i + 16)
                        pe.wait_ge(e("e_hid_done"), 2 * i + j)
                        for k in range(KD):
                            last = mm(PS[2][:, :], HEX[j][:, k, :], wg[:, k, :], start=(k == 0), stop=(k == KD - 1))
                        last.then_inc(e("e_g_done"), 1)
                        pe.wait_ge(e(f"ew_loaded{3 * j + 1}_"), 16 * i + 16)
                        for k in range(KD):
                            last = mm(PS[3][:, :], HEX[j][:, k, :], wu[:, k, :], start=(k == 0), stop=(k == KD - 1))
                        last.then_inc(e("e_u_done"), 1)
                        pe.wait_ge(e(f"he_loaded{1 - j}"), 16 * i + 16 * (1 + j))
                        for h in range(2):
                            for b in range(4):
                                last = tp(PS[h][:, b * P:(b + 1) * P],
                                          HE[1 - j][:, (4 * h + b) * P:(4 * h + b + 1) * P], ident)
                            last.then_inc(e(f"e_in_done{h}"), 1)
                        pe.wait_ge(e("e_hid_done"), 2 * i + j + 1)
                        for b in range(KF):
                            last = tp(PS[4][:, b * P:(b + 1) * P], HID[j][:, b * P:(b + 1) * P], ident)
                        last.then_inc(e("e_ht_done"), 1)
                        pe.wait_ge(e(f"ew_loaded{3 * j + 2}_"), 16 * i + 16)
                        pe.wait_ge(e("e_htx"), 2 * i + j + 1)
                        pe.wait_ge(e("e_y_dve"), 2 * i + j)
                        pe.wait_ge(e("e_y_act"), 2 * i + j)
                        for h in range(2):
                            for k in range(KF):
                                last = mm(PS[5 + h][:, :], HTX[j][:, k, :], wd[:, k, 512 * h:512 * (h + 1)],
                                          start=(k == 0), stop=(k == KF - 1))
                            last.then_inc(e(f"e_d_done{h}"), 1)
                pe.wait_ge(e("e_y_dve"), 2 * turns)
                pe.wait_ge(e("e_y_act"), 2 * turns)
                pe.wait_ge(e("e_hex_dve"), 2 * turns + 1)
                pe.wait_ge(e("e_hex_act"), 2 * turns + 1)
                holder.clear()

            small_vectors()
            ada_first()
            for l in range(DEPTH):
                hidden_t(l, 0)
                prep(l)
                attention(l)
                gate_rows(l, 0)
                merge(l)
                out_proj(l)
                hidden_t(l, 1)
                router(l)
                shared(l)
                gate_rows(l, 1)
                experts(l)

        @block.sync
        def _(sp):
            def small_loads():
                sp.dma_start(CROW[0:KD, :], A["c"].rearrange("o (k p) -> (o k) p", p=P)).then_inc(sem("c_loaded"), 16)
                sp.dma_start(CROW[KD:2 * KD, :], A["c_ctx"].rearrange("(k p) -> k p", p=P)).then_inc(sem("c_loaded"), 16)
                sp.dma_start(CST[:, :], A["consts"]).then_inc(sem("const_loaded"), 16)

            def vector_loads():
                for l in range(DEPTH):
                    for name, at, end in (("ada_b", V_ADAB, V_AG), ("attn_norm_g", V_AG, V_FG), ("ffn_norm_g", V_FG, V_QG),
                                          ("mla_q_norm_g", V_QG, V_KVG), ("mla_kv_norm_g", V_KVG, V_SUB), ("diff_sub_g", V_SUB, V_END)):
                        sp.dma_start(VROW[at:end, l, :], A[name][l, :].rearrange("(k p) -> k p", p=P)).then_inc(sem("rows_loaded"), 16)
                for t in range(TILES):
                    src = A["x"][0, t * P:(t + 1) * P, :] if t < LTILES else A["ctx"][0, (t - LTILES) * P:(t - LTILES + 1) * P, :]
                    sp.dma_start(X[:, t, :], src).then_inc(sem(f"x_loaded{t}"), 16)

            def source(l, name):
                w_in = A["w_in"][l].rearrange("(k p) n -> p k n", p=P)
                if name.startswith("ada"):
                    n = int(name[3:])
                    return A["ada_w"][l].rearrange("(k p) n -> p k n", p=P)[:, :, 512 * n:512 * (n + 1)], KD
                cols = {"ckv": (0, OFF_KD), "kd": (OFF_KD, OFF_VD), "vd": (OFF_VD, OFF_CQ), "cq": (OFF_CQ, OFF_QD), "qd": (OFF_QD, OFF_GATE)}
                if name in cols:
                    return w_in[:, :, cols[name][0]:cols[name][1]], KD
                if name[0] == "g":
                    c = OFF_GATE + 512 * int(name[1])
                    return w_in[:, :, c:c + 512], KD
                if name[:3] == "out":
                    c = 512 * int(name[3])
                    return A["w_out"][l].rearrange("(k p) n -> p k n", p=P)[:, :, c:c + 512], KD
                tensor, k = {"ukv": ("mla_w_ukv", 2), "uq": ("mla_w_uq", 4), "om": ("w_o_mla", 4), "od": ("w_o_diff", 4),
                             "shg": ("sh_w_gate", KD), "shu": ("sh_w_up", KD), "shd": ("sh_w_down", KF)}[name]
                return A[tensor][l].rearrange("(k p) n -> p k n", p=P), k

            def load(l, name):
                s, n = ring[l, name]
                now, old = before[l, name]
                if now and name == "cq":
                    for t in range(TILES):
                        sp.wait_ge(sem(f"y_gathered{t}"), 32)
                if old is not None:
                    chunk_free(sp, *old)
                elif s >= WSLOTS:
                    after(sp, "pe_O", ("O", now, "d", nq_of(now) - 1))
                src, k = source(l, name)
                width = src.shape[2]
                dst = SLOTS[s][:, 0:k * width].rearrange("p (k n) -> p k n", k=k)
                sp.dma_start(dst, src).then_inc(sem(f"w_loaded{s}"), 16)

            expert_w = [A["moe_w_gate"].rearrange("l e (k p) n -> (l e) p k n", p=P),
                        A["moe_w_up"].rearrange("l e (k p) n -> (l e) p k n", p=P),
                        A["moe_w_down"].rearrange("l e (k p) n -> (l e) p k n", p=P)]

            def experts(l):
                e = lambda name: sem(f"{name}{l}")
                nq = nq_of(l)
                sp.wait_ge(e("tab_ready"), 1)
                before_last = sp.value_load(TAB[0:1, 65:66], min_val=1, max_val=TURNS - 1)
                sp.wait_ge(e("sorted_stored"), 2 * 16 * nq)
                if l == 0:
                    sp.wait_ge(sem("pad_stored"), 16)

                def rows(j, n):
                    r = sp.value_load(TAB[0:1, 32 + n:33 + n] if isinstance(n, int) else TAB[0:1, bass.ds(n + 32, 1)], min_val=0, max_val=SORTED)
                    return r

                def weights(j, n):
                    ex = sp.value_load(TAB[0:1, n:n + 1] if isinstance(n, int) else TAB[0:1, bass.ds(n, 1)], min_val=0, max_val=NE - 1)
                    return ex + NE * l

                def load_w(ex, j, x):
                    k = KF if x == 2 else KD
                    sp.dma_start(ESLOT[3 * j + x].rearrange("p (k n) -> p k n", k=k),
                                 expert_w[x][bass.ds(ex, 1)].rearrange("o p k n -> p (o k) n")).then_inc(e(f"ew_loaded{3 * j + x}_"), 16)

                for s in range(WSLOTS + 1):
                    chunk_free(sp, *last_in_slot[l, s])
                after(sp, "pe_hT", ("hT", l, 1, KD - 1))
                for j in range(2):
                    sp.nop().then_inc(e(f"y_stored{j}_"), 16)
                r0 = rows(0, 0)
                sp.dma_start(HE[0], Hs[bass.ds(r0, P), :]).then_inc(e("he_loaded0"), 16)
                for j in range(2):
                    ex = weights(j, j)
                    for x in range(3):
                        load_w(ex, j, x)
                r1 = rows(1, 1)
                sp.dma_start(HE[1], Hs[bass.ds(r1, P), :]).then_inc(e("he_loaded1"), 16)
                def turn_of(i, more):
                    for j in range(2):
                        here = sp.snap(rows(j, 2 * i + j))
                        if more:
                            ex = sp.snap(weights(j, 2 * i + (2 + j)))
                        if more or j == 0:
                            r = sp.snap(rows(j, 2 * i + (2 + j)))
                        if more or j == 0:
                            sp.wait_ge(e("e_in_done1"), 2 * i + j + 1)
                            sp.dma_start(HE[j], Hs[bass.ds(r, P), :]).then_inc(e(f"he_loaded{j}"), 16)
                        if more:
                            sp.wait_ge(e("e_g_done"), 2 * i + j + 1)
                            load_w(ex, j, 0)
                            sp.wait_ge(e("e_u_done"), 2 * i + j + 1)
                            load_w(ex, j, 1)
                            sp.wait_ge(e("e_d_done1"), 2 * i + j + 1)
                            load_w(ex, j, 2)
                        sp.wait_ge(e("e_y_dve"), 2 * i + j + 1)
                        sp.wait_ge(e("e_y_act"), 2 * i + j + 1)
                        sp.dma_start(Ys[bass.ds(here, P), :], YB[j]).then_inc(e(f"y_stored{j}_"), 16)
                with sp.Fori(0, before_last) as i:
                    turn_of(i, True)
                turn_of(before_last, False)
                sp.wait_ge(e("y_stored1_"), 16 * before_last + 32)
                sp.nop().then_inc(e("experts_over"), 1)

            last_in_slot = {}
            for l in range(DEPTH):
                for cl, name, s in layer_chunks(l):
                    last_in_slot[l, s] = (cl, name)
            small_loads()
            for l in range(DEPTH):
                for cl, name, s in layer_chunks(l):
                    load(cl, name)
                    if (cl, name) == (0, "ada0"):
                        vector_loads()
                experts(l)
            for t in range(LTILES):
                after(sp, "dve_x", (DEPTH - 1, 1, t))
                sp.dma_start(A["out"][0, t * P:(t + 1) * P, :], X[:, t, :]).then_inc(sem("out_stored"), 16)
            sp.wait_ge(sem("out_stored"), 16 * LTILES)

        @block.scalar
        def _(act):
            fn = nc.scalar.activation

            def start():
                for l in range(DEPTH):
                    for name, at in (("mla_q_g", G_MQ), ("mla_k_g", G_MK), ("diff_q_g", G_DQ), ("diff_k_g", G_DK)):
                        g = A[name][l]
                        g = g.rearrange("m d -> (m d)") if len(g.shape) == 2 else g
                        n = g.shape[0]
                        act.dma_start(GAIN[:, l, at:at + n], g.rearrange("(o n) -> o n", o=1).to_broadcast([P, n])).then_inc(sem("gain_loaded"), 16)
                    act.dma_start(LAMR[:, l, :], A["diff_lam"][l].rearrange("m d -> (m d)").rearrange("(o n) -> o n", o=1)
                                  .to_broadcast([P, 4 * DD])).then_inc(sem("lam_loaded"), 16)
                act.dma_start(RB[:, :], A["router_b"].rearrange("(o n) -> o n", o=1).to_broadcast([P, NE])).then_inc(sem("router_loaded"), 16)
                act.dma_start(RW[:, :, :], A["router_w"].rearrange("(k p) n -> p k n", p=P)).then_inc(sem("router_loaded"), 16)
                ps = bank_read(act, ("small", 0))
                sig(fn(CT[:, 0, :], ps[:, 0:2 * KD], ACT.Exp, scale=-1.0), "act_c", 0)
                after(act, "dve_lam", 0)
                sig(fn(LT[:, 4:8], LT[:, 0:4], ACT.Exp), "act_lam", 0)

            def ada_rows():
                for n in range(4):
                    key = ("adar", 0, n)
                    ps = bank_read(act, key)
                    sig(fn(AROW[n], ps[0:2, :], ACT.Copy), "act_adar", n)
                    last_read(key, "act_adar", n)

            def norm(l, f):
                nt = TILES if f == 0 else nq_of(l)
                for t in range(nt):
                    if f == 1:
                        after(act, "dve_x", (l, 0, 1, t))
                        out = OWN[:, 1024 * t:1024 * (t + 1)]
                    else:
                        if l == 0:
                            act.wait_ge(sem(f"x_loaded{t}"), 16)
                        else:
                            after(act, "dve_x", (l - 1, 1, t))
                        out = XN[:, t, :]
                    sig(fn(out, X[:, t, :], ACT.Square, accum_out=SSX[:, t:t + 1]), "act_ssx", (l, f, t))
                if (l, f) == (0, 0):
                    ada_rows()
                after(act, "dve_scl", (l, f))
                for k in range(1, KD, 2):
                    ps = bank_read(act, ("hT", l, f, k))
                    if (l, f, k) == (0, 0, 1):
                        first_hidden(act)
                    for s, c0, cn in streams(nt * P):
                        ins = fn(HT[:, k, c0:c0 + cn], ps[:, c0:c0 + cn], ACT.Identity,
                                 bias=MODS[:, l, 24 * f + k, s:s + 1], scale=SCLS[:, l, f, k, s:s + 1])
                        last = s == streams(nt * P)[-1][0]
                        sig(ins, "act_hT", (l, f, k) if last else (l, f, k, s))
                    last_read(("hT", l, f, k), "act_hT", (l, f, k))

            def prep(l):
                early, late = norm_tasks(l)
                tasks = early + late
                done = 0

                def evac_t(i, task):
                    kind, t, half = task
                    ps = bank_read(act, ("T", l, i))
                    if kind in ("ckv", "cq"):
                        n, dst, v = (2, CKT, V_KVG) if kind == "ckv" else (4, CQT, V_QG)
                        for b in range(n):
                            sig(fn(dst[:, b, t * P:(t + 1) * P], ps[:, b * P:(b + 1) * P], ACT.Copy, scale=VEC[:, l, v + b:v + b + 1]),
                                "act_T", (l, i) if b == n - 1 else (l, i, b))
                    elif kind in ("ukv", "uq"):
                        dst = KTM if kind == "ukv" else QT
                        sig(fn(dst[0:HQ, 4 * half:4 * half + 4, t * P:(t + 1) * P],
                               ps[0:HQ, :].rearrange("p (h n) -> p h n", h=4), ACT.Copy), "act_T", (l, i))
                    else:
                        dst = KTD if kind == "kd" else QTD
                        sig(fn(dst[:, :, t * P:(t + 1) * P], ps[:, :].rearrange("p (h n) -> p h n", h=4), ACT.Copy), "act_T", (l, i))
                    last_read(("T", l, i), "act_T", (l, i))

                for i, (kind, t, half) in enumerate(tasks):
                    if i == len(early):
                        for tt in range(TILES):
                            key = ("proj", l, "vd", tt, 0)
                            ps = bank_read(act, key)
                            sig(fn(VS[:, 1, tt, :], ps[:, :], ACT.Copy), "act_vd", (l, tt))
                            last_read(key, "act_vd", (l, tt))
                        while done < i:
                            evac_t(done, tasks[done])
                            done += 1
                    ps = bank_read(act, ("proj", l, kind, t, half))
                    if kind == "ukv":
                        sig(fn(VS[:, 0, t, 256 * half:256 * (half + 1)].rearrange("p (h d) -> p h d", h=4),
                               ps[:, :].rearrange("p (h d) -> p h d", h=4)[:, :, NOPE:NOPE + MV], ACT.Copy), "act_vm", (l, t, half))
                    if i >= 2:
                        after(act, "dve_ss", (l, i - 2))
                    n = {"ckv": OFF_KD, "uq": 384}.get(kind, 512)
                    sig(fn(SQ[i % 2][:, 0:n], ps[:, 0:n], ACT.Square), "act_sq", (l, i))
                    if i - T_LAG >= done:
                        evac_t(done, tasks[done])
                        done += 1
                while done < len(tasks):
                    evac_t(done, tasks[done])
                    done += 1

            def gate_rows(l, which):
                for s in range(2 if l < DEPTH - 1 else 1):
                    for h in range(2):
                        key = ("gate", l, which, s, h)
                        ps = bank_read(act, key)
                        sig(fn(GATE[:, s, 512 * h:512 * (h + 1)], ps[:, :], ACT.Copy, scale=0.5 if which == 0 else 1.0),
                            "act_gate", (l, which, s, h))
                        last_read(key, "act_gate", (l, which, s, h))

            def attention(l):
                units = attention_units(l)
                nbuf, owner = [0], {}

                def probabilities(u, kind, t, h):
                    k0, kn = keys_of(t)
                    for m in range(1 if kind == "m" else 2):
                        b = nbuf[0] % NP
                        nbuf[0] += 1
                        if b in owner:
                            after(act, "pe_PT", ("PT", l, owner[b]))
                        owner[b] = u
                        book["pbuf" if m == 0 else "pbuf1", (l, u)] = b
                        c = (2 * u + m) % 8
                        after(act, "dve_mx", (l, u, m))
                        ps = bank_read(act, ("S", l, u, m))
                        name, key = ("act_p", (l, u)) if kind == "m" else ("act_pd", (l, u, m))
                        sig(fn(PB[b][:, 0:kn * P], ps[:, 0:kn * P], ACT.Exp, bias=MB[:, c:c + 1],
                               scale=MLA_SCALE if kind == "m" else DIFF_SCALE, accum_out=RSUM[:, c:c + 1]), name, key)
                        last_read(("S", l, u, m), name, key)

                def transposed(u, kind, t, h):
                    if u % 2:
                        return
                    k0, kn = keys_of(t)
                    if u >= 2:
                        key = book.get(("pv_done", (l, u - 2)), ("none", 0))
                        after(act, "pe_O", key)
                    ps = bank_read(act, ("PT", l, u))
                    sig(fn(PTS[0][:, 0:kn * P], ps[:, 0:kn * P], ACT.Copy), "act_pts", (l, u))
                    last_read(("PT", l, u), "act_pts", (l, u))

                def out_t(kind, t):
                    key = ("OT", l, kind, t)
                    ps = bank_read(act, key)
                    scale = 1.0 if kind == "m" else SUBG[:, 0:1]
                    sig(fn(OT[:, int(kind == "d"), :, t * P:(t + 1) * P], ps[:, :].rearrange("p (b n) -> p b n", b=4), ACT.Copy, scale=scale),
                        "act_oT", (l, kind, t))
                    last_read(key, "act_oT", (l, kind, t))

                after(act, "dve_subg", l)
                waiting = []
                for i in range(len(units) + A_VLAG + 2):
                    if i < len(units):
                        probabilities(i, *units[i])
                    if 0 <= i - A_TLAG < len(units):
                        transposed(i - A_TLAG, *units[i - A_TLAG])
                    if 0 <= i - A_VLAG < len(units):
                        kind, t, h = units[i - A_VLAG]
                        if h == (MH if kind == "m" else DH) - 1:
                            if kind == "d":
                                ps = bank_read(act, ("O", l, "d", t))
                                sig(fn(RTF[:, 0:512], ps[:, :], ACT.Square), "act_osq", (l, t))
                            waiting.append((i + 2, kind, t))
                    while waiting and waiting[0][0] <= i:
                        out_t(*waiting.pop(0)[1:])

            def merge(l):
                n = nq_of(l) * P
                for b in range(KD):
                    for j in range(2):
                        if b >= 2:
                            after(act, "dve_mg", (l, b - 2, j))
                        ps = bank_read(act, ("mg", l, b, j))
                        sig(fn(MT[b % 2][j][:, 0:n], ps[:, 0:n], ACT.Tanh, scale=0.5), "act_mg", (l, b, j))
                        last_read(("mg", l, b, j), "act_mg", (l, b, j))

            def router(l):
                nt = nq_of(l)
                ps = bank_read(act, ("logit", l))
                sig(fn(AFF[:, 0:nt * NE], ps[:, 0:nt * NE], ACT.Exp, scale=-1.0), "act_rt", l)
                last_read(("logit", l), "act_rt", l)
                for t in range(nt):
                    key = ("htok", l, t, 0)
                    ps = bank_read(act, key)
                    sig(fn(HTOK[t][:, 0:512], ps[:, :], ACT.Copy), "act_htok", (l, t))
                    last_read(key, "act_htok", (l, t))

            def shared(l):
                nt = nq_of(l)
                for f in range(KF):
                    if f >= 2:
                        after(act, "dve_sh", (l, f - 2))
                    ps = bank_read(act, ("sh", l, f, 0))
                    sig(fn(STH[f % 2][:, 0:nt * P], ps[:, 0:nt * P], ACT.Tanh, scale=0.5), "act_sh", (l, f))
                for t in range(nt):
                    for h in range(2):
                        if (l, t, h) == (0, 0, 0):
                            chunk_free(act, 1, "ada11")
                        key = ("shd", l, t, h)
                        ps = bank_read(act, key)
                        sig(fn(YS[:, t, 512 * h:512 * (h + 1)], ps[:, :], ACT.Copy), "act_ys", (l, t, h))
                        last_read(key, "act_ys", (l, t, h))

            def experts(l):
                e = lambda name: sem(f"{name}{l}")
                act.wait_ge(e("tab_ready"), 1)
                turns = act.value_load(TAB[0:1, 64:65], min_val=1, max_val=TURNS)

                def rows(j):
                    fn(HEX[j][:, 4:8, :], PS[1][:, :].rearrange("p (b n) -> p b n", b=4), ACT.Copy).then_inc(e("e_hex_act"), 1)

                act.wait_ge(e("e_in_done1"), 1)
                rows(0)
                with act.Fori(0, turns) as i:
                    for j in range(2):
                        act.wait_ge(e("e_g_done"), 2 * i + (j + 1))
                        fn(THB[j], PS[2][:, :], ACT.Tanh, scale=0.5).then_inc(e("e_th"), 1)
                        act.wait_ge(e("e_in_done1"), 2 * i + (j + 2))
                        rows(1 - j)
                        act.wait_ge(e("e_ht_done"), 2 * i + (j + 1))
                        fn(HTX[j][:, :, :], PS[4][:, :].rearrange("p (b n) -> p b n", b=4), ACT.Copy).then_inc(e("e_htx"), 1)
                        act.wait_ge(e(f"y_stored{j}_"), 16 * i + 16)
                        act.wait_ge(e("e_d_done1"), 2 * i + (j + 1))
                        fn(YB[j][:, 512:1024], PS[6][:, :], ACT.Copy).then_inc(e("e_y_act"), 1)

            def combine(l):
                for t in range(nq_of(l)):
                    act.wait_ge(sem(f"y_gathered{t}"), 32 * (l + 1))
                    sig(fn(YG[t][0], YG[t][0], ACT.Copy, scale=WTS[:, t, 0:1]), "act_yw", (l, t))

            start()
            for l in range(DEPTH):
                norm(l, 0)
                prep(l)
                attention(l)
                gate_rows(l, 0)
                merge(l)
                norm(l, 1)
                router(l)
                shared(l)
                gate_rows(l, 1)
                experts(l)
                combine(l)

        @block.vector
        def _(dve):
            tt, ts, stt = nc.vector.tensor_tensor, nc.vector.tensor_scalar, nc.vector.scalar_tensor_tensor
            red, cp, rec = nc.vector.tensor_reduce, nc.vector.tensor_copy, nc.vector.reciprocal

            def link(ins):
                chained(dve, "dve_step", ins)

            def start():
                dve.wait_ge(sem("lam_loaded"), 16 * DEPTH)
                r = LAMR.rearrange("p l (a b d) -> p l a b d", a=2, b=2)
                prod = RTF[:, 0:DEPTH * 2 * DD].rearrange("p (l a d) -> p l a d", l=DEPTH, a=2)
                for l in range(DEPTH):
                    link(tt(prod[:, l], r[:, l, :, 0], r[:, l, :, 1], ALU.mult))
                sig(red(LT[:, 0:4], RTF[:, 0:256].rearrange("p (a d) -> p a d", a=4), AX.X, ALU.add), "dve_lam", 0)
                after(dve, "act_lam", 0)
                for l in range(DEPTH):
                    lam_init = 0.8 - 0.6 * math.exp(-0.3 * l)
                    link(tt(NLAM[:, l:l + 1], LT[:, 5 + 2 * l:6 + 2 * l], LT[:, 4 + 2 * l:5 + 2 * l], ALU.subtract))
                    link(ts(NLAM[:, l:l + 1], NLAM[:, l:l + 1], -lam_init, None, ALU.add))
                after(dve, "act_c", 0)
                ps = bank_read(dve, ("small", 0))
                link(ts(CT[:, 1, :], CT[:, 0, :], 1.0, None, ALU.add))
                link(rec(CT[:, 0, :], CT[:, 1, :]))
                sig(tt(CS[:, :], CT[:, 0, :], ps[:, 0:2 * KD], ALU.mult), "dve_c", 0)
                last_read(("small", 0), "dve_c", 0)
                ps = bank_read(dve, ("small", 1))
                for l in range(DEPTH):
                    sig(cp(VEC[:, l, :], ps[:, P * l:P * l + V_END]), "dve_vec", l)
                last_read(("small", 1), "dve_vec", DEPTH - 1)
                after(dve, "dve_vec", DEPTH - 1)
                for n in range(4):
                    ada_bias(0, n)

            def ada_bias(l, n):
                ns = mod_streams(l, n)
                key = ("ada", l, n)
                ps = bank_read(dve, key)
                b = VEC[:, l, V_ADAB + 4 * n:V_ADAB + 4 * n + 4].rearrange("p (m o) -> p m o", o=1).to_broadcast([P, 4, ns])
                sig(tt(MODS[:, l, 4 * n:4 * n + 4, 0:ns], ps[:, 0:8].rearrange("p (m s) -> p m s", s=2)[:, :, 0:ns], b, ALU.add),
                    "dve_mod", (l, n))
                last_read(key, "dve_mod", (l, n))

            biased = [4]

            def ada_flush(l, n):
                while biased[0] <= 12 * l + n:
                    ada_bias(biased[0] // 12, biased[0] % 12)
                    biased[0] += 1

            def ada_work(phase, step):
                for l, n, k, s in ada_share(phase, step)[0]:
                    two = mod_streams(l, n) == 2
                    if two and k == 0 or not two and k == KD - 1:
                        ada_flush(*divmod(12 * l + n - 1, 12))
                    w = chunk(dve, l, f"ada{n}").rearrange("p (k n) -> p k n", k=KD)[:, k, :]
                    acc = ada_buffer(l, n, s)
                    b = s if two else n % 2
                    c = CS[:, s * KD + k:s * KD + k + 1]
                    if k == 0:
                        if b in acc_of:
                            after(dve, "pe_ada", acc_of[b])
                        acc_of[b] = ("ada", l, n)
                        ins = ts(acc, w, c, None, ALU.mult)
                    else:
                        after(dve, "dve_acc", (l, n, k - 1, s))
                        ins = stt(acc, w, c, acc, ALU.mult, ALU.add)
                    sig(ins, "dve_acc", (l, n, k, s))
                    book["chunk_done", (l, f"ada{n}")] = ("dve_acc", (l, n, k, s))

            acc_of = {}

            def modulation(l, f):
                sc, v = (8, V_AG) if f == 0 else (32, V_FG)
                g = VEC[:, l, v:v + KD].rearrange("p (m o) -> p m o", o=1)
                last = mod_streams(l, 4 * f + 4 * f) - 1
                for s in range(last + 1):
                    sig(stt(SCLS[:, l, f, :, s:s + 1], MODS[:, l, sc:sc + KD, s:s + 1], 1.0, g, ALU.add, ALU.mult), "dve_scl",
                        (l, f) if s == last else (l, f, s))
                after(dve, "dve_scl", (l, f))

            def norm(l, f):
                nt = TILES if f == 0 else nq_of(l)
                for t in range(nt):
                    after(dve, "pool_rx", (l, f, t))
                    sig(ts(XN[:, t, :], X[:, t, :], RX[:, t:t + 1], None, ALU.mult), "dve_xn", (l, f, t))

            def hidden(l, f):
                nt = TILES if f == 0 else nq_of(l)
                for k in range(0, KD, 2):
                    ps = bank_read(dve, ("hT", l, f, k))
                    if (l, f, k) == (0, 0, 0):
                        first_hidden(dve)
                    st = streams(nt * P)
                    for s, c0, cn in st:
                        sig(ts(HT[:, k, c0:c0 + cn], ps[:, c0:c0 + cn], SCLS[:, l, f, k, s:s + 1], MODS[:, l, 24 * f + k, s:s + 1], ALU.mult, ALU.add),
                            "dve_hT", (l, f, k) if s == st[-1][0] else (l, f, k, s))
                    last_read(("hT", l, f, k), "dve_hT", (l, f, k))

            def wide(col, n, w):
                return col.rearrange("p (g o) -> p g o", o=1).to_broadcast([P, n, w])

            def prep(l):
                early, late = norm_tasks(l)
                tasks = early + late

                def sums(i):
                    kind, t, half = tasks[i]
                    after(dve, "act_sq", (l, i))
                    if i >= 4:
                        after(dve, "pool_r", (l, i - 4))
                    sq, ss = SQ[i % 2], SS[:, i % 4]
                    if kind == "ckv":
                        sig(red(ss[:, 0:1], sq[:, 0:KVR], AX.X, ALU.add), "dve_ss", (l, i, 0))
                        ins = red(ss[:, 1:2], sq[:, KVR:OFF_KD], AX.X, ALU.add)
                    elif kind == "cq":
                        ins = red(ss[:, 0:1], sq[:, :], AX.X, ALU.add)
                    elif kind == "ukv":
                        ins = red(ss[:, 0:4], sq.rearrange("p (h d) -> p h d", h=4)[:, :, 0:NOPE], AX.X, ALU.add)
                    elif kind == "uq":
                        q = sq[:, 0:384].rearrange("p (h d) -> p h d", h=4)
                        sig(red(ss[:, 0:4], q[:, :, 0:NOPE], AX.X, ALU.add), "dve_ss", (l, i, 0))
                        ins = red(ss[:, 4:8], q[:, :, NOPE:HQ], AX.X, ALU.add)
                    else:
                        ins = red(ss[:, 0:8], sq.rearrange("p (h d) -> p h d", h=8), AX.X, ALU.add)
                    sig(ins, "dve_ss", (l, i))

                def scale(i):
                    kind, t, half = tasks[i]
                    key = ("proj", l, kind, t, half)
                    after(dve, "pool_r", (l, i))
                    if i >= 4:
                        after(dve, "pe_T", ("T", l, i - 4))
                    ps, r, tm = bank_read(dve, key), RR[:, i % 4], TM[i % 4]
                    name = tm_sem(kind) if kind in ("ckv", "cq") else "dve_sc"
                    if kind == "ckv":
                        sig(ts(KR[:, t, :], ps[:, KVR:OFF_KD], r[:, 1:2], None, ALU.mult), "dve_kr", (l, t))
                        ins = ts(tm[:, 0:KVR], ps[:, 0:KVR], r[:, 0:1], None, ALU.mult)
                    elif kind == "cq":
                        ins = ts(tm, ps[:, :], r[:, 0:1], None, ALU.mult)
                    elif kind == "ukv":
                        ins = tt(tm[:, 0:384].rearrange("p (h d) -> p h d", h=4)[:, :, 0:NOPE],
                                 ps[:, :].rearrange("p (h d) -> p h d", h=4)[:, :, 0:NOPE], wide(r[:, 0:4], 4, NOPE), ALU.mult)
                    elif kind == "uq":
                        q, o = (x[:, 0:384].rearrange("p (h d) -> p h d", h=4) for x in (ps, tm))
                        sig(tt(o[:, :, 0:NOPE], q[:, :, 0:NOPE], wide(r[:, 0:4], 4, NOPE), ALU.mult), name, (l, i, 0))
                        ins = tt(o[:, :, NOPE:HQ], q[:, :, NOPE:HQ], wide(r[:, 4:8], 4, ROPE), ALU.mult)
                    else:
                        ins = tt(tm.rearrange("p (h d) -> p h d", h=8), ps[:, :].rearrange("p (h d) -> p h d", h=8),
                                 wide(r[:, 0:8], 8, DD), ALU.mult)
                    sig(ins, name, (l, i))
                    last_read(key, name, (l, i))

                sums(0)
                for i in range(len(tasks)):
                    if i + 1 < len(tasks) and i + 1 != len(early):
                        sums(i + 1)
                    scale(i)
                    if l == 0 and i < len(early):
                        ada_work("prep", i)
                    if i + 1 == len(early):
                        if l == 0:
                            ada_work("vd", 0)
                            ada_flush(0, 10)
                        sums(i + 1)

            def gate_diagonals(l, which):
                m0 = 16 if which == 0 else 40
                for s in range(2 if l < DEPTH - 1 else 1):
                    for h in range(2):
                        if s:
                            after(dve, "pe_gate", ("gate", l, which, s - 1, h))
                        for b in range(4):
                            g = MODS[:, l, m0 + 4 * h + b, s:s + 1]
                            sig(ts(DIAG[:, h, b * P:(b + 1) * P], ident, g, None, ALU.mult), "dve_diag",
                                (l, which, s, h) if b == 3 else (l, which, s, h, b))

            def attention(l):
                units = attention_units(l)
                lam_init = 0.8 - 0.6 * math.exp(-0.3 * l)
                sig(ts(SUBG[:, :], VEC[:, l, V_SUB:V_SUB + 1], 1.0 - lam_init, None, ALU.mult), "dve_subg", l)

                def maxima(u, kind, t, h):
                    k0, kn = keys_of(t)
                    for m in range(1 if kind == "m" else 2):
                        c = (2 * u + m) % 8
                        ps = bank_read(dve, ("S", l, u, m))
                        link(red(MX[:, c:c + 1], ps[:, 0:kn * P], AX.X, ALU.max, negate=True))
                        sig(ts(MB[:, c:c + 1], MX[:, c:c + 1], MLA_SCALE if kind == "m" else DIFF_SCALE, None, ALU.mult),
                            "dve_mx", (l, u, m))

                def weights(u, kind, t, h):
                    k0, kn = keys_of(t)
                    c = (2 * u) % 8
                    if kind == "m":
                        after(dve, "act_p", (l, u))
                        sig(rec(RINV[:, t % 2, h:h + 1], RSUM[:, c:c + 1]), "dve_rinv", (l, u))
                        return
                    after(dve, "act_pd", (l, u, 1))
                    link(rec(RDIF[:, c:c + 2], RSUM[:, c:c + 2]))
                    link(tt(RDIF[:, c + 1:c + 2], RDIF[:, c + 1:c + 2], NLAM[:, l:l + 1], ALU.mult))
                    b0, b1 = (PB[book.get((x, (l, u)), 0)][:, 0:kn * P] for x in ("pbuf", "pbuf1"))
                    link(ts(b1, b1, RDIF[:, c + 1:c + 2], None, ALU.mult))
                    sig(stt(b0, b0, RDIF[:, c:c + 1], b1, ALU.mult, ALU.add), "dve_a", (l, u))

                def transposed(u, kind, t, h):
                    if u % 2 == 0:
                        return
                    k0, kn = keys_of(t)
                    if u >= 2:
                        after(dve, "pe_O", book.get(("pv_done", (l, u - 2)), ("none", 0)))
                    ps = bank_read(dve, ("PT", l, u))
                    sig(cp(PTS[1][:, 0:kn * P], ps[:, 0:kn * P]), "dve_pts", (l, u))
                    last_read(("PT", l, u), "dve_pts", (l, u))

                def out_rows(kind, t):
                    ps = bank_read(dve, ("O", l, kind, t))
                    before_ = ("OT", l, "m", t) if kind == "d" else ("OT", l, "d", t - 1) if t else None
                    if before_:
                        after(dve, "pe_OT", before_)
                    if kind == "m":
                        after(dve, "dve_rinv", (l, 12 * t + MH - 1))
                        r, n, w = RINV[:, t % 2, :], MH, MV
                    else:
                        after(dve, "pool_ro", (l, t))
                        r, n, w = RO, DH, DV
                    sig(tt(OTM.rearrange("p (h d) -> p h d", h=n), ps[:, :].rearrange("p (h d) -> p h d", h=n), wide(r, n, w), ALU.mult),
                        "dve_o", (l, kind, t))
                    last_read(("O", l, kind, t), "dve_o", (l, kind, t))

                waiting = []
                for i in range(len(units) + A_VLAG + 2):
                    if i < len(units):
                        maxima(i, *units[i])
                    if 0 <= i - 1 < len(units):
                        weights(i - 1, *units[i - 1])
                    if 0 <= i - A_TLAG < len(units):
                        transposed(i - A_TLAG, *units[i - A_TLAG])
                    if 0 <= i - A_VLAG < len(units):
                        kind, t, h = units[i - A_VLAG]
                        if h == (MH if kind == "m" else DH) - 1:
                            if kind == "d":
                                after(dve, "act_osq", (l, t))
                                sig(red(SSO[:, :], RTF[:, 0:512].rearrange("p (h d) -> p h d", h=DH), AX.X, ALU.add), "dve_sso", (l, t))
                            waiting.append((i + 1, kind, t))
                    while waiting and waiting[0][0] <= i:
                        out_rows(*waiting.pop(0)[1:])

            def merge(l):
                n = nq_of(l) * P
                for b in range(KD):
                    for j in range(2):
                        if b >= 2:
                            after(dve, "pool_y", (l, b - 2))
                        after(dve, "act_mg", (l, b, j))
                        key = ("mg", l, b, 2 + j)
                        ps = bank_read(dve, key)
                        sig(stt(MY[b % 2][j][:, 0:n], MT[b % 2][j][:, 0:n], 1.0, ps[:, 0:n], ALU.add, ALU.mult), "dve_mg", (l, b, j))
                        last_read(key, "dve_mg", (l, b, j))
                        if l == 0:
                            ada_work("merge", 2 * b + j)

            def out_proj(l):
                after(dve, "act_gate", (l, 0, 1 if l < DEPTH - 1 else 0, 1))
                for h in range(2):
                    for t in range(nq_of(l)):
                        key = ("out", l, h, t)
                        ps = bank_read(dve, key)
                        tmp = STG[:, 512 * (t % 2):512 * (t % 2 + 1)]
                        cols = slice(512 * h, 512 * (h + 1))
                        sig(tt(tmp, ps[:, :], GATE[:, t // LTILES, cols], ALU.mult), "dve_og", (l, h, t))
                        last_read(key, "dve_og", (l, h, t))
                        after(dve, "dve_og", (l, h, t))
                        sig(tt(X[:, t, cols], X[:, t, cols], tmp, ALU.add), "dve_x", (l, 0, h, t))

            def htok(l):
                for t in range(nq_of(l)):
                    key = ("htok", l, t, 1)
                    ps = bank_read(dve, key)
                    sig(cp(HTOK[t][:, 512:1024], ps[:, :]), "dve_htok", (l, t))
                    last_read(key, "dve_htok", (l, t))

            def route_choice(l):
                nt = nq_of(l)
                g3 = lambda x, a, b: x.rearrange("p (a b) -> p a b", a=a)
                aff, sel, t1 = (x[:, 0:nt * NE] for x in (AFF, SEL, TMPR))
                after(dve, "act_rt", l)
                dve.wait_ge(sem("router_loaded"), 32)
                link(ts(t1, aff, 1.0, None, ALU.add))
                link(rec(aff, t1))
                rb = RB[:, :].rearrange("p (o n) -> p o n", o=1).to_broadcast([P, nt, NE])
                link(tt(g3(sel, nt, NE), g3(aff, nt, NE), rb, ALU.add))
                s4 = g3(sel, nt * NG, EPG)
                pr = PAIR[:, 0:nt * NG * 6].rearrange("p (g n) -> p g n", n=6)
                link(tt(pr[:, :, 0:3], s4[:, :, 0:3], s4[:, :, 1:4], ALU.add))
                link(tt(pr[:, :, 3:5], s4[:, :, 0:2], s4[:, :, 2:4], ALU.add))
                link(tt(pr[:, :, 5:6], s4[:, :, 0:1], s4[:, :, 3:4], ALU.add))
                gs, gm, gk = (GRP[:, i, 0:nt * NG] for i in range(3))
                link(red(gs, pr, AX.X, ALU.max))
                link(red(gm[:, 0:nt], g3(gs, nt, NG), AX.X, ALU.max))
                link(tt(g3(gk, nt, NG), g3(gs, nt, NG), wide(gm[:, 0:nt], nt, NG), ALU.is_equal))
                tie = CST[:, C_TIE:C_TIE + NG].rearrange("p (o n) -> p o n", o=1).to_broadcast([P, nt, NG])
                link(tt(g3(gk, nt, NG), g3(gk, nt, NG), tie, ALU.mult))
                link(red(gm[:, 0:nt], g3(gk, nt, NG), AX.X, ALU.max))
                link(tt(g3(gk, nt, NG), g3(gk, nt, NG), wide(gm[:, 0:nt], nt, NG), ALU.is_equal))
                link(tt(s4, s4, wide(gk, nt * NG, EPG), ALU.mult))
                link(ts(gs, gk, 1.0, BIG, ALU.subtract, ALU.mult))
                link(tt(s4, s4, wide(gs, nt * NG, EPG), ALU.add))
                for t in range(nt):
                    link(nc.vector.max(out=BEST[:, t, :], in_=sel[:, NE * t:NE * (t + 1)]))
                    link(nc.vector.max_index(out=BIDX[:, t, :], in_max=BEST[:, t, :], in_values=sel[:, NE * t:NE * (t + 1)]))
                link(cp(FIDX[:, 0:nt, :], BIDX[:, 0:nt, 0:2]))
                iota = CST[:, C_IOTA:C_IOTA + NE].rearrange("p (o n) -> p o n", o=1).to_broadcast([P, nt, NE])
                for k in range(2):
                    link(tt(HOT[k][:, 0:nt, :], iota, FIDX[:, 0:nt, k:k + 1].to_broadcast([P, nt, NE]), ALU.is_equal))
                    link(tt(g3(t1, nt, NE), HOT[k][:, 0:nt, :], g3(aff, nt, NE), ALU.mult))
                    link(red(WTS[:, 0:nt, k], g3(t1, nt, NE), AX.X, ALU.add))
                link(tt(gm[:, 0:nt], WTS[:, 0:nt, 0], WTS[:, 0:nt, 1], ALU.add))
                link(rec(gs[:, 0:nt], gm[:, 0:nt]))
                link(tt(WTS[:, 0:nt, :], WTS[:, 0:nt, :], wide(gs[:, 0:nt], nt, 2), ALU.mult))
                sig(tt(MSK[:, 0:nt, :], HOT[0][:, 0:nt, :], HOT[1][:, 0:nt, :], ALU.add), "dve_mask", l)

            def route_places(l):
                nt = nq_of(l)
                g3 = lambda x, a: x.rearrange("p (a b) -> p a b", a=a)
                ps = bank_read(dve, ("place", l))
                cnt, inc, off = (CNT[:, i, :] for i in range(3))
                link(cp(cnt, ps[:, 64:64 + NE]))
                link(nc.vector.tensor_tensor_scan(inc, ones[:, 0:NE], cnt, 0.0, ALU.mult, ALU.add))
                link(tt(off, inc, cnt, ALU.subtract))
                t1 = TMPR[:, 0:nt * NE]
                off_w = off.rearrange("p (o n) -> p o n", o=1).to_broadcast([P, nt, NE])
                sig(tt(g3(SEL[:, 0:nt * NE], nt), g3(ps[:, 0:nt * NE], nt), off_w, ALU.add), "dve_plc", l)
                last_read(("place", l), "dve_plc", l)
                after(dve, "dve_plc", l)
                for k in range(2):
                    link(tt(g3(t1, nt), HOT[k][:, 0:nt, :], g3(SEL[:, 0:nt * NE], nt), ALU.mult))
                    link(red(SLF[:, 0:nt, k], g3(t1, nt), AX.X, ALU.add))
                sig(cp(SLOT[:, 0:nt, :], SLF[:, 0:nt, :]), "dve_slot", l)
                rc = CST[:, C_RCAND:C_RCAND + CAND]
                act_, run, row, hit = (CND[:, i, :] for i in range(4))
                link(tt(g3(act_, NE), wide(cnt, NE, TILES), g3(rc, NE), ALU.is_gt))
                link(nc.vector.tensor_tensor_scan(run, CONES, act_, 0.0, ALU.mult, ALU.add))
                link(tt(g3(row, NE), wide(off, NE, TILES), g3(rc, NE), ALU.add))
                link(stt(hit, run, CST[:, C_JOB:C_JOB + 1], act_, ALU.is_equal, ALU.mult))
                link(tt(act_, hit, CST[:, C_ECAND:C_ECAND + CAND], ALU.mult))
                link(red(JOBC[:, 0:1], act_, AX.X, ALU.add))
                link(tt(row, hit, row, ALU.mult))
                link(red(JOBC[:, 1:2], row, AX.X, ALU.add))
                link(red(JOBC[:, 2:3], hit, AX.X, ALU.add))
                link(ts(JOBC[:, 2:3], JOBC[:, 2:3], -float(SORTED), float(SORTED), ALU.mult, ALU.add))
                sig(tt(JOBC[:, 1:2], JOBC[:, 1:2], JOBC[:, 2:3], ALU.add), "dve_jobcol", l)
                link(ts(TABI[:, 0:1], run[0:1, CAND - 1:CAND], 1.0, None, ALU.add))
                link(ts(TAB[0:1, 64:65], TABI[:, 0:1], 1, None, ALU.arith_shift_right))
                link(ts(TAB[0:1, 65:66], TAB[0:1, 64:65], 1.0, None, ALU.subtract))

            def route_table(l):
                ps = bank_read(dve, ("jobs", l))
                link(cp(TAB[0:1, 0:32], ps[0:1, 0:32]))
                cp(TAB[0:1, 32:64], ps[0:1, P:P + 32]).then_inc(sem(f"tab_ready{l}"), 1)
                book["read", ("jobs", l)] = (f"tab_ready{l}", 0)
                book[f"tab_ready{l}", 0] = 1

            def shared(l, f):
                n = nq_of(l) * P
                after(dve, "act_sh", (l, f))
                ps = bank_read(dve, ("sh", l, f, 0))
                sig(stt(SVV[f % 2][:, 0:n], STH[f % 2][:, 0:n], 1.0, ps[:, 0:n], ALU.add, ALU.mult), "dve_sv", (l, f))
                last_read(("sh", l, f, 0), "dve_sv", (l, f))
                after(dve, "dve_sv", (l, f))
                ps = bank_read(dve, ("sh", l, f, 1))
                sig(stt(HET[:, f, 0:n], SVV[f % 2][:, 0:n], 0.5, ps[:, 0:n], ALU.mult, ALU.mult), "dve_sh", (l, f))
                last_read(("sh", l, f, 1), "dve_sh", (l, f))

            def experts(l):
                e = lambda name: sem(f"{name}{l}")
                dve.wait_ge(e("tab_ready"), 1)
                turns = dve.value_load(TAB[0:1, 64:65], min_val=1, max_val=TURNS)

                def rows(j):
                    cp(HEX[j][:, 0:4, :], PS[0][:, :].rearrange("p (b n) -> p b n", b=4)).then_inc(e("e_hex_dve"), 1)

                dve.wait_ge(e("e_in_done0"), 1)
                rows(0)
                with dve.Fori(0, turns) as i:
                    for j in range(2):
                        dve.wait_ge(e("e_th"), 2 * i + (j + 1))
                        stt(THB[j], THB[j], 1.0, PS[2][:, :], ALU.add, ALU.mult).then_inc(e("e_v"), 1)
                        dve.wait_ge(e("e_v"), 2 * i + (j + 1))
                        dve.wait_ge(e("e_u_done"), 2 * i + (j + 1))
                        stt(HID[j], THB[j], 0.5, PS[3][:, :], ALU.mult, ALU.mult).then_inc(e("e_hid_done"), 1)
                        dve.wait_ge(e("e_in_done0"), 2 * i + (j + 2))
                        rows(1 - j)
                        if j == 1:
                            dve.wait_ge(e("y_stored0_"), 16 * i + 32)
                        else:
                            dve.wait_ge(e("y_stored1_"), 16 * i + 16)
                        dve.wait_ge(e("e_d_done0"), 2 * i + (j + 1))
                        cp(YB[j][:, 0:512], PS[5][:, :]).then_inc(e("e_y_dve"), 1)
                dve.wait_ge(e("experts_over"), 1)

            def combine(l):
                for t in range(nq_of(l)):
                    y0, y1 = YG[t]
                    after(dve, "act_yw", (l, t))
                    link(stt(y0, y1, WTS[:, t, 1:2], y0, ALU.mult, ALU.add))
                    link(tt(y0, y0, GATE[:, t // LTILES, :], ALU.mult))
                    sig(tt(X[:, t, :], X[:, t, :], y0, ALU.add), "dve_x", (l, 1, t))

            start()
            for l in range(DEPTH):
                if l == 0:
                    after(dve, "dve_mod", (0, 3))
                modulation(l, 0)
                norm(l, 0)
                hidden(l, 0)
                prep(l)
                attention(l)
                if l == 0:
                    ada_flush(0, 10)
                    after(dve, "dve_mod", (0, 10))
                after(dve, "pe_OT", ("OT", l, "d", nq_of(l) - 1))
                gate_diagonals(l, 0)
                merge(l)
                if l == 0:
                    ada_flush(1, 11)
                    after(dve, "dve_mod", (1, 11))
                    modulation(0, 1)
                    modulation(1, 1)
                out_proj(l)
                norm(l, 1)
                hidden(l, 1)
                route_choice(l)
                htok(l)
                shared(l, 0)
                route_places(l)
                shared(l, 1)
                shared(l, 2)
                route_table(l)
                shared(l, 3)
                gate_diagonals(l, 1)
                after(dve, "act_gate", (l, 1, 1 if l < DEPTH - 1 else 0, 1))
                for t in range(nq_of(l)):
                    after(dve, "act_ys", (l, t, 1))
                    link(tt(YS[:, t, :], YS[:, t, :], GATE[:, t // LTILES, :], ALU.mult))
                    link(tt(X[:, t, :], X[:, t, :], YS[:, t, :], ALU.add))
                experts(l)
                combine(l)

        @block.gpsimd
        def _(pool):
            gt, gs_, gc = nc.gpsimd.tensor_tensor, nc.gpsimd.tensor_scalar, nc.gpsimd.tensor_copy

            def link(ins):
                chained(pool, "pool_step", ins)

            def start():
                link(pool.memset(HALF[:, :], -0.5))
                link(pool.memset(ZERO, 0.0))
                pool.dma_start(Hs[SORTED:SORTED + P, :], ZERO).then_inc(sem("pad_stored"), 16)
                pool.wait_ge(sem("gain_loaded"), 16 * 4 * DEPTH)
                pool.wait_ge(sem("const_loaded"), 16)

            def norm(l, f):
                nt = TILES if f == 0 else nq_of(l)
                for t in range(nt):
                    after(pool, "act_ssx", (l, f, t))
                    link(gs_(RX[:, t:t + 1], SSX[:, t:t + 1], 1.0 / D, EPS, ALU.mult, ALU.add))
                    sig(gt(RX[:, t:t + 1], RX[:, t:t + 1], HALF[:, 0:1], ALU.pow), "pool_rx", (l, f, t))

            def rotate(view, cos, sin, groups, q):
                x1, x2 = view
                shape = [P, groups, 2, q]
                c, s = (x.rearrange("p (o a q) -> p o a q", o=1, a=2).to_broadcast(shape) for x in (cos, sin))
                a, b, cc, d = (RT[:, i, 0:groups * 2 * q].rearrange("p (g a q) -> p g a q", g=groups, a=2) for i in range(4))
                link(gt(a, x1, c, ALU.mult))
                link(gt(b, x2, s, ALU.mult))
                link(gt(cc, x1, s, ALU.mult))
                link(gt(d, x2, c, ALU.mult))
                link(gt(x1, a, b, ALU.subtract))
                return gt(x2, cc, d, ALU.add)

            def halves(x, groups, q):
                v = x.rearrange("p g (a h q) -> p g a h q", a=2, h=2)
                return v[:, :, :, 0, :], v[:, :, :, 1, :]

            def prep(l):
                early, late = norm_tasks(l)
                tasks = early + late

                def roots(i):
                    kind, t, half = tasks[i]
                    after(pool, "dve_ss", (l, i))
                    ss, r = SS[:, i % 4], RR[:, i % 4]
                    parts = {"ckv": [(0, 1, KVR), (1, 2, ROPE)], "cq": [(0, 1, QR)], "ukv": [(0, 4, NOPE)],
                             "uq": [(0, 4, NOPE), (4, 8, ROPE)]}.get(kind, [(0, 8, DD)])
                    for a, b, w in parts:
                        link(gs_(r[:, a:b], ss[:, a:b], 1.0 / w, EPS, ALU.mult, ALU.add))
                    n = parts[-1][1]
                    sig(gt(r[:, 0:n], r[:, 0:n], HALF[:, 0:n], ALU.pow), "pool_r", (l, i))

                def gains(i):
                    kind, t, half = tasks[i]
                    if kind == "cq":
                        return
                    lat = t < LTILES
                    tm = TM[i % 4]
                    if kind == "ckv":
                        after(pool, "dve_kr", (l, t))
                        x = KR[:, t, :]
                        ins = gt(x, x, GAIN[:, l, G_MK + NOPE:G_MK + HQ], ALU.mult)
                        if lat:
                            link(ins)
                            ins = rotate(halves(x.rearrange("p (g d) -> p g d", g=1), 1, 8), CST[:, C_COSM + 16 * t:C_COSM + 16 * (t + 1)],
                                         CST[:, C_SINM + 16 * t:C_SINM + 16 * (t + 1)], 1, 8)
                        sig(ins, "pool_kr", (l, t))
                        return
                    after(pool, "dve_sc", (l, i))
                    row = lambda at, n, g: GAIN[:, l, at:at + n].rearrange("p (o n) -> p o n", o=1).to_broadcast([P, g, n])
                    if kind == "ukv":
                        k = tm[:, 0:384].rearrange("p (h d) -> p h d", h=4)
                        link(gt(k[:, :, 0:NOPE], k[:, :, 0:NOPE], row(G_MK, NOPE, 4), ALU.mult))
                        after(pool, "pool_kr", (l, t))
                        ins = gc(k[:, :, NOPE:HQ], KR[:, t, :].rearrange("p (o n) -> p o n", o=1).to_broadcast([P, 4, ROPE]))
                    elif kind == "uq":
                        q = tm[:, 0:384].rearrange("p (h d) -> p h d", h=4)
                        ins = gt(q, q, row(G_MQ, HQ, 4), ALU.mult)
                        if lat:
                            link(ins)
                            ins = rotate(halves(q[:, :, NOPE:HQ], 4, 8), CST[:, C_COSM + 16 * t:C_COSM + 16 * (t + 1)],
                                         CST[:, C_SINM + 16 * t:C_SINM + 16 * (t + 1)], 4, 8)
                    else:
                        x = tm.rearrange("p (h d) -> p h d", h=4)
                        ins = gt(x, x, row(G_DK if kind == "kd" else G_DQ, 2 * DD, 4), ALU.mult)
                        if lat:
                            link(ins)
                            ins = rotate(halves(tm.rearrange("p (h d) -> p h d", h=8), 8, 16), CST[:, C_COSD + 32 * t:C_COSD + 32 * (t + 1)],
                                         CST[:, C_SIND + 32 * t:C_SIND + 32 * (t + 1)], 8, 16)
                    sig(ins, "pool_tm", (l, i))

                roots(0)
                for i in range(len(tasks)):
                    if i + 1 < len(tasks) and i + 1 != len(early):
                        roots(i + 1)
                    gains(i)
                    if i + 1 == len(early):
                        roots(i + 1)

            def attention(l):
                for t in range(nq_of(l)):
                    after(pool, "dve_sso", (l, t))
                    link(gs_(RO[:, :], SSO[:, :], 1.0 / DV, EPS, ALU.mult, ALU.add))
                    sig(gt(RO[:, :], RO[:, :], HALF[:, 0:DH], ALU.pow), "pool_ro", (l, t))

            def merge(l):
                n = nq_of(l) * P
                for b in range(KD):
                    after(pool, "dve_mg", (l, b, 1))
                    sig(gt(YT[:, b, 0:n], MY[b % 2][0][:, 0:n], MY[b % 2][1][:, 0:n], ALU.add), "pool_y", (l, b))

            def scatter(l):
                after(pool, "dve_slot", l)
                for t in range(nq_of(l)):
                    after(pool, "act_htok", (l, t))
                    after(pool, "dve_htok", (l, t))
                    for k in range(2):
                        pool.indirect_dma_start(Hs[0:SORTED, :], bass.IndirectOffsetOnAxis(ap=SLOT[:, t, k:k + 1], axis=0),
                                                HTOK[t], None).then_inc(sem(f"sorted_stored{l}"), 16)

            def gather(l):
                pool.wait_ge(sem(f"experts_over{l}"), 1)
                for t in range(nq_of(l)):
                    for k in range(2):
                        pool.indirect_dma_start(YG[t][k], None, Ys[0:SORTED, :],
                                                bass.IndirectOffsetOnAxis(ap=SLOT[:, t, k:k + 1], axis=0)).then_inc(sem(f"y_gathered{t}"), 16)

            start()
            for l in range(DEPTH):
                norm(l, 0)
                prep(l)
                attention(l)
                merge(l)
                norm(l, 1)
                scatter(l)
                gather(l)


_INS = ["x", "c", "ctx", "c_ctx", "ada_w", "ada_b", "attn_norm_g", "ffn_norm_g", "w_in", "mla_q_norm_g", "mla_w_uq",
        "mla_kv_norm_g", "mla_w_ukv", "mla_q_g", "mla_k_g", "diff_q_g", "diff_k_g", "diff_lam", "diff_sub_g", "w_o_mla",
        "w_o_diff", "w_out", "router_w", "router_b", "moe_w_gate", "moe_w_up", "moe_w_down", "sh_w_gate", "sh_w_up", "sh_w_down"]


def kernel(**inputs):
    import numpy as _np
    import concourse.bacc as _bacc
    from concourse import mybir as _mybir
    from concourse.bass_utils import run_bass_kernel_spmd as _run

    def program(book):
        nc = _bacc.Bacc("TRN2", target_bir_lowering=False, num_devices=1)
        args = {}
        for name, a in arrays.items():
            args[name[3:]] = nc.dram_tensor(name, a.shape, _mybir.dt.from_np(a.dtype), kind="ExternalInput").ap()
        args["out"] = nc.dram_tensor("out_0", (1, SEQ, D), _mybir.dt.float32, kind="ExternalOutput").ap()
        build(nc, args, book)
        return nc

    arrays = {f"in_{name}": _np.ascontiguousarray(inputs[name]) for name in _INS}
    arrays["in_consts"] = constants()
    book = {}
    program(book)
    r = _run(program(book), [arrays], core_ids=[0])
    return r.results[0]["out_0"]
```

```python
import concourse.bass as bass
from concourse import mybir
from contextlib import ExitStack
import math
import numpy as np

F32 = mybir.dt.float32
F32R = mybir.dt.float32r
I32 = mybir.dt.int32
U32 = mybir.dt.uint32
ALU = mybir.AluOpType
ACT = mybir.ActivationFunctionType
AX = mybir.AxisListType

P = 128
D = 1024
KD = D // P
SEQ = 256
CTX = 256
NTOK = SEQ + CTX
TILES = NTOK // P
LTILES = SEQ // P
DEPTH = 2
EPS = 1e-6
GRID_W = 64
ROPE_BASE = 10000.0
MH, NOPE, ROPE, MV = 8, 64, 32, 64
HQ = NOPE + ROPE
QR, KVR = 512, 256
DH, DD, DV = 4, 64, 128
MLA_SCALE = 1.0 / math.sqrt(HQ)
DIFF_SCALE = 1.0 / math.sqrt(DD)
OFF_KD = KVR + ROPE
OFF_VD = OFF_KD + 2 * DH * DD
OFF_CQ = OFF_VD + DH * DV
OFF_QD = OFF_CQ + QR
OFF_GATE = OFF_QD + 2 * DH * DD
NE, EPG, NG = 16, 4, 4
FE = 512
KF = FE // P
CAND = NE * TILES
SORTED = 2 * NTOK
ROWS = [P, P // 2]
assert DEPTH == 2
TURNS = (NE + (SORTED - NE) // P + 1) // 2
CHUNK = 4096
WSLOTS = 4
BIG = 1.0e30

C_ID, C_TRI, C_ONE = 0, 128, 256
C_IOTA, C_TIE, C_ECAND, C_RCAND, C_JOB = 384, 400, 404, 468, 532
C_COSM, C_SINM, C_COSD, C_SIND = 533, 565, 597, 661
C_END = 725


def constants():
    c = np.zeros((P, C_END), np.float32)
    c[:, C_ID:C_ID + P] = np.eye(P)
    c[:, C_TRI:C_TRI + P] = np.triu(np.ones((P, P)), 1)
    c[:, C_ONE:C_ONE + P] = 1.0
    c[:, C_IOTA:C_IOTA + NE] = np.arange(NE)
    c[:, C_TIE:C_TIE + NG] = NG - np.arange(NG)
    c[:, C_ECAND:C_ECAND + CAND] = np.arange(CAND) // TILES
    c[:, C_RCAND:C_RCAND + CAND] = np.arange(CAND) % TILES
    c[:, C_JOB] = np.arange(P) + 1
    pos = np.arange(SEQ)
    for width, cos_at, sin_at in ((ROPE, C_COSM, C_SINM), (DD, C_COSD, C_SIND)):
        axis = width // 2
        inv = (np.float32(ROPE_BASE) ** (-np.arange(0, axis, 2, dtype=np.float32) / np.float32(axis))).astype(np.float32)
        row = (pos // GRID_W).astype(np.float32)[:, None] * inv
        col = (pos % GRID_W).astype(np.float32)[:, None] * inv
        ang = np.concatenate([row, col], axis=1)
        for at, table in ((cos_at, np.cos(ang)), (sin_at, np.sin(ang))):
            for t in range(LTILES):
                c[:, at + t * axis:at + (t + 1) * axis] = table[t * P:(t + 1) * P]
    return c


V_ADAB, V_AG, V_FG, V_QG, V_KVG, V_SUB, V_END = 0, 48, 56, 64, 68, 70, 71
G_MQ, G_MK, G_DQ, G_DK, G_END = 0, 96, 192, 320, 448


def layer_chunks(l):
    if l == 0:
        order = [(0, f"ada{n}", n) for n in range(4)]
        order += [(0, "ckv", 0), (0, "ada4", 1), (0, "ada5", 2), (0, "cq", 3), (0, "ada6", 0), (0, "kd", 1), (0, "ada7", 2),
                  (0, "ada8", 3), (0, "qd", 0), (0, "ada9", 1), (0, "vd", 2), (0, "ada10", 3), (0, "uq", 0), (0, "ukv", 1),
                  (0, "om", 2), (0, "od", 3), (0, "g0", 0), (0, "g2", 1), (0, "ada11", 4)]
        order += [(1, f"ada{n}", 5 - n % 2) for n in range(4)]
        order += [(0, "g1", 0), (0, "g3", 1)]
        order += [(1, f"ada{n}", 5 - n % 2) for n in range(4, 11)]
        order += [(0, "out0", 2), (1, "ada11", 4), (0, "out1", 3), (0, "shg", 0), (0, "shu", 1), (0, "shd", 4)]
        return order
    return [(l, name, s) for name, s in (
        ("ckv", 0), ("cq", 1), ("kd", 2), ("qd", 3), ("vd", 0), ("uq", 1), ("ukv", 2), ("om", 3), ("od", 0), ("g0", 1), ("g2", 2),
        ("g1", 4), ("g3", 5), ("out0", 1), ("out1", 2), ("shg", 0), ("shu", 1), ("shd", 4))]


def mod_streams(l, n):
    return 2 if l < DEPTH - 1 or n < 4 else 1


ADA_PLAN = {"prep": ([(0, n) for n in range(4, 10)], 16, 6),
            "vd": ([(0, 10)], 1, 16),
            "merge": ([(0, 11)] + [(1, n) for n in range(12)], 16, 9)}


def ada_share(phase, step):
    chunks, steps, per = ADA_PLAN[phase]
    ops = [(l, n, k, s) for l, n in chunks for k in range(KD) for s in range(mod_streams(l, n))]
    assert len(ops) <= steps * per
    mine = ops[step * per:(step + 1) * per]
    return mine, [(l, n) for l, n, k, s in mine if k == KD - 1 and s == mod_streams(l, n) - 1]


def norm_tasks(l):
    nq = TILES if l < DEPTH - 1 else LTILES
    tasks = [("ckv", t, 0) for t in range(TILES)]
    tasks += [("cq", t, 0) for t in range(nq)]
    tasks += [("kd", t, 0) for t in range(TILES)]
    tasks += [("qd", t, 0) for t in range(nq)]
    late = [("uq", t, h) for t in range(nq) for h in range(2)]
    late += [("ukv", t, h) for t in range(TILES) for h in range(2)]
    return tasks, late


def attention_units(l):
    nq = TILES if l < DEPTH - 1 else LTILES
    return [u for t in range(nq) for u in [("m", t, h) for h in range(MH)] + [("d", t, h) for h in range(DH)]]


T_LAG = 3
A_TLAG = 3
A_VLAG = 5
NP = 5


SHARED = {"pe_small": "pe_start", "pe_adar": "pe_start", "act_c": "act_start", "act_lam": "act_start", "act_adar": "act_start",
          "dve_c": "dve_start", "dve_vec": "dve_start", "dve_lam": "dve_start",
          "pe_logit": "pe_route", "pe_htok": "pe_route", "pe_place": "pe_route", "pe_jobs": "pe_route",
          "dve_mask": "dve_route", "dve_plc": "dve_route", "dve_slot": "dve_route", "dve_jobcol": "dve_route",
          "pe_sh": "pe_shared", "pe_shd": "pe_shared"}


def keys_of(t):
    return (0, TILES) if t < LTILES else (LTILES, TILES - LTILES)


def build(nc, A, book):
    ctx = ExitStack()
    with ctx:
        place = {}

        def sb(name, shape, dt=F32):
            place[name] = (nc.sbuf_base + 31) // 32 * 32
            return ctx.enter_context(nc.sbuf_tensor(name, shape, dt))

        def rounded(name):
            n = {"HT": KD * NTOK, "OT": 8 * NTOK, "VS": TILES * D, "W": WSLOTS * CHUNK, "QT": CHUNK, "KTM": CHUNK}[name]
            return nc.alloc_sbuf_tensor_at(name + "_R", [P, n], F32R, offset=place[name])

        sems = {}

        def sem(name):
            if name not in sems:
                sems[name] = ctx.enter_context(nc.semaphore(name))
            return sems[name]

        counts, seen = {}, {}

        def sig(ins, name, key, n=1):
            counter = SHARED.get(name, name)
            counts[counter] = counts.get(counter, 0) + n
            book[name, key] = counts[counter]
            ins.then_inc(sem(counter), n)

        def after(eng, name, key):
            count = book.get((name, key), 1)
            counter = SHARED.get(name, name)
            if seen.get((id(eng), counter), 0) < count:
                seen[id(eng), counter] = count
                eng.wait_ge(sem(counter), count)

        def chained(eng, name, ins):
            sig(ins, name, counts.get(name, 0))
            after(eng, name, counts[name] - 1)

        X = sb("X", [P, TILES, D])
        HT = sb("HT", [P, KD, NTOK])
        QT = sb("QT", [P, MH, NTOK])
        KTM = sb("KTM", [P, MH, NTOK])
        QTD = sb("QTD", [P, DH, NTOK])
        KTD = sb("KTD", [P, DH, NTOK])
        VS = sb("VS", [P, 2, TILES, 512])
        OT = sb("OT", [P, 2, 4, NTOK])
        W = sb("W", [P, WSLOTS, CHUNK])
        STG = sb("STG", [P, 4096])
        CST = sb("CST", [P, C_END])
        GAIN = sb("GAIN", [P, DEPTH, G_END])
        VEC = sb("VEC", [P, DEPTH, V_END])
        CS = sb("CS", [P, 2 * KD])
        CT = sb("CT", [P, 2, 2 * KD])
        MODS = sb("MODS", [P, DEPTH, 48, 2])
        SCLS = sb("SCLS", [P, DEPTH, 2, KD, 2])
        NLAM = sb("NLAM", [P, DEPTH])
        LT = sb("LT", [P, 8])
        SUBG = sb("SUBG", [P, 1])
        RW = sb("RW", [P, KD, NE])
        RB = sb("RB", [P, NE])
        SSX = sb("SSX", [P, TILES])
        RX = sb("RX", [P, TILES])
        HALF = sb("HALF", [P, 16])
        SS = sb("SS", [P, 4, 16])
        RR = sb("RR", [P, 4, 16])
        KR = sb("KR", [P, TILES, ROPE])
        RT = sb("RT", [P, 4, 256])
        MX = sb("MX", [P, 8])
        MB = sb("MB", [P, 8])
        RSUM = sb("RSUM", [P, 8])
        RINV = sb("RINV", [P, 2, 8])
        RDIF = sb("RDIF", [P, 8])
        SSO = sb("SSO", [P, 4])
        RO = sb("RO", [P, 4])
        TAB = sb("TAB", [1, 72], I32)
        SLOT = sb("SLOT", [P, TILES, 2], U32)
        WTS = sb("WTS", [P, TILES, 2])

        SQ = [STG[:, 512 * i:512 * (i + 1)] for i in range(2)]
        TM = [STG[:, 1024 + 512 * i:1024 + 512 * (i + 1)] for i in range(4)]
        PB = [STG[:, 512 * i:512 * (i + 1)] for i in range(NP)]
        PTS = [STG[:, 2560 + 512 * i:2560 + 512 * (i + 1)] for i in range(2)]
        OTM = STG[:, 3584:4096]
        OWN = OT[:, :, :, :].rearrange("p a k n -> p (a k n)")
        CQT = OWN[:, 0:2048].rearrange("p (k n) -> p k n", k=4)
        CKT = OWN[:, 2048:3072].rearrange("p (k n) -> p k n", k=2)
        XN = QT[:, :, :].rearrange("p a n -> p (a n)").rearrange("p (t d) -> p t d", t=TILES)
        YT = QT
        GATE = QTD[:, :, :].rearrange("p a n -> p (a n)").rearrange("p (s d) -> p s d", s=2)
        HET = KTD
        YS = VS[:, :, :, :].rearrange("p a t n -> p (a t n)").rearrange("p (t d) -> p t d", t=TILES)
        ESLOT = [W[:, 2, :], W[:, 3, :], QT[:, :, :].rearrange("p a n -> p (a n)"),
                 W[:, 0, :], W[:, 1, :], KTM[:, :, :].rearrange("p a n -> p (a n)")]
        HE = [OWN[:, 1024 * i:1024 * (i + 1)] for i in range(2)]
        HR, OR, VR, WR, QR_, KR_ = (rounded(name) for name in ("HT", "OT", "VS", "W", "QT", "KTM"))
        HEXH = [OR[:, 2048 + 1024 * i:2048 + 1024 * (i + 1)] for i in range(2)]
        HEXL = [HR[:, 1024 * i:1024 * (i + 1)] for i in range(2)]
        HTXH, HTXL = (HR[:, 2048 + 512 * i:2048 + 512 * (i + 1)] for i in range(2))
        HIGH = [VR[:, 1024 * i:1024 * (i + 1)] for i in range(4)]
        ELOW = [WR[:, 2 * CHUNK:3 * CHUNK], WR[:, 3 * CHUNK:], QR_[:, :], WR[:, 0:CHUNK], WR[:, CHUNK:2 * CHUNK], KR_[:, :]]
        HID = [STG[:, 512 * i:512 * (i + 1)] for i in range(2)]
        THB = [STG[:, 1024 + 512 * i:1024 + 512 * (i + 1)] for i in range(2)]
        YB = [STG[:, 2048 + 1024 * i:2048 + 1024 * (i + 1)] for i in range(2)]
        HTOK = [OWN[:, 1024 * i:1024 * (i + 1)] for i in range(TILES)]
        KFLAT = KTM[:, :, :].rearrange("p a n -> p (a n)")
        YG = [[(OWN if i < 2 else KFLAT)[:, 1024 * (2 * (i % 2) + k):1024 * (2 * (i % 2) + k + 1)] for k in range(2)]
              for i in range(TILES)]
        DIAG = STG[:, 0:1024].rearrange("p (h n) -> p h n", h=2)
        MT = [[STG[:, 1024 * b + 512 * j:1024 * b + 512 * (j + 1)] for j in range(2)] for b in range(2)]
        MY = [[STG[:, 2048 + 1024 * b + 512 * j:2048 + 1024 * b + 512 * (j + 1)] for j in range(2)] for b in range(2)]
        STH = [STG[:, 2048 + 512 * i:2048 + 512 * (i + 1)] for i in range(2)]
        SVV = [STG[:, 3072 + 512 * i:3072 + 512 * (i + 1)] for i in range(2)]
        RTF = RT[:, :, :].rearrange("p a n -> p (a n)")
        ACC = [[STG[:, 3072 + 512 * i:3584 + 512 * i] for i in range(2)], [RTF[:, 512 * i:512 * (i + 1)] for i in range(2)]]
        AROW = [STG[0:2, 512 * i:512 * (i + 1)] for i in range(4)]
        ZERO = HT[:, 4:6, :].rearrange("p a n -> p (a n)")
        at = [0]

        def route(*shape, dt=None):
            n = int(np.prod(shape))
            v = STG[:, at[0]:at[0] + n]
            at[0] += n
            v = v.bitcast(dt) if dt is not None else v
            if len(shape) == 2:
                v = v.rearrange("p (a b) -> p a b", a=shape[0])
            return v

        AFF, SEL, TMPR = (route(TILES * NE) for _ in range(3))
        PAIR = route(TILES * NG * 6)
        GRP = route(3, TILES * NG)
        BEST = route(TILES, 8)
        BIDX = route(TILES, 8, dt=U32)
        FIDX = route(TILES, 2)
        HOT = [route(TILES, NE) for _ in range(2)]
        MSK = route(TILES, NE)
        CNT = route(3, NE)
        SLF = route(TILES, 2)
        CND = route(4, CAND)
        JOBC = route(4)
        TABI = route(1, dt=I32)[0:1, :]
        CONES = CST[:, C_ONE:C_ONE + CAND]
        assert at[0] <= 2048

        def MASK(t):
            return MSK[:, t, :]

        def tm_sem(kind, t):
            if kind in ("ckv", "cq") or t >= LTILES and kind != "ukv":
                return "dve_tm"
            return "pool_tm"

        def first_hidden(eng):
            eng.wait_ge(sem("pad_stored"), 16)
            after(eng, "dve_vec", DEPTH - 1)
            after(eng, "dve_lam", 0)

        ROW_LOADS = 6 * DEPTH
        LAMR = HT[:, 0:2, 0:256]
        VROW = HT[:, 2:4, 0:P]
        CROW = HT[0:2 * KD, 6, 0:P]

        PS = [ctx.enter_context(nc.psum_tensor(f"PS{i}", [P, 512], F32)) for i in range(8)]
        Hs = nc.dram_tensor("sorted_h", [SORTED + P, D], F32, kind="Internal").ap()
        Ys = nc.dram_tensor("sorted_y", [SORTED + P, D], F32, kind="Internal").ap()

        SLOTS = [W[:, i, :] for i in range(WSLOTS)] + [
            KTM[:, :, :].rearrange("p a n -> p (a n)"), VS[:, :, :, :].rearrange("p a t n -> p (a t n)")]
        ident = CST[:, C_ID:C_ID + P]
        ones = CST[:, C_ONE:C_ONE + P]

        bank_of, turn, holder = {}, [0, 0], {}

        def bank_open(pe, key, acc=False):
            b = 6 + turn[1] % 2 if acc else turn[0] % 6
            turn[acc] += 1
            if b in holder:
                after(pe, *book.get(("read", holder[b]), ("none", 0)))
            holder[b] = key
            book["bank", key] = b
            return PS[b]

        def bank_read(eng, key):
            after(eng, "pe_" + key[0], key)
            return PS[book.get(("bank", key), 0)]

        def last_read(key, name, event):
            book["read", key] = (name, event)

        def product(last, key):
            sig(last, "pe_" + key[0], key)

        ring, before, in_slot = {}, {}, {}
        for l in range(DEPTH):
            for cl, name, s in layer_chunks(l):
                was_in, old = in_slot.get(s, (None, None))
                before[cl, name] = (l, old if was_in == l else None)
                n = 1 + (ring[old][1] if old else 0)
                ring[cl, name] = (s, n)
                in_slot[s] = (l, (cl, name))

        def chunk(eng, l, name):
            s, n = ring[l, name]
            if seen.get((id(eng), s), 0) < n:
                seen[id(eng), s] = n
                eng.wait_ge(sem(f"w_loaded{s}"), 16 * n)
            return SLOTS[s]

        def chunk_free(eng, l, name):
            after(eng, *book.get(("chunk_done", (l, name)), ("none", 0)))

        def ada_buffer(l, n, s):
            i = s if mod_streams(l, n) == 2 else n % 2
            return ACC[(l, n) >= (0, 11)][i]

        def chunk_done(l, name, product_key):
            book["chunk_done", (l, name)] = ("pe_" + product_key[0], product_key)

        def nq_of(l):
            return TILES if l < DEPTH - 1 else LTILES

        def after_layer(eng, l, t):
            after(eng, *(("dve_x", (l, 1, t)) if t == nq_of(l) - 1 else ("pool_x", (l, t))))

        def streams(n):
            return [(0, 0, SEQ)] + ([(1, SEQ, CTX)] if n > SEQ else [])

        block = ctx.enter_context(nc.Block())

        @block.tensor
        def _(pe):
            mm, tp = nc.tensor.matmul, nc.tensor.transpose

            def small_vectors():
                pe.wait_ge(sem("const_loaded"), 16)
                pe.wait_ge(sem("c_loaded"), 32)
                product(tp(bank_open(pe, ("small", 0))[:, 0:2 * KD], CROW, ident[0:2 * KD, 0:2 * KD]), ("small", 0))

            def small_rows():
                pe.wait_ge(sem("rows_loaded"), 16 * ROW_LOADS)
                ps = bank_open(pe, ("small", 1))
                for l in range(DEPTH):
                    last = tp(ps[:, P * l:P * l + V_END], VROW[0:V_END, l, :], ident[0:V_END, 0:V_END])
                product(last, ("small", 1))

            def ada_first():
                for n in range(4):
                    key = ("adar", 0, n)
                    ps = bank_open(pe, key)
                    w = chunk(pe, 0, f"ada{n}").rearrange("p (k n) -> p k n", k=KD)
                    after(pe, "dve_c", 0)
                    for k in range(KD):
                        last = mm(ps[0:2, :], CS[:, k::KD], w[:, k, :], start=(k == 0), stop=(k == KD - 1))
                    product(last, key)
                    chunk_done(0, f"ada{n}", key)
                    if n == 0:
                        small_rows()
                for n in range(4):
                    after(pe, "act_adar", n)
                    key = ("ada", 0, n)
                    ps = bank_open(pe, key)
                    for c in range(4):
                        last = tp(ps[:, 2 * c:2 * c + 2], AROW[n][:, c * P:(c + 1) * P], ident[0:2, 0:2])
                    product(last, key)

            def ada_columns(phase, step):
                for l, n in ada_share(phase, step)[1]:
                    for s in range(mod_streams(l, n)):
                        after(pe, "dve_acc", (l, n, KD - 1, s))
                    key = ("ada", l, n)
                    ps = bank_open(pe, key)
                    for c in range(4):
                        for s in range(mod_streams(l, n)):
                            last = mm(ps[:, 2 * c + s:2 * c + s + 1], ada_buffer(l, n, s)[:, c * P:(c + 1) * P],
                                      ones[:, 0:1], start=True, stop=True)
                    product(last, key)

            def gate_rows(l, which):
                for s in range(2 if l < DEPTH - 1 else 1):
                    for h in range(2):
                        after(pe, "dve_diag", (l, which, s, h))
                        key = ("gate", l, which, s, h)
                        ps = bank_open(pe, key)
                        product(mm(ps[:, :], ones, DIAG[:, h, :], start=True, stop=True), key)

            def hidden_t(l, f):
                nt = TILES if f == 0 else nq_of(l)
                after(pe, "dve_xn", (l, f, nt - 1))
                for k in range(KD):
                    ps = bank_open(pe, ("hT", l, f, k))
                    for t in range(nt):
                        last = tp(ps[:, t * P:(t + 1) * P], XN[:, t, k * P:(k + 1) * P], ident)
                    product(last, ("hT", l, f, k))

            def project(l, kind, t, half):
                key = ("proj", l, kind, t, half)
                w = chunk(pe, l, kind)
                if kind == "ukv":
                    w = w[:, 0:2 * D].rearrange("p (k n) -> p k n", k=2)
                    src, n0, n, kk = CKT, 512 * half, 512, 2
                elif kind == "uq":
                    w = w[:, 0:4 * MH * HQ].rearrange("p (k n) -> p k n", k=4)
                    src, n0, n, kk = CQT, 384 * half, 384, 4
                elif kind == "ckv":
                    w = w[:, 0:KD * OFF_KD].rearrange("p (k n) -> p k n", k=KD)
                    src, n0, n, kk = HT, 0, OFF_KD, KD
                else:
                    w = w.rearrange("p (k n) -> p k n", k=KD)
                    src, n0, n, kk = HT, 0, 512, KD
                ps = bank_open(pe, key)
                for k in range(kk):
                    last = mm(ps[:, 0:n], src[:, k, t * P:(t + 1) * P], w[:, k, n0:n0 + n],
                              start=(k == 0), stop=(k == kk - 1))
                product(last, key)
                chunk_done(l, kind, key)

            def task_t(l, i, task):
                kind, t, half = task
                after(pe, tm_sem(kind, t), (l, i))
                ps = bank_open(pe, ("T", l, i))
                src = TM[i % 4]
                if kind in ("ukv", "uq"):
                    for h in range(4):
                        last = tp(ps[0:HQ, h * P:(h + 1) * P], src[:, h * HQ:(h + 1) * HQ], ident)
                else:
                    for b in range(2 if kind == "ckv" else 4):
                        last = tp(ps[:, b * P:(b + 1) * P], src[:, b * P:(b + 1) * P], ident)
                product(last, ("T", l, i))

            def prep(l):
                early, late = norm_tasks(l)
                tasks = early + late
                after(pe, "dve_hT", (l, 0, KD - 2))
                after(pe, "act_hT", (l, 0, KD - 1))
                done = 0
                for i, (kind, t, half) in enumerate(tasks):
                    if i == len(early):
                        for tt in range(TILES):
                            project(l, "vd", tt, 0)
                            if l == 0 and tt < 2:
                                ada_columns("prep", len(early) - 2 + tt)
                        if l == 0:
                            ada_columns("vd", 0)
                        while done < i:
                            task_t(l, done, tasks[done])
                            done += 1
                        after(pe, "act_T", (l, TILES + nq_of(l) - 1))
                    project(l, kind, t, half)
                    if l == 0 and 2 <= i < len(early):
                        ada_columns("prep", i - 2)
                    if i - T_LAG >= done:
                        task_t(l, done, tasks[done])
                        done += 1
                while done < len(tasks):
                    task_t(l, done, tasks[done])
                    done += 1

            def attention(l):
                units = attention_units(l)
                ntask = sum(map(len, norm_tasks(l)))
                after(pe, "act_T", (l, ntask - 1))
                after(pe, "act_vd", (l, TILES - 1))
                after(pe, "act_vm", (l, TILES - 1, 1))
                maps = 0

                def scores(u, kind, t, h):
                    k0, kn = keys_of(t)
                    for m in range(1 if kind == "m" else 2):
                        key = ("S", l, u, m)
                        ps = bank_open(pe, key)
                        if kind == "m":
                            last = mm(ps[:, 0:kn * P], QT[0:HQ, h, t * P:(t + 1) * P],
                                      KTM[0:HQ, h, k0 * P:(k0 + kn) * P], start=True, stop=True)
                        else:
                            last = mm(ps[:, 0:kn * P], QTD[64 * m:64 * m + 64, h, t * P:(t + 1) * P],
                                      KTD[64 * m:64 * m + 64, h, k0 * P:(k0 + kn) * P], start=True, stop=True)
                        product(last, key)

                def prob_t(u, kind, t, h):
                    k0, kn = keys_of(t)
                    after(pe, "act_p" if kind == "m" else "dve_a", (l, u))
                    key = ("PT", l, u)
                    ps = bank_open(pe, key)
                    src = PB[book.get(("pbuf", (l, u)), 0)]
                    for c in range(kn):
                        last = tp(ps[:, c * P:(c + 1) * P], src[:, c * P:(c + 1) * P], ident)
                    product(last, key)

                def values(u, kind, t, h):
                    k0, kn = keys_of(t)
                    key = ("O", l, kind, t)
                    if h == 0:
                        bank_open(pe, key, acc=True)
                    ps = PS[book["bank", key]]
                    after(pe, "act_pts" if u % 2 == 0 else "dve_pts", (l, u))
                    w = MV if kind == "m" else DV
                    for c in range(kn):
                        last = mm(ps[:, h * w:(h + 1) * w], PTS[u % 2][:, c * P:(c + 1) * P],
                                  VS[:, int(kind == "d"), k0 + c, h * w:(h + 1) * w], start=(c == 0), stop=(c == kn - 1))
                    done = h == (MH if kind == "m" else DH) - 1
                    product(last, key if done else ("O", l, u))
                    book["pv_done", (l, u)] = key if done else ("O", l, u)

                def out_t(kind, t):
                    after(pe, "dve_o" , (l, kind, t))
                    key = ("OT", l, kind, t)
                    ps = bank_open(pe, key)
                    for b in range(4):
                        last = tp(ps[:, b * P:(b + 1) * P], OTM[:, b * P:(b + 1) * P], ident)
                    product(last, key)

                waiting = []
                for i in range(len(units) + A_VLAG + 2):
                    if i < len(units):
                        scores(i, *units[i])
                    if 0 <= i - A_TLAG < len(units):
                        prob_t(i - A_TLAG, *units[i - A_TLAG])
                    if 0 <= i - A_VLAG < len(units):
                        kind, t, h = units[i - A_VLAG]
                        values(i - A_VLAG, kind, t, h)
                        if h == (MH if kind == "m" else DH) - 1:
                            waiting.append((i + 2, kind, t))
                    while waiting and waiting[0][0] <= i:
                        out_t(*waiting.pop(0)[1:])

            def merge(l):
                nt = nq_of(l)
                n = nt * P
                after(pe, "act_oT", (l, "d", nt - 1))
                om = chunk(pe, l, "om").rearrange("p (k n) -> p k n", k=4)
                od = chunk(pe, l, "od").rearrange("p (k n) -> p k n", k=4)
                for b in range(KD):
                    c = (b % 4) * P
                    g = [chunk(pe, l, f"g{b // 4}"), chunk(pe, l, f"g{2 + b // 4}")]
                    for j, (kk, w, src, c0) in enumerate((
                            (KD, g[0].rearrange("p (k n) -> p k n", k=KD), HT, c),
                            (KD, g[1].rearrange("p (k n) -> p k n", k=KD), HT, c),
                            (4, om, OT[:, 0], b * P), (4, od, OT[:, 1], b * P))):
                        key = ("mg", l, b, j)
                        ps = bank_open(pe, key)
                        for k in range(kk):
                            last = mm(ps[:, 0:n], w[:, k, c0:c0 + P], src[:, k, 0:n], start=(k == 0), stop=(k == kk - 1))
                        product(last, key)
                        chunk_done(l, (f"g{b // 4}", f"g{2 + b // 4}", "om", "od")[j], key)
                        if l == 0 and b and j < 2:
                            ada_columns("merge", 2 * (b - 1) + j)

            def out_proj(l):
                if l == 0:
                    ada_columns("merge", 14)
                after(pe, "pool_y", (l, KD - 1))
                for h in range(2):
                    w = chunk(pe, l, f"out{h}").rearrange("p (k n) -> p k n", k=KD)
                    for t in range(nq_of(l)):
                        key = ("out", l, h, t)
                        ps = bank_open(pe, key)
                        for k in range(KD):
                            last = mm(ps[:, :], YT[:, k, t * P:(t + 1) * P], w[:, k, :], start=(k == 0), stop=(k == KD - 1))
                        product(last, key)
                        chunk_done(l, f"out{h}", key)
                        if l == 0 and h == 0 and t == 1:
                            ada_columns("merge", 15)

            def router(l):
                after(pe, "dve_hT", (l, 1, KD - 2))
                after(pe, "act_hT", (l, 1, KD - 1))
                key = ("logit", l)
                pe.wait_ge(sem("router_loaded"), 32)
                ps = bank_open(pe, key)
                for t in range(nq_of(l)):
                    for k in range(KD):
                        last = mm(ps[:, NE * t:NE * (t + 1)], HT[:, k, t * P:(t + 1) * P], RW[:, k, :],
                                  start=(k == 0), stop=(k == KD - 1))
                product(last, key)
                for t in range(nq_of(l)):
                    for h in range(2):
                        key = ("htok", l, t, h)
                        ps = bank_open(pe, key)
                        for b in range(4):
                            last = tp(ps[:, b * P:(b + 1) * P], HT[:, 4 * h + b, t * P:(t + 1) * P], ident)
                        product(last, key)

            def places(l):
                nt = nq_of(l)
                after(pe, "dve_mask", l)
                key = ("place", l)
                ps = bank_open(pe, key)
                for t in range(nt):
                    for s in range(t + 1):
                        mm(ps[:, NE * t:NE * (t + 1)], CST[:, C_TRI:C_TRI + P] if s == t else ones,
                           MASK(s), start=(s == 0), stop=(s == t))
                for s in range(nt):
                    last = mm(ps[:, 64:64 + NE], ones, MASK(s), start=(s == 0), stop=(s == nt - 1))
                product(last, key)

            def job_rows(l):
                after(pe, "dve_jobcol", l)
                key = ("jobs", l)
                ps = bank_open(pe, key)
                for j in range(2):
                    last = mm(ps[0:1, j * P:(j + 1) * P], JOBC[:, j:j + 1], ident, start=True, stop=True)
                product(last, key)

            def shared(l):
                nt = nq_of(l)
                n = nt * P
                w = [chunk(pe, l, x).rearrange("p (k n) -> p k n", k=KD) for x in ("shg", "shu")]
                for f in range(KF):
                    for j in range(2):
                        key = ("sh", l, f, j)
                        ps = bank_open(pe, key)
                        for k in range(KD):
                            last = mm(ps[:, 0:n], w[j][:, k, f * P:(f + 1) * P], HT[:, k, 0:n], start=(k == 0), stop=(k == KD - 1))
                        product(last, key)
                        chunk_done(l, ("shg", "shu")[j], key)
                    if f == 0:
                        places(l)
                    if f == 1:
                        job_rows(l)
                gate_rows(l, 1)
                w = chunk(pe, l, "shd").rearrange("p (k n) -> p k n", k=KF)
                after(pe, "dve_sh", (l, KF - 1))
                for t in range(nt):
                    for h in range(2):
                        key = ("shd", l, t, h)
                        ps = bank_open(pe, key)
                        for k in range(KF):
                            last = mm(ps[:, :], HET[:, k, t * P:(t + 1) * P], w[:, k, 512 * h:512 * (h + 1)],
                                      start=(k == 0), stop=(k == KF - 1))
                        product(last, key)
                        chunk_done(l, "shd", key)

            def experts(l):
                e = lambda name: sem(f"{name}{l}")
                for b in range(8):
                    after(pe, *book.get(("read", holder[b]), ("none", 0)))
                pe.wait_ge(e("tab_ready"), 1)
                before_last = pe.value_load(TAB[0:1, 65:66], min_val=1, max_val=TURNS - 1)

                def rows(j):
                    for h in range(2):
                        for b in range(4):
                            last = tp(PS[h][:, b * P:(b + 1) * P], HE[j][:, (4 * h + b) * P:(4 * h + b + 1) * P], ident)
                    last.then_inc(e("e_in_done"), 1)

                def weights_times(x, j, low, pool_low):
                    for p in range(4):
                        if p < 3:
                            pe.wait_ge(e("e_low"), low(p))
                        else:
                            pe.wait_ge(e("e_plow"), pool_low)
                        wh = HIGH[p]
                        wl = ELOW[3 * j + x][:, 1024 * p:1024 * (p + 1)]
                        xh, xl = (HEXH[j], HEXL[j]) if x < 2 else (HTXH, HTXL)
                        for c in range(2):
                            k = 2 * p + c if x < 2 else p
                            ps = (PS[2 if j == 0 else 7], PS[3], PS[5 + c])[x]
                            first, final = (k == 0, k == KD - 1) if x < 2 else (k == 0, k == KF - 1)
                            xs = slice(k * P, (k + 1) * P)
                            ws = slice(512 * c, 512 * (c + 1))
                            mm(ps[:, :], xh[:, xs], wh[:, ws], start=first, stop=False)
                            mm(ps[:, :], xh[:, xs], wl[:, ws], start=False, stop=False)
                            last = mm(ps[:, :], xl[:, xs], wh[:, ws], start=False, stop=final)
                        last.then_inc(e("e_piece"), 1)

                pe.wait_ge(e("he_loaded0"), 16)
                rows(0)
                pe.wait_ge(e("he_loaded1"), 16)
                pe.wait_ge(e("e_hexl"), 2)
                rows(1)
                weights_times(0, 0, lambda p: p + 1, 1)
                pe.wait_ge(e("e_hexl"), 4)

                def turn(i, more):
                    i9, i3, i6 = pe.snap(18 * i), pe.snap(2 * i), pe.snap(6 * i)
                    for j in range(2):
                        weights_times(1, j, lambda p: i9 + (9 * j + 4 + p), i6 + (3 * j + 2))
                        if more or j == 0:
                            weights_times(0, 1 - j, lambda p: i9 + (9 * j + 7 + p), i6 + (3 * j + 3))
                        pe.wait_ge(e("e_hid_done"), i3 + (j + 1))
                        for b in range(KF):
                            last = tp(PS[4][:, b * P:(b + 1) * P], HID[j][:, b * P:(b + 1) * P], ident)
                        last.then_inc(e("e_ht_done"), 1)
                        if more:
                            pe.wait_ge(e(f"he_loaded{j}"), 16 * i + 32)
                            pe.wait_ge(e("e_hexl"), 4 * i + (2 * j + 4))
                            rows(j)
                        pe.wait_ge(e("e_htxl"), i3 + (j + 1))
                        pe.wait_ge(e("e_y"), 4 * i + (2 * j + 2))
                        weights_times(2, j, lambda p: i9 + (9 * j + (10 if more or j == 0 else 7) + p),
                                      i6 + (3 * j + (4 if more or j == 0 else 3)))
                        if more:
                            pe.wait_ge(e("e_hexl"), 4 * i + (2 * j + 6))

                with pe.Fori(0, before_last) as i:
                    turn(i, True)
                turn(before_last, False)
                pe.wait_ge(e("e_y"), 4 * before_last + 6)
                holder.clear()

            small_vectors()
            ada_first()
            for l in range(DEPTH):
                hidden_t(l, 0)
                prep(l)
                attention(l)
                gate_rows(l, 0)
                merge(l)
                out_proj(l)
                hidden_t(l, 1)
                router(l)
                shared(l)
                experts(l)

        @block.sync
        def _(sp):
            def small_loads():
                sp.dma_start(CROW[0:KD, :], A["c"].rearrange("o (k p) -> (o k) p", p=P)).then_inc(sem("c_loaded"), 16)
                sp.dma_start(CROW[KD:2 * KD, :], A["c_ctx"].rearrange("(k p) -> k p", p=P)).then_inc(sem("c_loaded"), 16)
                sp.dma_start(CST[:, :], A["consts"]).then_inc(sem("const_loaded"), 16)

            def vector_loads():
                for l in range(DEPTH):
                    for name, at, end in (("ada_b", V_ADAB, V_AG), ("attn_norm_g", V_AG, V_FG), ("ffn_norm_g", V_FG, V_QG),
                                          ("mla_q_norm_g", V_QG, V_KVG), ("mla_kv_norm_g", V_KVG, V_SUB), ("diff_sub_g", V_SUB, V_END)):
                        sp.dma_start(VROW[at:end, l, :], A[name][l, :].rearrange("(k p) -> k p", p=P)).then_inc(sem("rows_loaded"), 16)

            def token_loads():
                for t in range(TILES):
                    src = A["x"][0, t * P:(t + 1) * P, :] if t < LTILES else A["ctx"][0, (t - LTILES) * P:(t - LTILES + 1) * P, :]
                    sp.dma_start(X[:, t, :], src).then_inc(sem(f"x_loaded{t}"), 16)

            def source(l, name):
                w_in = A["w_in"][l].rearrange("(k p) n -> p k n", p=P)
                if name.startswith("ada"):
                    n = int(name[3:])
                    return A["ada_w"][l].rearrange("(k p) n -> p k n", p=P)[:, :, 512 * n:512 * (n + 1)], KD
                cols = {"ckv": (0, OFF_KD), "kd": (OFF_KD, OFF_VD), "vd": (OFF_VD, OFF_CQ), "cq": (OFF_CQ, OFF_QD), "qd": (OFF_QD, OFF_GATE)}
                if name in cols:
                    return w_in[:, :, cols[name][0]:cols[name][1]], KD
                if name[0] == "g":
                    c = OFF_GATE + 512 * int(name[1])
                    return w_in[:, :, c:c + 512], KD
                if name[:3] == "out":
                    c = 512 * int(name[3])
                    return A["w_out"][l].rearrange("(k p) n -> p k n", p=P)[:, :, c:c + 512], KD
                tensor, k = {"ukv": ("mla_w_ukv", 2), "uq": ("mla_w_uq", 4), "om": ("w_o_mla", 4), "od": ("w_o_diff", 4),
                             "shg": ("sh_w_gate", KD), "shu": ("sh_w_up", KD), "shd": ("sh_w_down", KF)}[name]
                return A[tensor][l].rearrange("(k p) n -> p k n", p=P), k

            def load(l, name):
                s, n = ring[l, name]
                now, old = before[l, name]
                if now and name == "ckv":
                    for t in range(TILES):
                        sp.wait_ge(sem(f"y_gathered{t}"), 32)
                if old is not None:
                    chunk_free(sp, *old)
                elif s >= WSLOTS:
                    after(sp, "pe_O", ("O", now, "d", nq_of(now) - 1))
                src, k = source(l, name)
                width = src.shape[2]
                dst = SLOTS[s][:, 0:k * width].rearrange("p (k n) -> p k n", k=k)
                sp.dma_start(dst, src).then_inc(sem(f"w_loaded{s}"), 16)

            expert_w = [A["moe_w_gate"].rearrange("l e (k p) n -> (l e) p k n", p=P),
                        A["moe_w_up"].rearrange("l e (k p) n -> (l e) p k n", p=P),
                        A["moe_w_down"].rearrange("l e (k p) n -> (l e) p k n", p=P)]

            def experts(l):
                e = lambda name: sem(f"{name}{l}")
                nq = nq_of(l)
                sp.wait_ge(e("tab_ready"), 1)
                before_last = sp.value_load(TAB[0:1, 65:66], min_val=1, max_val=TURNS - 1)

                def rows(j, n):
                    r = sp.value_load(TAB[0:1, 32 + n:33 + n] if isinstance(n, int) else TAB[0:1, bass.ds(n + 32, 1)], min_val=0, max_val=SORTED)
                    return r

                def weights(j, n):
                    ex = sp.value_load(TAB[0:1, n:n + 1] if isinstance(n, int) else TAB[0:1, bass.ds(n, 1)], min_val=0, max_val=NE - 1)
                    return ex + NE * l

                def load_w(ex, j, x):
                    k = KF if x == 2 else KD
                    sp.dma_start(ESLOT[3 * j + x].rearrange("p (k n) -> p k n", k=k),
                                 expert_w[x][bass.ds(ex, 1)].rearrange("o p k n -> p (o k) n")).then_inc(e(f"ew_loaded{3 * j + x}_"), 16)

                def load_rows(j, n):
                    r = rows(j, n)
                    sp.dma_start(HE[j][0:ROWS[l], :], Hs[bass.ds(r, ROWS[l]), :]).then_inc(e(f"he_loaded{j}"), 16)

                for s in (2, 3):
                    chunk_free(sp, *last_in_slot[l, s])
                after(sp, "pe_hT", ("hT", l, 1, KD - 1))
                ex = [sp.snap(weights(j, j)) for j in range(2)]
                load_w(ex[0], 0, 0)
                load_w(ex[0], 0, 1)
                load_w(ex[0], 0, 2)
                sp.wait_ge(e("sorted_stored"), 2 * 16 * nq)
                if l == 0:
                    sp.wait_ge(sem("pad_stored"), 16)
                load_rows(0, 0)
                load_rows(1, 1)
                for x, s in enumerate((0, 1, 4)):
                    chunk_free(sp, *last_in_slot[l, s])
                    load_w(ex[1], 1, x)
                for j in range(2):
                    sp.nop().then_inc(e(f"y_stored{j}_"), 16)
                sp.nop().then_inc(e("e_y"), 2)
                for n in range(2):
                    sp.wait_ge(e("e_in_done"), n + 1)
                    load_rows(n, n + 2)

                def turn_of(i, more):
                    for j in range(2):
                        here = sp.snap(rows(j, 2 * i + j))
                        if more:
                            ex = sp.snap(weights(j, 2 * i + (2 + j)))
                            r = sp.snap(rows(j, 2 * i + (4 + j)))
                            sp.wait_ge(e("e_piece"), 24 * i + (12 * j + 4))
                            load_w(ex, j, 0)
                            sp.wait_ge(e("e_piece"), 24 * i + (12 * j + 8))
                            load_w(ex, j, 1)
                            sp.wait_ge(e("e_in_done"), 2 * i + (j + 3))
                            sp.dma_start(HE[j][0:ROWS[l], :], Hs[bass.ds(r, ROWS[l]), :]).then_inc(e(f"he_loaded{j}"), 16)
                            sp.wait_ge(e("e_piece"), 24 * i + (12 * j + 16))
                            load_w(ex, j, 2)
                        sp.wait_ge(e("e_y"), 4 * i + (2 * j + 4))
                        sp.dma_start(Ys[bass.ds(here, ROWS[l]), :], YB[j][0:ROWS[l], :]).then_inc(e(f"y_stored{j}_"), 16)
                with sp.Fori(0, before_last) as i:
                    turn_of(i, True)
                turn_of(before_last, False)
                for j in range(2):
                    sp.wait_ge(e(f"he_loaded{j}"), 16 * before_last + 32)
                sp.wait_ge(e("y_stored1_"), 16 * before_last + 32)
                sp.nop().then_inc(e("experts_over"), 1)

            last_in_slot = {}
            for l in range(DEPTH):
                for cl, name, s in layer_chunks(l):
                    last_in_slot[l, s] = (cl, name)
            small_loads()
            for l in range(DEPTH):
                for cl, name, s in layer_chunks(l):
                    load(cl, name)
                    if (cl, name) == (0, "ada0"):
                        vector_loads()
                    if (cl, name) == (0, "ada3"):
                        token_loads()
                experts(l)
            for t in range(LTILES):
                after_layer(sp, DEPTH - 1, t)
                sp.dma_start(A["out"][0, t * P:(t + 1) * P, :], X[:, t, :]).then_inc(sem("out_stored"), 16)
            sp.wait_ge(sem("out_stored"), 16 * LTILES)

        @block.scalar
        def _(act):
            fn = nc.scalar.activation

            def start():
                for l in range(DEPTH):
                    for name, at in (("mla_q_g", G_MQ), ("mla_k_g", G_MK), ("diff_q_g", G_DQ), ("diff_k_g", G_DK)):
                        g = A[name][l]
                        g = g.rearrange("m d -> (m d)") if len(g.shape) == 2 else g
                        n = g.shape[0]
                        act.dma_start(GAIN[:, l, at:at + n], g.rearrange("(o n) -> o n", o=1).to_broadcast([P, n])).then_inc(sem("gain_loaded"), 16)
                    act.dma_start(LAMR[:, l, :], A["diff_lam"][l].rearrange("m d -> (m d)").rearrange("(o n) -> o n", o=1)
                                  .to_broadcast([P, 4 * DD])).then_inc(sem("lam_loaded"), 16)
                act.dma_start(RB[:, :], A["router_b"].rearrange("(o n) -> o n", o=1).to_broadcast([P, NE])).then_inc(sem("router_loaded"), 16)
                act.dma_start(RW[:, :, :], A["router_w"].rearrange("(k p) n -> p k n", p=P)).then_inc(sem("router_loaded"), 16)
                ps = bank_read(act, ("small", 0))
                sig(fn(CT[:, 0, :], ps[:, 0:2 * KD], ACT.Exp, scale=-1.0), "act_c", 0)
                after(act, "dve_lam", 0)
                sig(fn(LT[:, 4:8], LT[:, 0:4], ACT.Exp), "act_lam", 0)

            def ada_rows():
                for n in range(4):
                    key = ("adar", 0, n)
                    ps = bank_read(act, key)
                    sig(fn(AROW[n], ps[0:2, :], ACT.Copy), "act_adar", n)
                    last_read(key, "act_adar", n)

            def norm(l, f):
                nt = TILES if f == 0 else nq_of(l)
                for t in range(nt):
                    if f == 1:
                        after(act, "dve_x", (l, 0, 1, t))
                        out = OWN[:, 1024 * t:1024 * (t + 1)]
                    else:
                        if l == 0:
                            act.wait_ge(sem(f"x_loaded{t}"), 16)
                        else:
                            after_layer(act, l - 1, t)
                        out = XN[:, t, :]
                    sig(fn(out, X[:, t, :], ACT.Square, accum_out=SSX[:, t:t + 1]), "act_ssx", (l, f, t))
                if (l, f) == (0, 0):
                    ada_rows()
                after(act, "dve_scl", (l, f))
                for k in range(1, KD, 2):
                    ps = bank_read(act, ("hT", l, f, k))
                    if (l, f, k) == (0, 0, 1):
                        first_hidden(act)
                    for s, c0, cn in streams(nt * P):
                        ins = fn(HT[:, k, c0:c0 + cn], ps[:, c0:c0 + cn], ACT.Identity,
                                 bias=MODS[:, l, 24 * f + k, s:s + 1], scale=SCLS[:, l, f, k, s:s + 1])
                        last = s == streams(nt * P)[-1][0]
                        sig(ins, "act_hT", (l, f, k) if last else (l, f, k, s))
                    last_read(("hT", l, f, k), "act_hT", (l, f, k))

            def prep(l):
                early, late = norm_tasks(l)
                tasks = early + late
                done = 0

                def evac_t(i, task):
                    kind, t, half = task
                    ps = bank_read(act, ("T", l, i))
                    if kind in ("ckv", "cq"):
                        n, dst, v = (2, CKT, V_KVG) if kind == "ckv" else (4, CQT, V_QG)
                        for b in range(n):
                            sig(fn(dst[:, b, t * P:(t + 1) * P], ps[:, b * P:(b + 1) * P], ACT.Copy, scale=VEC[:, l, v + b:v + b + 1]),
                                "act_T", (l, i) if b == n - 1 else (l, i, b))
                    elif kind in ("ukv", "uq"):
                        dst = KTM if kind == "ukv" else QT
                        sig(fn(dst[0:HQ, 4 * half:4 * half + 4, t * P:(t + 1) * P],
                               ps[0:HQ, :].rearrange("p (h n) -> p h n", h=4), ACT.Copy), "act_T", (l, i))
                    else:
                        dst = KTD if kind == "kd" else QTD
                        sig(fn(dst[:, :, t * P:(t + 1) * P], ps[:, :].rearrange("p (h n) -> p h n", h=4), ACT.Copy), "act_T", (l, i))
                    last_read(("T", l, i), "act_T", (l, i))

                for i, (kind, t, half) in enumerate(tasks):
                    if i == len(early):
                        for tt in range(TILES):
                            key = ("proj", l, "vd", tt, 0)
                            ps = bank_read(act, key)
                            sig(fn(VS[:, 1, tt, :], ps[:, :], ACT.Copy), "act_vd", (l, tt))
                            last_read(key, "act_vd", (l, tt))
                        while done < i:
                            evac_t(done, tasks[done])
                            done += 1
                    ps = bank_read(act, ("proj", l, kind, t, half))
                    if kind == "ukv":
                        sig(fn(VS[:, 0, t, 256 * half:256 * (half + 1)].rearrange("p (h d) -> p h d", h=4),
                               ps[:, :].rearrange("p (h d) -> p h d", h=4)[:, :, NOPE:NOPE + MV], ACT.Copy), "act_vm", (l, t, half))
                    if i >= 2:
                        after(act, "dve_ss", (l, i - 2))
                    n = {"ckv": OFF_KD, "uq": 384}.get(kind, 512)
                    sig(fn(SQ[i % 2][:, 0:n], ps[:, 0:n], ACT.Square), "act_sq", (l, i))
                    if i - T_LAG >= done:
                        evac_t(done, tasks[done])
                        done += 1
                while done < len(tasks):
                    evac_t(done, tasks[done])
                    done += 1

            def gate_rows(l, which):
                for s in range(2 if l < DEPTH - 1 else 1):
                    for h in range(2):
                        key = ("gate", l, which, s, h)
                        ps = bank_read(act, key)
                        sig(fn(GATE[:, s, 512 * h:512 * (h + 1)], ps[:, :], ACT.Copy, scale=0.5 if which == 0 else 1.0),
                            "act_gate", (l, which, s, h))
                        last_read(key, "act_gate", (l, which, s, h))

            def attention(l):
                units = attention_units(l)
                nbuf, owner = [0], {}

                def probabilities(u, kind, t, h):
                    k0, kn = keys_of(t)
                    for m in range(1 if kind == "m" else 2):
                        b = nbuf[0] % NP
                        nbuf[0] += 1
                        if b in owner:
                            after(act, "pe_PT", ("PT", l, owner[b]))
                        owner[b] = u
                        book["pbuf" if m == 0 else "pbuf1", (l, u)] = b
                        c = (2 * u + m) % 8
                        after(act, "dve_mx", (l, u, m))
                        ps = bank_read(act, ("S", l, u, m))
                        name, key = ("act_p", (l, u)) if kind == "m" else ("act_pd", (l, u, m))
                        sig(fn(PB[b][:, 0:kn * P], ps[:, 0:kn * P], ACT.Exp, bias=MB[:, c:c + 1],
                               scale=MLA_SCALE if kind == "m" else DIFF_SCALE, accum_out=RSUM[:, c:c + 1]), name, key)
                        last_read(("S", l, u, m), name, key)

                def transposed(u, kind, t, h):
                    if u % 2:
                        return
                    k0, kn = keys_of(t)
                    if u >= 2:
                        key = book.get(("pv_done", (l, u - 2)), ("none", 0))
                        after(act, "pe_O", key)
                    ps = bank_read(act, ("PT", l, u))
                    sig(fn(PTS[0][:, 0:kn * P], ps[:, 0:kn * P], ACT.Copy), "act_pts", (l, u))
                    last_read(("PT", l, u), "act_pts", (l, u))

                def out_t(kind, t):
                    key = ("OT", l, kind, t)
                    ps = bank_read(act, key)
                    scale = 1.0 if kind == "m" else SUBG[:, 0:1]
                    sig(fn(OT[:, int(kind == "d"), :, t * P:(t + 1) * P], ps[:, :].rearrange("p (b n) -> p b n", b=4), ACT.Copy, scale=scale),
                        "act_oT", (l, kind, t))
                    last_read(key, "act_oT", (l, kind, t))

                after(act, "dve_subg", l)
                waiting = []
                for i in range(len(units) + A_VLAG + 2):
                    if i < len(units):
                        probabilities(i, *units[i])
                    if 0 <= i - A_TLAG < len(units):
                        transposed(i - A_TLAG, *units[i - A_TLAG])
                    if 0 <= i - A_VLAG < len(units):
                        kind, t, h = units[i - A_VLAG]
                        if h == (MH if kind == "m" else DH) - 1:
                            if kind == "d":
                                ps = bank_read(act, ("O", l, "d", t))
                                sig(fn(RTF[:, 0:512], ps[:, :], ACT.Square), "act_osq", (l, t))
                            waiting.append((i + 2, kind, t))
                    while waiting and waiting[0][0] <= i:
                        out_t(*waiting.pop(0)[1:])

            def merge(l):
                n = nq_of(l) * P
                for b in range(KD):
                    for j in range(2):
                        if b >= 2:
                            after(act, "dve_mg", (l, b - 2, j))
                        ps = bank_read(act, ("mg", l, b, j))
                        sig(fn(MT[b % 2][j][:, 0:n], ps[:, 0:n], ACT.Tanh, scale=0.5), "act_mg", (l, b, j))
                        last_read(("mg", l, b, j), "act_mg", (l, b, j))

            def router(l):
                nt = nq_of(l)
                ps = bank_read(act, ("logit", l))
                sig(fn(AFF[:, 0:nt * NE], ps[:, 0:nt * NE], ACT.Exp, scale=-1.0), "act_rt", l)
                last_read(("logit", l), "act_rt", l)
                for t in range(nt):
                    for h in range(2):
                        key = ("htok", l, t, h)
                        ps = bank_read(act, key)
                        sig(fn(HTOK[t][:, 512 * h:512 * (h + 1)], ps[:, :], ACT.Copy), "act_htok", (l, t, h))
                        last_read(key, "act_htok", (l, t, h))

            def shared(l):
                nt = nq_of(l)
                for f in range(KF):
                    if f >= 2:
                        after(act, "dve_sh", (l, f - 2))
                    ps = bank_read(act, ("sh", l, f, 0))
                    sig(fn(STH[f % 2][:, 0:nt * P], ps[:, 0:nt * P], ACT.Tanh, scale=0.5), "act_sh", (l, f))
                gate_rows(l, 1)
                chunk_free(act, *((1, "ada10") if l == 0 else (l, "g3")))
                for t in range(nt):
                    for h in range(2):
                        key = ("shd", l, t, h)
                        ps = bank_read(act, key)
                        sig(fn(YS[:, t, 512 * h:512 * (h + 1)], ps[:, :], ACT.Copy), "act_ys", (l, t, h))
                        last_read(key, "act_ys", (l, t, h))

            def experts(l):
                e = lambda name: sem(f"{name}{l}")
                act.wait_ge(e("tab_ready"), 1)
                before_last = act.value_load(TAB[0:1, 65:66], min_val=1, max_val=TURNS - 1)

                def high(x, j, p):
                    fn(HIGH[p], ESLOT[3 * j + x][:, 1024 * p:1024 * (p + 1)], ACT.Copy).then_inc(e("e_high"), 1)

                def rows(j):
                    for h in range(2):
                        fn(HEXH[j][:, 512 * h:512 * (h + 1)], PS[h][:, :], ACT.Copy).then_inc(e("e_hexh"), 1)

                after(act, "dve_ysx", (l, nq_of(l) - 1))
                act.wait_ge(e("ew_loaded0_"), 16)
                high(0, 0, 0)
                act.wait_ge(e("e_in_done"), 1)
                rows(0)
                for p in range(1, 4):
                    high(0, 0, p)
                act.wait_ge(e("e_in_done"), 2)
                rows(1)
                act.wait_ge(e("ew_loaded1_"), 16)
                for p in range(4):
                    act.wait_ge(e("e_piece"), p + 1)
                    high(1, 0, p)

                def turn(i, more):
                    i24 = act.snap(24 * i)
                    for j in range(2):
                        final = not more and j == 1
                        act.wait_ge(e("e_piece"), i24 + (12 * j + 4))
                        fn(THB[j], PS[2 if j == 0 else 7][:, :], ACT.Tanh, scale=0.5).then_inc(e("e_th"), 1)
                        used = 12 * j + 5
                        if not final:
                            act.wait_ge(e(f"ew_loaded{3 * (1 - j)}_"), 16 * i + 16 * (j + 1))
                            for p in range(4):
                                act.wait_ge(e("e_piece"), i24 + (used + p))
                                high(0, 1 - j, p)
                            used += 4
                        act.wait_ge(e(f"ew_loaded{3 * j + 2}_"), 16 * i + 16)
                        for p in range(4):
                            act.wait_ge(e("e_piece"), i24 + (used + p))
                            high(2, j, p)
                        used += 4
                        act.wait_ge(e("e_ht_done"), 2 * i + (j + 1))
                        fn(HTXH, PS[4][:, :], ACT.Copy).then_inc(e("e_htxh"), 1)
                        if more:
                            act.wait_ge(e("e_in_done"), 2 * i + (j + 3))
                            rows(j)
                        if not final:
                            act.wait_ge(e(f"ew_loaded{3 * (1 - j) + 1}_"), 16 * i + 16 * (j + 1))
                            for p in range(4):
                                act.wait_ge(e("e_piece"), i24 + (used + p))
                                high(1, 1 - j, p)
                        if j == 1:
                            act.wait_ge(e("y_stored0_"), 16 * i + 32)
                        else:
                            act.wait_ge(e("y_stored1_"), 16 * i + 16)
                        act.wait_ge(e("e_piece"), i24 + (used + 3))
                        for h in range(2):
                            fn(YB[j][:, 512 * h:512 * (h + 1)], PS[5 + h][:, :], ACT.Copy).then_inc(e("e_y"), 1)

                with act.Fori(0, before_last) as i:
                    turn(i, True)
                turn(before_last, False)

            def combine(l):
                for t in range(nq_of(l)):
                    act.wait_ge(sem(f"y_gathered{t}"), 32 * (l + 1))
                    sig(fn(YG[t][0], YG[t][0], ACT.Copy, scale=WTS[:, t, 0:1]), "act_yw", (l, t))

            start()
            for l in range(DEPTH):
                norm(l, 0)
                prep(l)
                attention(l)
                gate_rows(l, 0)
                merge(l)
                norm(l, 1)
                router(l)
                shared(l)
                experts(l)
                combine(l)

        @block.vector
        def _(dve):
            tt, ts, stt = nc.vector.tensor_tensor, nc.vector.tensor_scalar, nc.vector.scalar_tensor_tensor
            red, cp, rec = nc.vector.tensor_reduce, nc.vector.tensor_copy, nc.vector.reciprocal

            def link(ins):
                chained(dve, "dve_step", ins)

            def start():
                after(dve, "act_c", 0)
                ps = bank_read(dve, ("small", 0))
                link(ts(CT[:, 1, :], CT[:, 0, :], 1.0, None, ALU.add))
                link(rec(CT[:, 0, :], CT[:, 1, :]))
                sig(tt(CS[:, :], CT[:, 0, :], ps[:, 0:2 * KD], ALU.mult), "dve_c", 0)
                last_read(("small", 0), "dve_c", 0)
                dve.wait_ge(sem("lam_loaded"), 16 * DEPTH)
                r = LAMR.rearrange("p l (a b d) -> p l a b d", a=2, b=2)
                prod = RTF[:, 0:DEPTH * 2 * DD].rearrange("p (l a d) -> p l a d", l=DEPTH, a=2)
                for l in range(DEPTH):
                    link(tt(prod[:, l], r[:, l, :, 0], r[:, l, :, 1], ALU.mult))
                sig(red(LT[:, 0:4], RTF[:, 0:256].rearrange("p (a d) -> p a d", a=4), AX.X, ALU.add), "dve_lam", 0)
                after(dve, "act_lam", 0)
                for l in range(DEPTH):
                    lam_init = 0.8 - 0.6 * math.exp(-0.3 * l)
                    link(tt(NLAM[:, l:l + 1], LT[:, 5 + 2 * l:6 + 2 * l], LT[:, 4 + 2 * l:5 + 2 * l], ALU.subtract))
                    link(ts(NLAM[:, l:l + 1], NLAM[:, l:l + 1], -lam_init, None, ALU.add))
                ps = bank_read(dve, ("small", 1))
                for l in range(DEPTH):
                    sig(cp(VEC[:, l, :], ps[:, P * l:P * l + V_END]), "dve_vec", l)
                last_read(("small", 1), "dve_vec", DEPTH - 1)
                after(dve, "dve_vec", DEPTH - 1)
                for n in range(4):
                    ada_bias(0, n)

            def ada_bias(l, n):
                ns = mod_streams(l, n)
                key = ("ada", l, n)
                ps = bank_read(dve, key)
                b = VEC[:, l, V_ADAB + 4 * n:V_ADAB + 4 * n + 4].rearrange("p (m o) -> p m o", o=1).to_broadcast([P, 4, ns])
                sig(tt(MODS[:, l, 4 * n:4 * n + 4, 0:ns], ps[:, 0:8].rearrange("p (m s) -> p m s", s=2)[:, :, 0:ns], b, ALU.add),
                    "dve_mod", (l, n))
                last_read(key, "dve_mod", (l, n))

            biased = [4]

            def ada_flush(l, n):
                while biased[0] <= 12 * l + n:
                    ada_bias(biased[0] // 12, biased[0] % 12)
                    biased[0] += 1

            def ada_work(phase, step):
                for l, n, k, s in ada_share(phase, step)[0]:
                    two = mod_streams(l, n) == 2
                    if two and k == 0 or not two and k == KD - 1:
                        ada_flush(*divmod(12 * l + n - 1, 12))
                    w = chunk(dve, l, f"ada{n}").rearrange("p (k n) -> p k n", k=KD)[:, k, :]
                    acc = ada_buffer(l, n, s)
                    b = s if two else n % 2
                    c = CS[:, s * KD + k:s * KD + k + 1]
                    if k == 0:
                        if b in acc_of:
                            after(dve, "pe_ada", acc_of[b])
                        acc_of[b] = ("ada", l, n)
                        ins = ts(acc, w, c, None, ALU.mult)
                    else:
                        after(dve, "dve_acc", (l, n, k - 1, s))
                        ins = stt(acc, w, c, acc, ALU.mult, ALU.add)
                    sig(ins, "dve_acc", (l, n, k, s))
                    book["chunk_done", (l, f"ada{n}")] = ("dve_acc", (l, n, k, s))

            acc_of = {}

            def modulation(l, f):
                sc, v = (8, V_AG) if f == 0 else (32, V_FG)
                g = VEC[:, l, v:v + KD].rearrange("p (m o) -> p m o", o=1)
                last = mod_streams(l, 4 * f + 4 * f) - 1
                for s in range(last + 1):
                    sig(stt(SCLS[:, l, f, :, s:s + 1], MODS[:, l, sc:sc + KD, s:s + 1], 1.0, g, ALU.add, ALU.mult), "dve_scl",
                        (l, f) if s == last else (l, f, s))
                after(dve, "dve_scl", (l, f))

            def norm(l, f):
                nt = TILES if f == 0 else nq_of(l)
                for t in range(nt):
                    after(dve, "pool_rx", (l, f, t))
                    sig(ts(XN[:, t, :], X[:, t, :], RX[:, t:t + 1], None, ALU.mult), "dve_xn", (l, f, t))

            def hidden(l, f):
                nt = TILES if f == 0 else nq_of(l)
                for k in range(0, KD, 2):
                    ps = bank_read(dve, ("hT", l, f, k))
                    if (l, f, k) == (0, 0, 0):
                        first_hidden(dve)
                    st = streams(nt * P)
                    for s, c0, cn in st:
                        sig(ts(HT[:, k, c0:c0 + cn], ps[:, c0:c0 + cn], SCLS[:, l, f, k, s:s + 1], MODS[:, l, 24 * f + k, s:s + 1], ALU.mult, ALU.add),
                            "dve_hT", (l, f, k) if s == st[-1][0] else (l, f, k, s))
                    last_read(("hT", l, f, k), "dve_hT", (l, f, k))

            def wide(col, n, w):
                return col.rearrange("p (g o) -> p g o", o=1).to_broadcast([P, n, w])

            def prep(l):
                early, late = norm_tasks(l)
                tasks = early + late

                def sums(i):
                    kind, t, half = tasks[i]
                    after(dve, "act_sq", (l, i))
                    if i >= 4:
                        after(dve, "pool_r", (l, i - 4))
                    sq, ss = SQ[i % 2], SS[:, i % 4]
                    if kind == "ckv":
                        sig(red(ss[:, 0:1], sq[:, 0:KVR], AX.X, ALU.add), "dve_ss", (l, i, 0))
                        ins = red(ss[:, 1:2], sq[:, KVR:OFF_KD], AX.X, ALU.add)
                    elif kind == "cq":
                        ins = red(ss[:, 0:1], sq[:, :], AX.X, ALU.add)
                    elif kind == "ukv":
                        ins = red(ss[:, 0:4], sq.rearrange("p (h d) -> p h d", h=4)[:, :, 0:NOPE], AX.X, ALU.add)
                    elif kind == "uq":
                        q = sq[:, 0:384].rearrange("p (h d) -> p h d", h=4)
                        sig(red(ss[:, 0:4], q[:, :, 0:NOPE], AX.X, ALU.add), "dve_ss", (l, i, 0))
                        ins = red(ss[:, 4:8], q[:, :, NOPE:HQ], AX.X, ALU.add)
                    else:
                        ins = red(ss[:, 0:8], sq.rearrange("p (h d) -> p h d", h=8), AX.X, ALU.add)
                    sig(ins, "dve_ss", (l, i))

                def scale(i):
                    kind, t, half = tasks[i]
                    key = ("proj", l, kind, t, half)
                    after(dve, "pool_r", (l, i))
                    if i >= 4:
                        after(dve, "pe_T", ("T", l, i - 4))
                    ps, r, tm = bank_read(dve, key), RR[:, i % 4], TM[i % 4]
                    name = "dve_tm"
                    row = lambda at, n, g: GAIN[:, l, at:at + n].rearrange("p (o n) -> p o n", o=1).to_broadcast([P, g, n])
                    if kind == "ckv":
                        sig(ts(KR[:, t, :], ps[:, KVR:OFF_KD], r[:, 1:2], None, ALU.mult), "dve_kr", (l, t))
                        ins, gain = ts(tm[:, 0:KVR], ps[:, 0:KVR], r[:, 0:1], None, ALU.mult), None
                    elif kind == "cq":
                        ins, gain = ts(tm, ps[:, :], r[:, 0:1], None, ALU.mult), None
                    elif kind == "ukv":
                        k = tm[:, 0:384].rearrange("p (h d) -> p h d", h=4)[:, :, 0:NOPE]
                        ins = tt(k, ps[:, :].rearrange("p (h d) -> p h d", h=4)[:, :, 0:NOPE], wide(r[:, 0:4], 4, NOPE), ALU.mult)
                        gain = (k, row(G_MK, NOPE, 4))
                    elif kind == "uq":
                        q, o = (x[:, 0:384].rearrange("p (h d) -> p h d", h=4) for x in (ps, tm))
                        sig(tt(o[:, :, 0:NOPE], q[:, :, 0:NOPE], wide(r[:, 0:4], 4, NOPE), ALU.mult), name, (l, i, 0))
                        ins = tt(o[:, :, NOPE:HQ], q[:, :, NOPE:HQ], wide(r[:, 4:8], 4, ROPE), ALU.mult)
                        gain = (o, row(G_MQ, HQ, 4))
                    else:
                        ins = tt(tm.rearrange("p (h d) -> p h d", h=8), ps[:, :].rearrange("p (h d) -> p h d", h=8),
                                 wide(r[:, 0:8], 8, DD), ALU.mult)
                        gain = (tm.rearrange("p (h d) -> p h d", h=4), row(G_DK if kind == "kd" else G_DQ, 2 * DD, 4))
                    if gain:
                        x, g = gain
                        sig(ins, name, (l, i, 1))
                        after(dve, name, (l, i, 1))
                        ins = tt(x, x, g, ALU.mult)
                    sig(ins, name, (l, i))
                    last_read(key, name, (l, i))

                if l == 0:
                    dve.wait_ge(sem("gain_loaded"), 16 * 4 * DEPTH)
                sums(0)
                for i in range(len(tasks)):
                    if i + 1 < len(tasks) and i + 1 != len(early):
                        sums(i + 1)
                    scale(i)
                    if l == 0 and i < len(early):
                        ada_work("prep", i)
                    if i + 1 == len(early):
                        if l == 0:
                            ada_work("vd", 0)
                            ada_flush(0, 10)
                        sums(i + 1)

            def gate_diagonals(l, which):
                m0 = 16 if which == 0 else 40
                for s in range(2 if l < DEPTH - 1 else 1):
                    for h in range(2):
                        if s:
                            after(dve, "pe_gate", ("gate", l, which, s - 1, h))
                        for b in range(4):
                            g = MODS[:, l, m0 + 4 * h + b, s:s + 1]
                            sig(ts(DIAG[:, h, b * P:(b + 1) * P], ident, g, None, ALU.mult), "dve_diag",
                                (l, which, s, h) if b == 3 else (l, which, s, h, b))

            def attention(l):
                units = attention_units(l)
                lam_init = 0.8 - 0.6 * math.exp(-0.3 * l)
                sig(ts(SUBG[:, :], VEC[:, l, V_SUB:V_SUB + 1], 1.0 - lam_init, None, ALU.mult), "dve_subg", l)

                def maxima(u, kind, t, h):
                    k0, kn = keys_of(t)
                    for m in range(1 if kind == "m" else 2):
                        c = (2 * u + m) % 8
                        ps = bank_read(dve, ("S", l, u, m))
                        link(red(MX[:, c:c + 1], ps[:, 0:kn * P], AX.X, ALU.max, negate=True))
                        sig(ts(MB[:, c:c + 1], MX[:, c:c + 1], MLA_SCALE if kind == "m" else DIFF_SCALE, None, ALU.mult),
                            "dve_mx", (l, u, m))

                def weights(u, kind, t, h):
                    k0, kn = keys_of(t)
                    c = (2 * u) % 8
                    if kind == "m":
                        after(dve, "act_p", (l, u))
                        sig(rec(RINV[:, t % 2, h:h + 1], RSUM[:, c:c + 1]), "dve_rinv", (l, u))
                        return
                    after(dve, "act_pd", (l, u, 1))
                    link(rec(RDIF[:, c:c + 2], RSUM[:, c:c + 2]))
                    link(tt(RDIF[:, c + 1:c + 2], RDIF[:, c + 1:c + 2], NLAM[:, l:l + 1], ALU.mult))
                    b0, b1 = (PB[book.get((x, (l, u)), 0)][:, 0:kn * P] for x in ("pbuf", "pbuf1"))
                    link(ts(b1, b1, RDIF[:, c + 1:c + 2], None, ALU.mult))
                    sig(stt(b0, b0, RDIF[:, c:c + 1], b1, ALU.mult, ALU.add), "dve_a", (l, u))

                def transposed(u, kind, t, h):
                    if u % 2 == 0:
                        return
                    k0, kn = keys_of(t)
                    if u >= 2:
                        after(dve, "pe_O", book.get(("pv_done", (l, u - 2)), ("none", 0)))
                    ps = bank_read(dve, ("PT", l, u))
                    sig(cp(PTS[1][:, 0:kn * P], ps[:, 0:kn * P]), "dve_pts", (l, u))
                    last_read(("PT", l, u), "dve_pts", (l, u))

                def out_rows(kind, t):
                    ps = bank_read(dve, ("O", l, kind, t))
                    before_ = ("OT", l, "m", t) if kind == "d" else ("OT", l, "d", t - 1) if t else None
                    if before_:
                        after(dve, "pe_OT", before_)
                    if kind == "m":
                        after(dve, "dve_rinv", (l, 12 * t + MH - 1))
                        r, n, w = RINV[:, t % 2, :], MH, MV
                    else:
                        after(dve, "pool_ro", (l, t))
                        r, n, w = RO, DH, DV
                    sig(tt(OTM.rearrange("p (h d) -> p h d", h=n), ps[:, :].rearrange("p (h d) -> p h d", h=n), wide(r, n, w), ALU.mult),
                        "dve_o", (l, kind, t))
                    last_read(("O", l, kind, t), "dve_o", (l, kind, t))

                waiting = []
                for i in range(len(units) + A_VLAG + 2):
                    if i < len(units):
                        maxima(i, *units[i])
                    if 0 <= i - 1 < len(units):
                        weights(i - 1, *units[i - 1])
                    if 0 <= i - A_TLAG < len(units):
                        transposed(i - A_TLAG, *units[i - A_TLAG])
                    if 0 <= i - A_VLAG < len(units):
                        kind, t, h = units[i - A_VLAG]
                        if h == (MH if kind == "m" else DH) - 1:
                            if kind == "d":
                                after(dve, "act_osq", (l, t))
                                sig(red(SSO[:, :], RTF[:, 0:512].rearrange("p (h d) -> p h d", h=DH), AX.X, ALU.add), "dve_sso", (l, t))
                            waiting.append((i + 1, kind, t))
                    while waiting and waiting[0][0] <= i:
                        out_rows(*waiting.pop(0)[1:])

            def merge(l):
                n = nq_of(l) * P
                for b in range(KD):
                    for j in range(2):
                        if b >= 2:
                            after(dve, "pool_y", (l, b - 2))
                        after(dve, "act_mg", (l, b, j))
                        key = ("mg", l, b, 2 + j)
                        ps = bank_read(dve, key)
                        sig(stt(MY[b % 2][j][:, 0:n], MT[b % 2][j][:, 0:n], 1.0, ps[:, 0:n], ALU.add, ALU.mult), "dve_mg", (l, b, j))
                        last_read(key, "dve_mg", (l, b, j))
                        if l == 0:
                            ada_work("merge", 2 * b + j)

            def out_proj(l):
                after(dve, "act_gate", (l, 0, 1 if l < DEPTH - 1 else 0, 1))
                for h in range(2):
                    for t in range(nq_of(l)):
                        key = ("out", l, h, t)
                        ps = bank_read(dve, key)
                        tmp = STG[:, 512 * (t % 2):512 * (t % 2 + 1)]
                        cols = slice(512 * h, 512 * (h + 1))
                        sig(tt(tmp, ps[:, :], GATE[:, t // LTILES, cols], ALU.mult), "dve_og", (l, h, t))
                        last_read(key, "dve_og", (l, h, t))
                        if l == 0 and (h, t) == (1, 0):
                            ada_flush(1, 11)
                        after(dve, "dve_og", (l, h, t))
                        sig(tt(X[:, t, cols], X[:, t, cols], tmp, ALU.add), "dve_x", (l, 0, h, t))

            def route_choice(l):
                nt = nq_of(l)
                g3 = lambda x, a, b: x.rearrange("p (a b) -> p a b", a=a)
                aff, sel, t1 = (x[:, 0:nt * NE] for x in (AFF, SEL, TMPR))
                after(dve, "act_rt", l)
                dve.wait_ge(sem("router_loaded"), 32)
                link(ts(t1, aff, 1.0, None, ALU.add))
                link(rec(aff, t1))
                rb = RB[:, :].rearrange("p (o n) -> p o n", o=1).to_broadcast([P, nt, NE])
                link(tt(g3(sel, nt, NE), g3(aff, nt, NE), rb, ALU.add))
                s4 = g3(sel, nt * NG, EPG)
                pr = PAIR[:, 0:nt * NG * 6].rearrange("p (g n) -> p g n", n=6)
                link(tt(pr[:, :, 0:3], s4[:, :, 0:3], s4[:, :, 1:4], ALU.add))
                link(tt(pr[:, :, 3:5], s4[:, :, 0:2], s4[:, :, 2:4], ALU.add))
                link(tt(pr[:, :, 5:6], s4[:, :, 0:1], s4[:, :, 3:4], ALU.add))
                gs, gm, gk = (GRP[:, i, 0:nt * NG] for i in range(3))
                link(red(gs, pr, AX.X, ALU.max))
                link(red(gm[:, 0:nt], g3(gs, nt, NG), AX.X, ALU.max))
                link(tt(g3(gk, nt, NG), g3(gs, nt, NG), wide(gm[:, 0:nt], nt, NG), ALU.is_equal))
                tie = CST[:, C_TIE:C_TIE + NG].rearrange("p (o n) -> p o n", o=1).to_broadcast([P, nt, NG])
                link(tt(g3(gk, nt, NG), g3(gk, nt, NG), tie, ALU.mult))
                link(red(gm[:, 0:nt], g3(gk, nt, NG), AX.X, ALU.max))
                link(tt(g3(gk, nt, NG), g3(gk, nt, NG), wide(gm[:, 0:nt], nt, NG), ALU.is_equal))
                link(tt(s4, s4, wide(gk, nt * NG, EPG), ALU.mult))
                link(ts(gs, gk, 1.0, BIG, ALU.subtract, ALU.mult))
                link(tt(s4, s4, wide(gs, nt * NG, EPG), ALU.add))
                for t in range(nt):
                    link(nc.vector.max(out=BEST[:, t, :], in_=sel[:, NE * t:NE * (t + 1)]))
                    link(nc.vector.max_index(out=BIDX[:, t, :], in_max=BEST[:, t, :], in_values=sel[:, NE * t:NE * (t + 1)]))
                link(cp(FIDX[:, 0:nt, :], BIDX[:, 0:nt, 0:2]))
                iota = CST[:, C_IOTA:C_IOTA + NE].rearrange("p (o n) -> p o n", o=1).to_broadcast([P, nt, NE])
                for k in range(2):
                    link(tt(HOT[k][:, 0:nt, :], iota, FIDX[:, 0:nt, k:k + 1].to_broadcast([P, nt, NE]), ALU.is_equal))
                    link(tt(g3(t1, nt, NE), HOT[k][:, 0:nt, :], g3(aff, nt, NE), ALU.mult))
                    link(red(WTS[:, 0:nt, k], g3(t1, nt, NE), AX.X, ALU.add))
                link(tt(gm[:, 0:nt], WTS[:, 0:nt, 0], WTS[:, 0:nt, 1], ALU.add))
                link(rec(gs[:, 0:nt], gm[:, 0:nt]))
                link(tt(WTS[:, 0:nt, :], WTS[:, 0:nt, :], wide(gs[:, 0:nt], nt, 2), ALU.mult))
                sig(tt(MSK[:, 0:nt, :], HOT[0][:, 0:nt, :], HOT[1][:, 0:nt, :], ALU.add), "dve_mask", l)

            def route_places(l):
                nt = nq_of(l)
                g3 = lambda x, a: x.rearrange("p (a b) -> p a b", a=a)
                ps = bank_read(dve, ("place", l))
                cnt, inc, off = (CNT[:, i, :] for i in range(3))
                link(cp(cnt, ps[:, 64:64 + NE]))
                link(nc.vector.tensor_tensor_scan(inc, ones[:, 0:NE], cnt, 0.0, ALU.mult, ALU.add))
                link(tt(off, inc, cnt, ALU.subtract))
                t1 = TMPR[:, 0:nt * NE]
                off_w = off.rearrange("p (o n) -> p o n", o=1).to_broadcast([P, nt, NE])
                sig(tt(g3(SEL[:, 0:nt * NE], nt), g3(ps[:, 0:nt * NE], nt), off_w, ALU.add), "dve_plc", l)
                last_read(("place", l), "dve_plc", l)
                after(dve, "dve_plc", l)
                for k in range(2):
                    link(tt(g3(t1, nt), HOT[k][:, 0:nt, :], g3(SEL[:, 0:nt * NE], nt), ALU.mult))
                    link(red(SLF[:, 0:nt, k], g3(t1, nt), AX.X, ALU.add))
                sig(cp(SLOT[:, 0:nt, :], SLF[:, 0:nt, :]), "dve_slot", l)
                rc = PAIR[:, 0:CAND]
                link(ts(rc, CST[:, C_RCAND:C_RCAND + CAND], float(ROWS[l]), None, ALU.mult))
                act_, run, row, hit = (CND[:, i, :] for i in range(4))
                link(tt(g3(act_, NE), wide(cnt, NE, TILES), g3(rc, NE), ALU.is_gt))
                link(nc.vector.tensor_tensor_scan(run, CONES, act_, 0.0, ALU.mult, ALU.add))
                link(tt(g3(row, NE), wide(off, NE, TILES), g3(rc, NE), ALU.add))
                link(stt(hit, run, CST[:, C_JOB:C_JOB + 1], act_, ALU.is_equal, ALU.mult))
                link(tt(act_, hit, CST[:, C_ECAND:C_ECAND + CAND], ALU.mult))
                link(red(JOBC[:, 0:1], act_, AX.X, ALU.add))
                link(tt(row, hit, row, ALU.mult))
                link(red(JOBC[:, 1:2], row, AX.X, ALU.add))
                link(red(JOBC[:, 2:3], hit, AX.X, ALU.add))
                link(ts(JOBC[:, 2:3], JOBC[:, 2:3], -float(SORTED), float(SORTED), ALU.mult, ALU.add))
                sig(tt(JOBC[:, 1:2], JOBC[:, 1:2], JOBC[:, 2:3], ALU.add), "dve_jobcol", l)
                link(ts(TABI[:, 0:1], run[0:1, CAND - 1:CAND], 1.0, None, ALU.add))
                link(ts(TAB[0:1, 64:65], TABI[:, 0:1], 1, None, ALU.arith_shift_right))
                link(ts(TAB[0:1, 65:66], TAB[0:1, 64:65], 1.0, None, ALU.subtract))

            def route_table(l):
                ps = bank_read(dve, ("jobs", l))
                link(cp(TAB[0:1, 0:32], ps[0:1, 0:32]))
                cp(TAB[0:1, 32:64], ps[0:1, P:P + 32]).then_inc(sem(f"tab_ready{l}"), 1)
                book["read", ("jobs", l)] = (f"tab_ready{l}", 0)
                book[f"tab_ready{l}", 0] = 1

            def shared(l, f):
                n = nq_of(l) * P
                after(dve, "act_sh", (l, f))
                ps = bank_read(dve, ("sh", l, f, 0))
                sig(stt(SVV[f % 2][:, 0:n], STH[f % 2][:, 0:n], 1.0, ps[:, 0:n], ALU.add, ALU.mult), "dve_sv", (l, f))
                last_read(("sh", l, f, 0), "dve_sv", (l, f))
                after(dve, "dve_sv", (l, f))
                ps = bank_read(dve, ("sh", l, f, 1))
                sig(stt(HET[:, f, 0:n], SVV[f % 2][:, 0:n], 0.5, ps[:, 0:n], ALU.mult, ALU.mult), "dve_sh", (l, f))
                last_read(("sh", l, f, 1), "dve_sh", (l, f))

            def experts(l):
                e = lambda name: sem(f"{name}{l}")
                dve.wait_ge(e("tab_ready"), 1)
                before_last = dve.value_load(TAB[0:1, 65:66], min_val=1, max_val=TURNS - 1)

                def low(x, j, ready):
                    for p in range(3):
                        dve.wait_ge(e("e_high"), ready(p))
                        cols = slice(1024 * p, 1024 * (p + 1))
                        tt(ELOW[3 * j + x][:, cols], ESLOT[3 * j + x][:, cols], HIGH[p], ALU.subtract).then_inc(e("e_low"), 1)

                def rows(j, ready):
                    for h in range(2):
                        dve.wait_ge(e("e_hexh"), ready(h))
                        cols = slice(512 * h, 512 * (h + 1))
                        tt(HEXL[j][:, cols], PS[h][:, :], HEXH[j][:, cols], ALU.subtract).then_inc(e("e_hexl"), 1)

                rows(0, lambda h: h + 1)
                low(0, 0, lambda p: p + 1)
                rows(1, lambda h: h + 3)
                low(1, 0, lambda p: p + 5)

                def turn(i, more):
                    i24, i2 = dve.snap(24 * i), dve.snap(2 * i)
                    for j in range(2):
                        final = not more and j == 1
                        dve.wait_ge(e("e_th"), i2 + (j + 1))
                        stt(THB[j], THB[j], 1.0, PS[2 if j == 0 else 7][:, :], ALU.add, ALU.mult).then_inc(e("e_v"), 1)
                        if not final:
                            low(0, 1 - j, lambda p: i24 + (12 * j + 9 + p))
                        dve.wait_ge(e("e_v"), i2 + (j + 1))
                        dve.wait_ge(e("e_piece"), i24 + (12 * j + 8))
                        stt(HID[j], THB[j], 0.5, PS[3][:, :], ALU.mult, ALU.mult).then_inc(e("e_hid_done"), 1)
                        low(2, j, lambda p: i24 + (12 * j + (9 if final else 13) + p))
                        dve.wait_ge(e("e_htxh"), i2 + (j + 1))
                        tt(HTXL, PS[4][:, :], HTXH, ALU.subtract).then_inc(e("e_htxl"), 1)
                        if more:
                            rows(j, lambda h: 4 * i + (2 * j + 5 + h))
                        if not final:
                            low(1, 1 - j, lambda p: i24 + (12 * j + 17 + p))

                with dve.Fori(0, before_last) as i:
                    turn(i, True)
                turn(before_last, False)
                dve.wait_ge(e("experts_over"), 1)

            def combine(l):
                for t in range(nq_of(l)):
                    y0, y1 = YG[t]
                    after(dve, "act_yw", (l, t))
                    link(stt(y0, y1, WTS[:, t, 1:2], y0, ALU.mult, ALU.add))
                    sig(tt(y0, y0, GATE[:, t // LTILES, :], ALU.mult), "dve_yg", (l, t))
                    if t == nq_of(l) - 1:
                        after(dve, "dve_yg", (l, t))
                        sig(tt(X[:, t, :], X[:, t, :], y0, ALU.add), "dve_x", (l, 1, t))

            start()
            for l in range(DEPTH):
                if l == 0:
                    after(dve, "dve_mod", (0, 3))
                modulation(l, 0)
                norm(l, 0)
                hidden(l, 0)
                prep(l)
                attention(l)
                if l == 0:
                    ada_flush(0, 10)
                    after(dve, "dve_mod", (0, 10))
                after(dve, "pe_OT", ("OT", l, "d", nq_of(l) - 1))
                gate_diagonals(l, 0)
                merge(l)
                if l == 0:
                    ada_flush(0, 11)
                    after(dve, "dve_mod", (0, 11))
                    modulation(0, 1)
                out_proj(l)
                if l == 0:
                    after(dve, "dve_mod", (1, 11))
                    modulation(1, 1)
                norm(l, 1)
                hidden(l, 1)
                route_choice(l)
                shared(l, 0)
                route_places(l)
                shared(l, 1)
                route_table(l)
                shared(l, 2)
                shared(l, 3)
                gate_diagonals(l, 1)
                after(dve, "act_gate", (l, 1, 1 if l < DEPTH - 1 else 0, 1))
                for t in range(nq_of(l)):
                    after(dve, "act_ys", (l, t, 1))
                    link(tt(YS[:, t, :], YS[:, t, :], GATE[:, t // LTILES, :], ALU.mult))
                    sig(tt(X[:, t, :], X[:, t, :], YS[:, t, :], ALU.add), "dve_ysx", (l, t))
                    after(dve, "dve_ysx", (l, t))
                experts(l)
                combine(l)

        @block.gpsimd
        def _(pool):
            gt, gs_, gc = nc.gpsimd.tensor_tensor, nc.gpsimd.tensor_scalar, nc.gpsimd.tensor_copy

            def link(ins):
                chained(pool, "pool_step", ins)

            def start():
                link(pool.memset(HALF[:, :], -0.5))
                link(pool.memset(ZERO, 0.0))
                pool.dma_start(Hs[SORTED:SORTED + P, :], ZERO).then_inc(sem("pad_stored"), 16)
                pool.wait_ge(sem("const_loaded"), 16)

            def norm(l, f):
                nt = TILES if f == 0 else nq_of(l)
                for t in range(nt):
                    after(pool, "act_ssx", (l, f, t))
                    link(gs_(RX[:, t:t + 1], SSX[:, t:t + 1], 1.0 / D, EPS, ALU.mult, ALU.add))
                    sig(gt(RX[:, t:t + 1], RX[:, t:t + 1], HALF[:, 0:1], ALU.pow), "pool_rx", (l, f, t))

            def rotate(view, cos, sin, groups, q):
                x1, x2 = view
                shape = [P, groups, 2, q]
                c, s = (x.rearrange("p (o a q) -> p o a q", o=1, a=2).to_broadcast(shape) for x in (cos, sin))
                a, b, cc, d = (RT[:, i, 0:groups * 2 * q].rearrange("p (g a q) -> p g a q", g=groups, a=2) for i in range(4))
                link(gt(a, x1, c, ALU.mult))
                link(gt(b, x2, s, ALU.mult))
                link(gt(cc, x1, s, ALU.mult))
                link(gt(d, x2, c, ALU.mult))
                link(gt(x1, a, b, ALU.subtract))
                return gt(x2, cc, d, ALU.add)

            def halves(x, groups, q):
                v = x.rearrange("p g (a h q) -> p g a h q", a=2, h=2)
                return v[:, :, :, 0, :], v[:, :, :, 1, :]

            def prep(l):
                early, late = norm_tasks(l)
                tasks = early + late

                def roots(i):
                    kind, t, half = tasks[i]
                    after(pool, "dve_ss", (l, i))
                    ss, r = SS[:, i % 4], RR[:, i % 4]
                    parts = {"ckv": [(0, 1, KVR), (1, 2, ROPE)], "cq": [(0, 1, QR)], "ukv": [(0, 4, NOPE)],
                             "uq": [(0, 4, NOPE), (4, 8, ROPE)]}.get(kind, [(0, 8, DD)])
                    for a, b, w in parts:
                        link(gs_(r[:, a:b], ss[:, a:b], 1.0 / w, EPS, ALU.mult, ALU.add))
                    n = parts[-1][1]
                    sig(gt(r[:, 0:n], r[:, 0:n], HALF[:, 0:n], ALU.pow), "pool_r", (l, i))

                def gains(i):
                    kind, t, half = tasks[i]
                    if kind == "cq":
                        return
                    lat = t < LTILES
                    tm = TM[i % 4]
                    if kind == "ckv":
                        after(pool, "dve_kr", (l, t))
                        x = KR[:, t, :]
                        ins = gt(x, x, GAIN[:, l, G_MK + NOPE:G_MK + HQ], ALU.mult)
                        if lat:
                            link(ins)
                            ins = rotate(halves(x.rearrange("p (g d) -> p g d", g=1), 1, 8), CST[:, C_COSM + 16 * t:C_COSM + 16 * (t + 1)],
                                         CST[:, C_SINM + 16 * t:C_SINM + 16 * (t + 1)], 1, 8)
                        sig(ins, "pool_kr", (l, t))
                        return
                    if tm_sem(kind, t) == "dve_tm":
                        return
                    after(pool, "dve_tm", (l, i))
                    if kind == "ukv":
                        k = tm[:, 0:384].rearrange("p (h d) -> p h d", h=4)
                        after(pool, "pool_kr", (l, t))
                        ins = gc(k[:, :, NOPE:HQ], KR[:, t, :].rearrange("p (o n) -> p o n", o=1).to_broadcast([P, 4, ROPE]))
                    elif kind == "uq":
                        q = tm[:, 0:384].rearrange("p (h d) -> p h d", h=4)
                        ins = rotate(halves(q[:, :, NOPE:HQ], 4, 8), CST[:, C_COSM + 16 * t:C_COSM + 16 * (t + 1)],
                                     CST[:, C_SINM + 16 * t:C_SINM + 16 * (t + 1)], 4, 8)
                    else:
                        ins = rotate(halves(tm.rearrange("p (h d) -> p h d", h=8), 8, 16), CST[:, C_COSD + 32 * t:C_COSD + 32 * (t + 1)],
                                     CST[:, C_SIND + 32 * t:C_SIND + 32 * (t + 1)], 8, 16)
                    sig(ins, "pool_tm", (l, i))

                roots(0)
                for i in range(len(tasks)):
                    if i + 1 < len(tasks) and i + 1 != len(early):
                        roots(i + 1)
                    gains(i)
                    if i + 1 == len(early):
                        roots(i + 1)

            def attention(l):
                for t in range(nq_of(l)):
                    after(pool, "dve_sso", (l, t))
                    link(gs_(RO[:, :], SSO[:, :], 1.0 / DV, EPS, ALU.mult, ALU.add))
                    sig(gt(RO[:, :], RO[:, :], HALF[:, 0:DH], ALU.pow), "pool_ro", (l, t))

            def merge(l):
                n = nq_of(l) * P
                for b in range(KD):
                    after(pool, "dve_mg", (l, b, 1))
                    sig(gt(YT[:, b, 0:n], MY[b % 2][0][:, 0:n], MY[b % 2][1][:, 0:n], ALU.add), "pool_y", (l, b))

            def scatter(l):
                after(pool, "dve_slot", l)
                for t in range(nq_of(l)):
                    after(pool, "act_htok", (l, t, 1))
                    for k in range(2):
                        pool.indirect_dma_start(Hs[0:SORTED, :], bass.IndirectOffsetOnAxis(ap=SLOT[:, t, k:k + 1], axis=0),
                                                HTOK[t], None).then_inc(sem(f"sorted_stored{l}"), 16)

            def experts(l):
                e = lambda name: sem(f"{name}{l}")
                pool.wait_ge(e("tab_ready"), 1)
                before_last = pool.value_load(TAB[0:1, 65:66], min_val=1, max_val=TURNS - 1)

                def low(x, j, ready):
                    pool.wait_ge(e("e_high"), ready)
                    gt(ELOW[3 * j + x][:, 3072:4096], ESLOT[3 * j + x][:, 3072:4096], HIGH[3], ALU.subtract).then_inc(e("e_plow"), 1)

                low(0, 0, 4)
                low(1, 0, 8)

                def turn(i, more):
                    i24 = pool.snap(24 * i)
                    for j in range(2):
                        final = not more and j == 1
                        if not final:
                            low(0, 1 - j, i24 + (12 * j + 12))
                        low(2, j, i24 + (12 * j + (12 if final else 16)))
                        if not final:
                            low(1, 1 - j, i24 + (12 * j + 20))

                with pool.Fori(0, before_last) as i:
                    turn(i, True)
                turn(before_last, False)

            def gather(l):
                pool.wait_ge(sem(f"experts_over{l}"), 1)
                for t in range(nq_of(l)):
                    for k in range(2):
                        pool.indirect_dma_start(YG[t][k], None, Ys[0:SORTED, :],
                                                bass.IndirectOffsetOnAxis(ap=SLOT[:, t, k:k + 1], axis=0)).then_inc(sem(f"y_gathered{t}"), 16)

            def combine(l):
                for t in range(nq_of(l) - 1):
                    after(pool, "dve_yg", (l, t))
                    sig(gt(X[:, t, :], X[:, t, :], YG[t][0], ALU.add), "pool_x", (l, t))

            start()
            for l in range(DEPTH):
                norm(l, 0)
                prep(l)
                attention(l)
                merge(l)
                norm(l, 1)
                scatter(l)
                experts(l)
                gather(l)
                combine(l)


_INS = ["x", "c", "ctx", "c_ctx", "ada_w", "ada_b", "attn_norm_g", "ffn_norm_g", "w_in", "mla_q_norm_g", "mla_w_uq",
        "mla_kv_norm_g", "mla_w_ukv", "mla_q_g", "mla_k_g", "diff_q_g", "diff_k_g", "diff_lam", "diff_sub_g", "w_o_mla",
        "w_o_diff", "w_out", "router_w", "router_b", "moe_w_gate", "moe_w_up", "moe_w_down", "sh_w_gate", "sh_w_up", "sh_w_down"]


def kernel(**inputs):
    import numpy as _np
    import concourse.bacc as _bacc
    from concourse import mybir as _mybir
    from concourse.bass_utils import run_bass_kernel_spmd as _run

    def program(book):
        nc = _bacc.Bacc("TRN2", target_bir_lowering=False, num_devices=1)
        args = {}
        for name, a in arrays.items():
            args[name[3:]] = nc.dram_tensor(name, a.shape, _mybir.dt.from_np(a.dtype), kind="ExternalInput").ap()
        args["out"] = nc.dram_tensor("out_0", (1, SEQ, D), _mybir.dt.float32, kind="ExternalOutput").ap()
        build(nc, args, book)
        return nc

    arrays = {f"in_{name}": _np.ascontiguousarray(inputs[name]) for name in _INS}
    arrays["in_consts"] = constants()
    book = {}
    program(book)
    r = _run(program(book), [arrays], core_ids=[0])
    return r.results[0]["out_0"]
```
